# Optimizing a Trainium2 kernel written in Bass

```python
import math
import jax, jax.numpy as jnp
from jax import lax
import numpy as np

D_MODEL = 1024
BATCH = 1
SEQ = 256
DEPTH = 2

N_A_LAYERS = DEPTH // 2
N_B_LAYERS = DEPTH - N_A_LAYERS
LRU_WIDTH = 1280
LRU_BLOCK = 256
LRU_HEADS = LRU_WIDTH // LRU_BLOCK
CONV_WIDTH = 4
LRU_C = 8.0
N_HEADS = 8
N_KV_HEADS = 4
HEAD_DIM = 128
KV_GROUP = N_HEADS // N_KV_HEADS
MOBA_BLOCK = 256
MOBA_TOPK = 3
Q_CHUNK = 16
REL_BUCKETS = 32
REL_MAX_DIST = 128
D_FF = -(-8 * D_MODEL // (3 * 256)) * 256
RMS_EPS = 1e-6
NEG_INF = -1e30


def rmsnorm(x, g):
    xf = x.astype(jnp.float32)
    y = xf * lax.rsqrt(jnp.mean(xf * xf, axis=-1, keepdims=True) + RMS_EPS)
    return (y * g.astype(jnp.float32)).astype(x.dtype)

def modulate(h, shift, scale):
    return h * (1 + scale[:, None, :]) + shift[:, None, :]

def swiglu(h, w_gate, w_up, w_down):
    return (jax.nn.silu(h @ w_gate) * (h @ w_up)) @ w_down

def _lru_combine(left, right):
    a_l, b_l = left
    a_r, b_r = right
    return a_l * a_r, a_r * b_l + b_r

def rglru_mixer(h, w_in, conv_w, conv_b, w_gates, b_gates, lru_lambda, w_out):
    B, S, _ = h.shape
    u = h @ w_in
    y_br = jax.nn.gelu(u[..., :LRU_WIDTH])
    x_br = u[..., LRU_WIDTH:]
    xp = jnp.pad(x_br, ((0, 0), (CONV_WIDTH - 1, 0), (0, 0)))
    xc = sum(xp[:, k:k + S, :] * conv_w[k] for k in range(CONV_WIDTH)) + conv_b
    xb = xc.reshape(B, S, LRU_HEADS, LRU_BLOCK)
    g = jnp.einsum('bshi,hio->bsho', xb, w_gates)
    gr = g[..., :LRU_BLOCK].reshape(B, S, LRU_WIDTH) + b_gates[0]
    gi = g[..., LRU_BLOCK:].reshape(B, S, LRU_WIDTH) + b_gates[1]
    r = jax.nn.sigmoid(gr.astype(jnp.float32))
    i = jax.nn.sigmoid(gi.astype(jnp.float32))
    log_a = -LRU_C * r * jax.nn.softplus(-lru_lambda.astype(jnp.float32))
    a = jnp.exp(log_a)
    mult = jnp.sqrt(-jnp.expm1(2.0 * log_a))
    b = mult * (i * xc.astype(jnp.float32))
    _, hs = lax.associative_scan(_lru_combine, (a, b), axis=1)
    return (hs.astype(h.dtype) * y_br) @ w_out

def shared_kv(x, shift, scale, g, w_kv):
    B, S, _ = x.shape
    h = modulate(rmsnorm(x, g), shift, scale)
    kv = h @ w_kv
    nb = -(-S // MOBA_BLOCK)
    pad = nb * MOBA_BLOCK - S
    def blk(t):
        t = t.reshape(B, S, N_KV_HEADS, HEAD_DIM).transpose(0, 2, 1, 3)
        t = jnp.pad(t, ((0, 0), (0, 0), (0, pad), (0, 0)))
        return t.reshape(B, N_KV_HEADS, nb, MOBA_BLOCK, HEAD_DIM)
    k_blocks = blk(kv[..., :N_KV_HEADS * HEAD_DIM])
    v_blocks = blk(kv[..., N_KV_HEADS * HEAD_DIM:])
    k_mean = jnp.mean(k_blocks.astype(jnp.float32), axis=3)
    return k_blocks, v_blocks, k_mean

def t5_bucket(dist):
    dist = jnp.maximum(dist, 0)
    max_exact = REL_BUCKETS // 2
    d = jnp.maximum(dist, 1).astype(jnp.float32)
    large = max_exact + (jnp.log(d / max_exact) / math.log(REL_MAX_DIST / max_exact)
                         * (REL_BUCKETS - max_exact)).astype(jnp.int32)
    large = jnp.minimum(large, REL_BUCKETS - 1)
    return jnp.where(dist < max_exact, dist, large)

def moba_mixer(h, w_q, w_o, k_blocks, v_blocks, k_mean, rel_bias):
    B, S, _ = h.shape
    nb = k_blocks.shape[2]
    s_pad = nb * MOBA_BLOCK
    n_sel = min(MOBA_TOPK, nb)
    scale = HEAD_DIM ** -0.5
    q = (h @ w_q).reshape(B, S, N_HEADS, HEAD_DIM).transpose(0, 2, 1, 3)
    q = jnp.pad(q, ((0, 0), (0, 0), (0, s_pad - S), (0, 0)))
    kv_head = jnp.arange(N_HEADS) // KV_GROUP
    km = k_mean[:, kv_head]
    bi = jnp.arange(B)[:, None, None, None]
    kvh = kv_head[None, :, None, None]
    hi5 = jnp.arange(N_HEADS)[None, :, None, None, None]
    bias_tab = rel_bias.astype(jnp.float32)
    blk_pos = jnp.arange(MOBA_BLOCK)

    def chunk(ci):
        t0 = ci * Q_CHUNK
        qf = lax.dynamic_slice_in_dim(q, t0, Q_CHUNK, axis=2).astype(jnp.float32)
        pos = t0 + jnp.arange(Q_CHUNK)
        own = t0 // MOBA_BLOCK
        gate = jnp.einsum('bhcd,bhnd->bhcn', qf, km)
        gate = jnp.where(jnp.arange(nb) < own, gate, NEG_INF)
        _, idx = lax.top_k(gate, n_sel)
        sel_valid = jnp.arange(n_sel) < own
        ksel = k_blocks[bi, kvh, idx].astype(jnp.float32)
        vsel = v_blocks[bi, kvh, idx].astype(jnp.float32)
        s_sel = jnp.einsum('bhcd,bhcnkd->bhcnk', qf, ksel) * scale
        kpos_sel = idx[..., None] * MOBA_BLOCK + blk_pos
        dist_sel = pos[None, None, :, None, None] - kpos_sel
        s_sel = jnp.where(sel_valid[:, None], s_sel + bias_tab[hi5, t5_bucket(dist_sel)], NEG_INF)
        k_own = lax.dynamic_index_in_dim(k_blocks, own, axis=2, keepdims=False)[:, kv_head].astype(jnp.float32)
        v_own = lax.dynamic_index_in_dim(v_blocks, own, axis=2, keepdims=False)[:, kv_head].astype(jnp.float32)
        s_own = jnp.einsum('bhcd,bhkd->bhck', qf, k_own) * scale
        dist_own = pos[:, None] - (own * MOBA_BLOCK + blk_pos)[None, :]
        s_own = jnp.where(dist_own >= 0, s_own + bias_tab[:, t5_bucket(dist_own)], NEG_INF)
        logits = jnp.concatenate([s_sel.reshape(B, N_HEADS, Q_CHUNK, n_sel * MOBA_BLOCK), s_own], axis=-1)
        p = jax.nn.softmax(logits, axis=-1)
        p_sel = p[..., :n_sel * MOBA_BLOCK].reshape(B, N_HEADS, Q_CHUNK, n_sel, MOBA_BLOCK)
        p_own = p[..., n_sel * MOBA_BLOCK:]
        o = jnp.einsum('bhcnk,bhcnkd->bhcd', p_sel, vsel) + jnp.einsum('bhck,bhkd->bhcd', p_own, v_own)
        return o.astype(h.dtype)

    o = lax.map(chunk, jnp.arange(s_pad // Q_CHUNK))
    o = o.transpose(1, 0, 3, 2, 4).reshape(B, s_pad, N_HEADS * HEAD_DIM)[:, :S]
    return o @ w_o

def first_inputs(seed: int = 0) -> dict:
    key = jax.random.key(seed)
    ks = jax.random.split(key, 32)
    nrm = lambda k, shape, s: jax.random.normal(k, shape, jnp.float32) * s
    D = D_MODEL
    u = jax.random.uniform(ks[10], (N_A_LAYERS, LRU_WIDTH), jnp.float32, 0.9, 0.999)
    a_base = u ** (1.0 / LRU_C)
    lru_lambda = jnp.log(a_base) - jnp.log1p(-a_base)
    return {
        "x": nrm(ks[0], (BATCH, SEQ, D), 1.0),
        "c": nrm(ks[1], (BATCH, D), 1.0),
        "mod_w": nrm(ks[2], (DEPTH, D, 6 * D), 0.5 * D ** -0.5),
        "mod_b": nrm(ks[3], (DEPTH, 6 * D), 0.02),
        "norm_mix": 1.0 + nrm(ks[4], (DEPTH, D), 0.02),
        "norm_ffn": 1.0 + nrm(ks[5], (DEPTH, D), 0.02),
        "lru_w_in": nrm(ks[6], (N_A_LAYERS, D, 2 * LRU_WIDTH), D ** -0.5),
        "lru_conv_w": nrm(ks[7], (N_A_LAYERS, CONV_WIDTH, LRU_WIDTH), CONV_WIDTH ** -0.5),
        "lru_conv_b": nrm(ks[8], (N_A_LAYERS, LRU_WIDTH), 0.02),
        "lru_w_gates": nrm(ks[9], (N_A_LAYERS, LRU_HEADS, LRU_BLOCK, 2 * LRU_BLOCK), LRU_BLOCK ** -0.5),
        "lru_b_gates": nrm(ks[11], (N_A_LAYERS, 2, LRU_WIDTH), 0.02),
        "lru_lambda": lru_lambda,
        "lru_w_out": nrm(ks[12], (N_A_LAYERS, LRU_WIDTH, D), LRU_WIDTH ** -0.5),
        "kv_mod_w": nrm(ks[13], (D, 2 * D), 0.5 * D ** -0.5),
        "kv_mod_b": nrm(ks[14], (2 * D,), 0.02),
        "kv_norm": 1.0 + nrm(ks[15], (D,), 0.02),
        "w_kv": nrm(ks[16], (D, 2 * N_KV_HEADS * HEAD_DIM), D ** -0.5),
        "attn_w_q": nrm(ks[17], (N_B_LAYERS, D, N_HEADS * HEAD_DIM), D ** -0.5),
        "attn_w_o": nrm(ks[18], (N_B_LAYERS, N_HEADS * HEAD_DIM, D), (N_HEADS * HEAD_DIM) ** -0.5),
        "rel_bias": nrm(ks[19], (N_HEADS, REL_BUCKETS), 0.2),
        "ffn_w_gate": nrm(ks[20], (DEPTH, D, D_FF), D ** -0.5),
        "ffn_w_up": nrm(ks[21], (DEPTH, D, D_FF), D ** -0.5),
        "ffn_w_down": nrm(ks[22], (DEPTH, D_FF, D), D_FF ** -0.5),
        "final_norm": 1.0 + nrm(ks[23], (D,), 0.02),
    }

def first_block(x, c, mod_w, mod_b, norm_mix, norm_ffn, lru_w_in, lru_conv_w, lru_conv_b,
              lru_w_gates, lru_b_gates, lru_lambda, lru_w_out, kv_mod_w, kv_mod_b, kv_norm,
              w_kv, attn_w_q, attn_w_o, rel_bias, ffn_w_gate, ffn_w_up, ffn_w_down, final_norm):
    D = D_MODEL
    cs = jax.nn.silu(c)
    kv = None
    for l in range(DEPTH):
        if l == N_A_LAYERS:
            kv_mod = cs @ kv_mod_w + kv_mod_b
            kv = shared_kv(x, kv_mod[:, :D], kv_mod[:, D:], kv_norm, w_kv)
        mod = cs @ mod_w[l] + mod_b[l]
        sh_m, sc_m, g_m = mod[:, :D], mod[:, D:2 * D], mod[:, 2 * D:3 * D]
        sh_f, sc_f, g_f = mod[:, 3 * D:4 * D], mod[:, 4 * D:5 * D], mod[:, 5 * D:]
        h = modulate(rmsnorm(x, norm_mix[l]), sh_m, sc_m)
        if l < N_A_LAYERS:
            mix = rglru_mixer(h, lru_w_in[l], lru_conv_w[l], lru_conv_b[l], lru_w_gates[l],
                              lru_b_gates[l], lru_lambda[l], lru_w_out[l])
        else:
            j = l - N_A_LAYERS
            mix = moba_mixer(h, attn_w_q[j], attn_w_o[j], kv[0], kv[1], kv[2], rel_bias)
        x = x + g_m[:, None, :] * mix
        h = modulate(rmsnorm(x, norm_ffn[l]), sh_f, sc_f)
        x = x + g_f[:, None, :] * swiglu(h, ffn_w_gate[l], ffn_w_up[l], ffn_w_down[l])
    return rmsnorm(x, final_norm)


DEPTH_2 = 1

GRID_W = 64
NORM_EPS = 1e-6
RWKV_HEADS = 8
RWKV_HEAD = 64
RWKV_W = RWKV_HEADS * RWKV_HEAD
DECAY_LORA = 64
ICLR_LORA = 64
GATE_LORA = 128
VRES_LORA = 32
RWKV_LN_EPS = 64e-5
N_DIR = 2
RWKV_COLS = 3 * RWKV_W + N_DIR * DECAY_LORA + N_DIR * ICLR_LORA + GATE_LORA
POOL_WINDOWS = (2, 4, 8, 16)
POOL_GROUPS = len(POOL_WINDOWS)
POOL_GROUP_W = 128
POOL_W = POOL_GROUPS * POOL_GROUP_W
ATT_HEADS = 8
ATT_KV_HEADS = 2
ATT_GROUP = ATT_HEADS // ATT_KV_HEADS
ATT_HEAD = 64
ATT_W = ATT_HEADS * ATT_HEAD
ATT_COLS = (ATT_HEADS + 2 * ATT_KV_HEADS) * ATT_HEAD
ROPE_AXIS_DIM = ATT_HEAD // 2
ROPE_THETA = 10000.0
Q_BLOCK = 128
N_BRANCH = 3
GATE_COLS = N_BRANCH * D_MODEL
N_PROJ = RWKV_COLS + POOL_W + ATT_COLS + GATE_COLS
N_EXPERTS = 16
EXPERT_FF = 1024
CAPACITY_FACTOR = 2


def rms_norm(x, g, eps=NORM_EPS):
    xf = x.astype(jnp.float32)
    y = xf * lax.rsqrt(jnp.mean(xf * xf, axis=-1, keepdims=True) + eps)
    return (y * g.astype(jnp.float32)).astype(x.dtype)

def centred_token_shift(p, mu_prev, mu_next):
    zero = jnp.zeros_like(p[:, :1])
    p_prev = jnp.concatenate([zero, p[:, :-1]], axis=1)
    p_next = jnp.concatenate([p[:, 1:], zero], axis=1)
    return p + mu_prev * (p_prev - p) + mu_next * (p_next - p)

def _heads(z):
    return z.reshape(z.shape[:-1] + (RWKV_HEADS, RWKV_HEAD))

def rwkv7_bidir(p, hn, vres, v_first, w0, w2, a0, a2, g2, k_k, k_a, r_k, ln_w, ln_b):
    B, S, _ = p.shape
    f32 = jnp.float32
    dt = p.dtype
    pf = p.astype(f32)
    offs = np.cumsum([RWKV_W, RWKV_W, RWKV_W, N_DIR * DECAY_LORA, N_DIR * ICLR_LORA]).tolist()
    r, k, v, wd, ad, gd = jnp.split(pf, offs, axis=-1)
    wd = wd.reshape(B, S, N_DIR, DECAY_LORA)
    ad = ad.reshape(B, S, N_DIR, ICLR_LORA)
    w_raw = w0.astype(f32) + jnp.einsum('bsel,elc->bsec', jnp.tanh(wd), w2.astype(f32))
    decay = jnp.exp(-jnp.exp(-jax.nn.softplus(-w_raw) - 0.5))
    a = jax.nn.sigmoid(a0.astype(f32) + jnp.einsum('bsel,elc->bsec', ad, a2.astype(f32)))
    g = jnp.einsum('bsl,lc->bsc', jax.nn.sigmoid(gd), g2.astype(f32))
    if v_first is None:
        v_first = v
    else:
        v0, v1, v2 = vres
        mix = jax.nn.sigmoid(v0.astype(f32) + jnp.einsum('bsd,dl,lc->bsc', hn.astype(f32), v1.astype(f32), v2.astype(f32)))
        v = v + (v_first - v) * mix
    kk = _heads(k * k_k.astype(f32))
    kk = kk / jnp.maximum(jnp.linalg.norm(kk, axis=-1, keepdims=True), 1e-12)
    k_dir = k[:, :, None, :] * (1.0 + (a - 1.0) * k_a.astype(f32))

    def both(z):
        return jnp.stack([z, jnp.flip(z, 1)], axis=2)

    def per_dir(z):
        return jnp.stack([z[:, :, 0], jnp.flip(z[:, :, 1], 1)], axis=2)

    def time_major(z):
        return _heads(z).transpose(1, 2, 0, 3, 4)

    inputs = (time_major(both(r)), time_major(per_dir(decay)), time_major(per_dir(k_dir)),
              time_major(both(v)), both(kk).transpose(1, 2, 0, 3, 4), time_major(per_dir(a)))

    def step(state, inp):
        r_t, w_t, k_t, v_t, kk_t, a_t = inp
        sa = jnp.einsum('dbhij,dbhj->dbhi', state, -kk_t)
        state = (state * w_t[..., None, :] + sa[..., :, None] * (kk_t * a_t)[..., None, :]
                 + v_t[..., :, None] * k_t[..., None, :])
        return state, jnp.einsum('dbhij,dbhj->dbhi', state, r_t)

    state0 = jnp.zeros((N_DIR, B, RWKV_HEADS, RWKV_HEAD, RWKV_HEAD), f32)
    _, ys = lax.scan(step, state0, inputs)
    y = (ys[:, 0] + jnp.flip(ys[:, 1], 0)).transpose(1, 0, 2, 3)
    mu = jnp.mean(y, axis=-1, keepdims=True)
    var = jnp.mean(jnp.square(y - mu), axis=-1, keepdims=True)
    yn = (y - mu) * lax.rsqrt(var + RWKV_LN_EPS) * _heads(ln_w.astype(f32)) + _heads(ln_b.astype(f32))
    bonus = jnp.sum(_heads(r) * _heads(k_dir.sum(axis=2)) * _heads(r_k.astype(f32)), axis=-1, keepdims=True) * _heads(v)
    out = (yn + bonus).reshape(B, S, RWKV_W) * g
    return out.astype(dt), v_first

def multiscale_pool(z, pool_w, pool_scale):
    B, S, _ = z.shape
    zg = z.astype(jnp.float32).reshape(B, S, POOL_GROUPS, POOL_GROUP_W)
    csum = jnp.concatenate([jnp.zeros((B, 1, POOL_GROUPS, POOL_GROUP_W), jnp.float32), jnp.cumsum(zg, axis=1)], axis=1)
    t = jnp.arange(S)
    outs = []
    for gi, w in enumerate(POOL_WINDOWS):
        lo = w // 2
        hi = w - lo - 1
        start = jnp.clip(t - lo, 0, S)
        end = jnp.clip(t + hi + 1, 0, S)
        cnt = (end - start).astype(jnp.float32)
        outs.append((csum[:, end, gi] - csum[:, start, gi]) / cnt[None, :, None] - zg[:, :, gi])
    pooled = jnp.stack(outs, axis=2)
    y = jnp.einsum('bsgc,gcd->bsgd', pooled, pool_w.astype(jnp.float32)).reshape(B, S, POOL_W)
    return (y * pool_scale.astype(jnp.float32)).astype(z.dtype)

def axial_rope(seq):
    rows = seq // GRID_W
    row = jnp.repeat(jnp.arange(rows, dtype=jnp.float32), GRID_W)
    col = jnp.tile(jnp.arange(GRID_W, dtype=jnp.float32), rows)
    freqs = ROPE_THETA ** (-jnp.arange(0, ROPE_AXIS_DIM, 2, dtype=jnp.float32) / ROPE_AXIS_DIM)
    ang = jnp.concatenate([row[:, None] * freqs, col[:, None] * freqs], axis=-1)
    return jnp.cos(ang), jnp.sin(ang)

def apply_rope(x, cos, sin):
    xp = x.reshape(x.shape[:-1] + (ATT_HEAD // 2, 2))
    x0, x1 = xp[..., 0], xp[..., 1]
    c = cos[None, :, None, :]
    s = sin[None, :, None, :]
    return jnp.stack([x0 * c - x1 * s, x0 * s + x1 * c], axis=-1).reshape(x.shape)

def gqa_axial(p_att, q_norm, k_norm):
    B, S, _ = p_att.shape
    dt = p_att.dtype
    q, k, v = jnp.split(p_att, [ATT_W, ATT_W + ATT_KV_HEADS * ATT_HEAD], axis=-1)
    q = rms_norm(q.reshape(B, S, ATT_HEADS, ATT_HEAD), q_norm).astype(jnp.float32)
    k = rms_norm(k.reshape(B, S, ATT_KV_HEADS, ATT_HEAD), k_norm).astype(jnp.float32)
    cos, sin = axial_rope(S)
    q = (apply_rope(q, cos, sin) * (ATT_HEAD ** -0.5)).astype(dt)
    k = apply_rope(k, cos, sin).astype(dt)
    v = v.reshape(B, S, ATT_KV_HEADS, ATT_HEAD)
    n_blocks = S // Q_BLOCK
    q_blocks = q.reshape(B, n_blocks, Q_BLOCK, ATT_KV_HEADS, ATT_GROUP, ATT_HEAD).transpose(1, 0, 3, 4, 2, 5)
    k_t = k.transpose(0, 2, 1, 3)
    v_t = v.transpose(0, 2, 1, 3)

    def block(qb):
        s = jnp.einsum('bkgqd,bksd->bkgqs', qb, k_t).astype(jnp.float32)
        pr = jax.nn.softmax(s, axis=-1).astype(dt)
        return jnp.einsum('bkgqs,bksd->bkgqd', pr, v_t)

    o = lax.map(block, q_blocks)
    return o.transpose(1, 0, 4, 2, 3, 5).reshape(B, S, ATT_W)

def expert_choice_ffn(h, router, w_gate, w_up, w_down):
    B, S, D = h.shape
    cap = CAPACITY_FACTOR * S // N_EXPERTS
    aff = jax.nn.softmax(jnp.einsum('bsd,de->bse', h, router).astype(jnp.float32), axis=-1)
    vals, idx = lax.top_k(aff.transpose(0, 2, 1), cap)
    xg = jax.vmap(lambda hb, ib: hb[ib])(h, idx)
    hid = jax.nn.silu(jnp.einsum('becd,edf->becf', xg, w_gate)) * jnp.einsum('becd,edf->becf', xg, w_up)
    y = jnp.einsum('becf,efd->becd', hid, w_down) * vals[..., None].astype(h.dtype)
    return jax.vmap(lambda ib, yb: jnp.zeros((S, D), yb.dtype).at[ib.reshape(-1)].add(yb.reshape(-1, D)))(idx, y)

def second_inputs(seed: int = 0) -> dict:
    key = jax.random.key(seed)
    ks = iter(jax.random.split(key, 40))

    def nrm(shape, scale):
        return jax.random.normal(next(ks), shape, jnp.float32) * scale

    def uni(shape, lo, hi):
        return jax.random.uniform(next(ks), shape, jnp.float32, lo, hi)

    L = DEPTH_2
    Lv = DEPTH_2 - 1
    return {
        'x': nrm((BATCH, SEQ, D_MODEL), 1.0),
        'norm_mix': 1.0 + nrm((L, D_MODEL), 0.05),
        'w_in': nrm((L, D_MODEL, N_PROJ), D_MODEL ** -0.5),
        'shift_prev': uni((L, RWKV_COLS), 0.0, 0.5),
        'shift_next': uni((L, RWKV_COLS), 0.0, 0.5),
        'rwkv_w0': uni((L, N_DIR, RWKV_W), -5.0, 1.0),
        'rwkv_w2': nrm((L, N_DIR, DECAY_LORA, RWKV_W), 0.5 * DECAY_LORA ** -0.5),
        'rwkv_a0': nrm((L, N_DIR, RWKV_W), 0.5),
        'rwkv_a2': nrm((L, N_DIR, ICLR_LORA, RWKV_W), ICLR_LORA ** -0.5),
        'rwkv_g2': nrm((L, GATE_LORA, RWKV_W), GATE_LORA ** -0.5),
        'rwkv_k_k': 0.85 + nrm((L, RWKV_W), 0.05),
        'rwkv_k_a': 1.0 + nrm((L, RWKV_W), 0.05),
        'rwkv_r_k': nrm((L, RWKV_W), 0.1),
        'rwkv_ln_w': 1.0 + nrm((L, RWKV_W), 0.05),
        'rwkv_ln_b': nrm((L, RWKV_W), 0.02),
        'vres_v0': 0.5 + nrm((Lv, RWKV_W), 0.3),
        'vres_w1': nrm((Lv, D_MODEL, VRES_LORA), D_MODEL ** -0.5),
        'vres_w2': nrm((Lv, VRES_LORA, RWKV_W), VRES_LORA ** -0.5),
        'pool_w': nrm((L, POOL_GROUPS, POOL_GROUP_W, POOL_GROUP_W), POOL_GROUP_W ** -0.5),
        'pool_scale': 1.0 + nrm((L, POOL_W), 0.1),
        'q_norm': 1.0 + nrm((L, ATT_HEAD), 0.05),
        'k_norm': 1.0 + nrm((L, ATT_HEAD), 0.05),
        'w_branch_rwkv': nrm((L, RWKV_W, D_MODEL), RWKV_W ** -0.5),
        'w_branch_pool': nrm((L, POOL_W, D_MODEL), POOL_W ** -0.5),
        'w_branch_attn': nrm((L, ATT_W, D_MODEL), ATT_W ** -0.5),
        'w_out': nrm((L, D_MODEL, D_MODEL), D_MODEL ** -0.5),
        'norm_ffn': 1.0 + nrm((L, D_MODEL), 0.05),
        'router': nrm((L, D_MODEL, N_EXPERTS), D_MODEL ** -0.5),
        'exp_gate': nrm((L, N_EXPERTS, D_MODEL, EXPERT_FF), D_MODEL ** -0.5),
        'exp_up': nrm((L, N_EXPERTS, D_MODEL, EXPERT_FF), D_MODEL ** -0.5),
        'exp_down': nrm((L, N_EXPERTS, EXPERT_FF, D_MODEL), EXPERT_FF ** -0.5),
        'norm_final': 1.0 + nrm((D_MODEL,), 0.05),
    }

def second_block(x, norm_mix, w_in, shift_prev, shift_next, rwkv_w0, rwkv_w2, rwkv_a0, rwkv_a2, rwkv_g2,
              rwkv_k_k, rwkv_k_a, rwkv_r_k, rwkv_ln_w, rwkv_ln_b, vres_v0, vres_w1, vres_w2,
              pool_w, pool_scale, q_norm, k_norm, w_branch_rwkv, w_branch_pool, w_branch_attn, w_out,
              norm_ffn, router, exp_gate, exp_up, exp_down, norm_final):
    B, S, D = x.shape
    split_at = [RWKV_COLS, RWKV_COLS + POOL_W, RWKV_COLS + POOL_W + ATT_COLS]
    v_first = None
    for l in range(DEPTH_2):
        hn = rms_norm(x, norm_mix[l])
        proj = jnp.einsum('bsd,dn->bsn', hn, w_in[l])
        p_rwkv, p_pool, p_att, p_gate = jnp.split(proj, split_at, axis=-1)
        p_rwkv = centred_token_shift(p_rwkv, shift_prev[l], shift_next[l])
        vres = None if l == 0 else (vres_v0[l - 1], vres_w1[l - 1], vres_w2[l - 1])
        y_a, v_first = rwkv7_bidir(p_rwkv, hn, vres, v_first, rwkv_w0[l], rwkv_w2[l], rwkv_a0[l], rwkv_a2[l],
                                   rwkv_g2[l], rwkv_k_k[l], rwkv_k_a[l], rwkv_r_k[l], rwkv_ln_w[l], rwkv_ln_b[l])
        y_b = multiscale_pool(p_pool, pool_w[l], pool_scale[l])
        y_c = gqa_axial(p_att, q_norm[l], k_norm[l])
        gates = jax.nn.sigmoid(p_gate).reshape(B, S, N_BRANCH, D)
        merged = (gates[:, :, 0] * (y_a @ w_branch_rwkv[l]) + gates[:, :, 1] * (y_b @ w_branch_pool[l])
                  + gates[:, :, 2] * (y_c @ w_branch_attn[l]))
        x = x + merged @ w_out[l]
        x = x + expert_choice_ffn(rms_norm(x, norm_ffn[l]), router[l], exp_gate[l], exp_up[l], exp_down[l])
    return rms_norm(x, norm_final)


def setup_inputs(seed=0):
    out = dict(first_inputs(seed))
    for name, value in second_inputs(seed + 1).items():
        if name != "x":
            out[name + "_2"] = value
    return out


def reference(
    x, c, mod_w, mod_b, norm_mix, norm_ffn, lru_w_in, lru_conv_w, lru_conv_b, lru_w_gates,
    lru_b_gates, lru_lambda, lru_w_out, kv_mod_w, kv_mod_b, kv_norm, w_kv, attn_w_q, attn_w_o,
    rel_bias, ffn_w_gate, ffn_w_up, ffn_w_down, final_norm, norm_mix_2, w_in_2, shift_prev_2,
    shift_next_2, rwkv_w0_2, rwkv_w2_2, rwkv_a0_2, rwkv_a2_2, rwkv_g2_2, rwkv_k_k_2, rwkv_k_a_2,
    rwkv_r_k_2, rwkv_ln_w_2, rwkv_ln_b_2, vres_v0_2, vres_w1_2, vres_w2_2, pool_w_2,
    pool_scale_2, q_norm_2, k_norm_2, w_branch_rwkv_2, w_branch_pool_2, w_branch_attn_2,
    w_out_2, norm_ffn_2, router_2, exp_gate_2, exp_up_2, exp_down_2, norm_final_2,
):
    x = first_block(
        x, c, mod_w, mod_b, norm_mix, norm_ffn, lru_w_in, lru_conv_w, lru_conv_b, lru_w_gates,
        lru_b_gates, lru_lambda, lru_w_out, kv_mod_w, kv_mod_b, kv_norm, w_kv, attn_w_q,
        attn_w_o, rel_bias, ffn_w_gate, ffn_w_up, ffn_w_down, final_norm,
    )
    return second_block(
        x, norm_mix_2, w_in_2, shift_prev_2, shift_next_2, rwkv_w0_2, rwkv_w2_2, rwkv_a0_2,
        rwkv_a2_2, rwkv_g2_2, rwkv_k_k_2, rwkv_k_a_2, rwkv_r_k_2, rwkv_ln_w_2, rwkv_ln_b_2,
        vres_v0_2, vres_w1_2, vres_w2_2, pool_w_2, pool_scale_2, q_norm_2, k_norm_2,
        w_branch_rwkv_2, w_branch_pool_2, w_branch_attn_2, w_out_2, norm_ffn_2, router_2,
        exp_gate_2, exp_up_2, exp_down_2, norm_final_2,
    )


_drawn_inputs = setup_inputs


def setup_inputs(seed=0):
    import zlib

    import numpy as np

    out = dict(_drawn_inputs(seed))
    spreads = {}
    factors = {'norm_mix': 5.992,
     'norm_ffn': 4.035,
     'lru_b_gates': 8.0,
     'kv_mod_b': 5.261,
     'kv_norm': 8.0,
     'rel_bias': 3.622,
     'rwkv_w2_2': 4.364,
     'rwkv_k_k_2': 3.687,
     'rwkv_ln_w_2': 3.194,
     'rwkv_ln_b_2': 7.976,
     'q_norm_2': 8.0,
     'k_norm_2': 8.0,
     'norm_ffn_2': 2.979}
    for name, (base, spread) in spreads.items():
        noise = np.random.default_rng([zlib.crc32(name.encode()), seed]).standard_normal(out[name].shape)
        drawn = base * np.exp(spread * noise) if base else spread * noise
        out[name] = __import__('jax').numpy.asarray(drawn.astype(out[name].dtype))
    for name, factor in factors.items():
        out[name] = (out[name] * factor).astype(out[name].dtype)
    return out
```

```python
import contextlib
import math

import numpy as np
import concourse.bass as bass
from concourse import mybir

F32 = mybir.dt.float32
ALU = mybir.AluOpType
ACT = mybir.ActivationFunctionType
AX = mybir.AxisListType.X

P = 128
T = 256
NT = T // P
D = 1024
KD = D // P
LRU = 1280
KL = LRU // P
LRU_HEADS = 5
FF = 2816
KF = FF // P
HEADS, KV_HEADS, HD = 8, 4, 128
BUCKETS, MAX_DIST = 32, 128
NEG = -1e30
RW = 512
KR = RW // P
RWKV_COLS, POOL_W, ATT_COLS, GATE_COLS = 1920, 512, 768, 3072
WINDOWS = (2, 4, 8, 16)
EXPERTS, EFF, CAP = 16, 1024, 32
EPS = 1e-6
LN_EPS = 64e-5

SLOTS = 6
TPC = 32
LEVELS = 7



def columns():
    sizes = [
        ("c", KD), ("mod_b", 112), ("norm_mix0", KD), ("norm_mix1", KD), ("norm_ffn0", KD), ("norm_ffn1", KD),
        ("kv_norm", KD), ("final_norm", KD), ("conv_w", 4 * KL), ("conv_b", KL), ("b_gates", 2 * KL),
        ("lambda", KL), ("norm_mix_2", KD), ("shift_prev", 15), ("shift_next", 15), ("w0", 2 * KR),
        ("a0", 2 * KR), ("k_k", KR), ("k_a", KR), ("r_k", KR), ("ln_w", KR), ("ln_b", KR), ("pool_scale", KR),
        ("q_norm", 1), ("k_norm", 1), ("norm_ffn_2", KD), ("norm_final", KD), ("rel_bias", HEADS),
        ("w2", RW), ("a2", RW), ("g2", RW), ("pool_w", 4 * P), ("router", KD * EXPERTS),
        ("eps", 1), ("ln_eps", 1), ("zero", 1), ("one", 1), ("iota", CAP),
        ("ident", P), ("ones", P), ("blk", P), ("pair", P), ("half", P),
        ("cos", T), ("sin", T), ("inv_cnt", 4 * T), ("onehot", 2 * T),
        ("strict", 2 * P), ("incl", 2 * P), ("level", LEVELS * P),
    ]
    at, out = 0, {}
    for name, n in sizes:
        out[name] = (at, n)
        at += n
    return out, at


COLS, NCOLS = columns()
SEGMENTS = [
    ("mods", 112 * KD), ("lru_in", 20 * KD), ("lru_gates", LRU_HEADS * 8), ("lru_out", KD * KL),
    ("ffn0_gu", 2 * KF * KD), ("ffn0_down", KD * KF), ("k", KV_HEADS * KD), ("v", KV_HEADS * KD),
    ("q", HEADS * KD), ("o", KD * HEADS), ("ffn1_gu", 2 * KF * KD), ("ffn1_down", KD * KF),
    ("in2_main", 25 * KD), ("gates_branches", 24 * (KD + KR)), ("out2", KD * KD), ("experts", EXPERTS * 3 * KD * KD),
]
NTILES = sum(n for _, n in SEGMENTS)
NCHUNKS = NTILES // TPC
assert NTILES % TPC == 0



class Counter:
    def __init__(self, sem):
        self.sem, self.count = sem, 0


class Loop:
    def __init__(self, n):
        self.n, self.entry, self.per = n, {}, {}


class Token:

    def __init__(self, counter, value, loop):
        self.counter, self.value, self.loop = counter, value, loop


class Later:

    def __init__(self):
        self.tok = None


class Engine:

    def __init__(self, prog, name, counter):
        self.prog, self.name, self.c = prog, name, counter
        self.ops, self.seen = [], {}

    def wait(self, *toks):
        for t in toks:
            if t is None:
                continue
            if isinstance(t, (list, tuple)):
                self.wait(*t)
                continue
            if isinstance(t, Later):
                self.ops.append(("wait", t, self.prog.loop))
                continue
            key = (id(t.counter), id(t.loop))
            if self.seen.get(key, -1) < t.value:
                self.seen[key] = t.value
                self.ops.append(("wait", t, self.prog.loop))

    def do(self, fn, *toks, counter=None):
        self.wait(*toks)
        c = counter or self.c
        c.count += 1
        self.ops.append(("op", fn, c))
        return Token(c, c.count, self.prog.loop)

    def run(self, fn, *toks):
        self.wait(*toks)
        self.ops.append(("op", fn, None))

    def last(self):
        return Token(self.c, self.c.count, self.prog.loop) if self.c.count else None

    def emit(self, e, ops=None, i=None):
        for op in self.ops if ops is None else ops:
            if op[0] == "wait":
                _, t, here = op
                late = isinstance(t, Later)
                t = t.tok if late else t
                v = t.value
                if t.loop is not None:
                    per = t.loop.per[t.counter]
                    if t.loop is here:
                        v = (v - per if late else v) + i * per
                    else:
                        v = v + (t.loop.n - 1) * per
                e.wait_ge(t.counter.sem, v)
            elif op[0] == "op16":
                op[1](e, i).then_inc(op[2].sem, 16)
            elif op[0] == "op":
                ins = op[1](e, i)
                if op[2] is not None:
                    ins.then_inc(op[2].sem, 1)
            else:
                with e.Fori(0, op[1]) as j:
                    self.emit(e, op[2], j)


class Program:
    def __init__(self, nc, ctx):
        self.nc, self.ctx, self.loop = nc, ctx, None
        self.counters = []
        self.pe, self.dve, self.act, self.pool = [
            Engine(self, n, self.counter(n)) for n in ("pe_done", "dve_done", "act_done", "pool_done")]
        self.engines = [self.pe, self.dve, self.act, self.pool]

    def counter(self, name):
        c = Counter(self.ctx.enter_context(self.nc.semaphore(name)))
        self.counters.append(c)
        return c

    def all_join(self):
        last = [e.last() for e in self.engines]
        for e in self.engines:
            e.wait(*last)

    @contextlib.contextmanager
    def repeat(self, n):
        loop = Loop(n)
        loop.entry = {c: c.count for c in self.counters}
        outer = [(e.ops, e.seen) for e in self.engines]
        for e in self.engines:
            e.ops, e.seen = [], {}
        self.loop = loop
        first_tile = self.feed.tiles
        yield loop
        self.loop = None
        taken = self.feed.tiles - first_tile
        assert taken % (SLOTS * TPC) == 0, "a chunk's slot is the same in every iteration"
        self.feed.tiles = first_tile + n * taken
        for c in self.counters:
            loop.per[c] = c.count - loop.entry[c]
            c.count = loop.entry[c] + n * loop.per[c]
        for e, (ops, seen) in zip(self.engines, outer):
            body = e.ops
            e.ops, e.seen = ops, seen
            if body:
                e.ops.append(("loop", n, body))


class Banks:

    def __init__(self, banks):
        self.banks, self.reader, self.at = banks, [None] * len(banks), 0

    def take(self):
        b = self.at
        self.at = (b + 1) % len(self.banks)
        return b, self.banks[b], self.reader[b]


class Feed:

    def __init__(self, prog, ring):
        self.prog, self.ring = prog, ring
        self.filled = [prog.counter(f"filled{s}") for s in range(SLOTS)]
        self.freed = prog.counter("freed")
        self.tiles = 0

    def tile(self, n=1):
        k = self.tiles % TPC
        assert k + n <= TPC
        s = self.tiles // TPC % SLOTS
        if k == 0:
            c = self.filled[s]
            c.count += 16
            self.prog.pe.wait(Token(c, c.count, self.prog.loop))
        self.tiles += n
        return self.ring[:, (s * TPC + k) * P:(s * TPC + k + n) * P]

    def ends_chunk(self):
        return self.tiles % TPC == 0


class Arena:
    def __init__(self, t, n):
        self.t, self.n, self.at, self.high = t, n, 0, 0

    def take(self, n):
        a = self.t[:, self.at:self.at + n]
        self.at += n
        self.high = max(self.high, self.at)
        assert self.at <= self.n, (self.at, self.n)
        return a


def tiles(ap, n):
    return ap.rearrange("p (a b) -> p a b", b=n)


def build(nc, weights, packed, x_in, bias_scratch, out):
    with contextlib.ExitStack() as ctx:
        pr = Program(nc, ctx)
        PE, V, A, G = pr.pe, pr.dve, pr.act, pr.pool

        def sbuf(name, n):
            return ctx.enter_context(nc.sbuf_tensor(name, [P, n], F32))

        ring = sbuf("weight_ring", SLOTS * TPC * P)
        pk = sbuf("packed_consts", NCOLS)
        xT_ = sbuf("residual_T", KD * T)
        hT_ = sbuf("normed_T", KD * T)
        mod = sbuf("modulation", 112)
        gain = sbuf("norm_gain", KD)
        silu_c = sbuf("silu_c", 3 * KD)
        rstd = sbuf("rstd", 3 * T)
        NAR = (nc.sbuf_bytes_remaining // 4 - 64) if not callable(nc.sbuf_bytes_remaining) else nc.sbuf_bytes_remaining() // 4 - 64
        arena = Arena(sbuf("arena", NAR), NAR)
        banks = Banks([ctx.enter_context(nc.psum_tensor(f"bank{b}", [P, 512], F32)) for b in range(8)])
        feed = pr.feed = Feed(pr, ring)
        s_in, s_x, s_bias_w, s_bias_r, s_out = [pr.counter(n) for n in ("in", "x_in", "bias_w", "bias_r", "out")]
        packed_in = Token(s_in, 16, None)
        x_loaded = Token(s_x, 16, None)

        xT, hT = tiles(xT_[:, :], T), tiles(hT_[:, :], T)

        def col(name, j=0, n=1):
            a = COLS[name][0] + j
            return pk[:, a:a + n]

        ident, ones, blk = col("ident", 0, P), col("ones", 0, P), col("blk", 0, P)

        for e in pr.engines:
            e.wait(packed_in)

        def mm(out, lhsT, rhs, start, stop, *toks, signal=False, weight=False):
            fn = lambda e, i: e.matmul(out(i) if callable(out) else out, lhsT, rhs(i) if callable(rhs) else rhs,
                                       start=start, stop=stop, skip_group_check=True)
            if weight and feed.ends_chunk():
                return PE.do(fn, *toks, counter=feed.freed)
            if signal:
                return PE.do(fn, *toks)
            PE.run(fn, *toks)

        def flip(out, in_, *toks, signal=True):
            n = in_.shape[0]
            fn = lambda e, i: e.transpose(out, in_, ident[0:n, 0:n])
            if signal:
                return PE.do(fn, *toks)
            PE.run(fn, *toks)

        def r(x, i):
            return x(i) if callable(x) else x

        def tt(eng, out, a, b, op, *toks):
            return eng.do(lambda e, i: e.tensor_tensor(r(out, i), r(a, i), r(b, i), op), *toks)

        def ts(eng, out, a, s1, s2, op0, op1, *toks):
            return eng.do(lambda e, i: e.tensor_scalar(r(out, i), r(a, i), r(s1, i), r(s2, i), op0, op1)
                          if s2 is not None else e.tensor_scalar(r(out, i), r(a, i), r(s1, i), None, op0), *toks)

        def stt(out, a, s, b, op0, op1, *toks):
            return V.do(lambda e, i: e.scalar_tensor_tensor(out=r(out, i), in0=r(a, i), scalar=r(s, i), in1=r(b, i),
                                                           op0=op0, op1=op1), *toks)

        def act(out, in_, f, *toks, **kw):
            return A.do(lambda e, i: e.activation(r(out, i), r(in_, i), f, **{k: r(v, i) for k, v in kw.items()}), *toks)

        def copy(eng, out, in_, *toks):
            if eng is A:
                return act(out, in_, ACT.Copy, *toks)
            if callable(out) or callable(in_):
                return eng.do(lambda e, i: e.tensor_scalar(r(out, i), r(in_, i), 1.0, None, ALU.mult), *toks)
            return eng.do(lambda e, i: e.tensor_copy(out, in_), *toks)

        def recip(out, in_, *toks):
            return V.do(lambda e, i: e.reciprocal(r(out, i), r(in_, i)), *toks)

        def sigmoid(out, in_, *toks, half_bias=None):
            kw = {"scale": 0.5}
            if half_bias is not None:
                kw["bias"] = half_bias
            t = act(out, in_, ACT.Tanh, *toks, **kw)
            return ts(V, out, out, 0.5, 0.5, ALU.mult, ALU.add, t)

        def linear(n_tiles, kt, rhs, ready, read):
            for n in range(n_tiles):
                b, bank, before = banks.take()
                for k in range(kt):
                    w = feed.tile()
                    t = mm(bank[:, 0:T], w, rhs(k), k == 0, k == kt - 1, before if k == 0 else None, ready(k),
                           signal=k == kt - 1, weight=True)
                banks.reader[b] = read(n, bank[:, 0:T], t)
            return t

        def rms_rstd(src, scratch, *toks):
            b, bank, before = banks.take()
            sq = tiles(scratch, T)
            for k in range(KD):
                q = tt(V, sq[:, k, :], src[:, k, :], src[:, k, :], ALU.mult, *toks)
                t = mm(bank[:, 0:T], ones, sq[:, k, :], k == 0, k == KD - 1, before, q, signal=k == KD - 1)
            banks.reader[b] = t2 = inv_sqrt(rstd, bank[:, 0:T], 1.0 / D, EPS, "eps", T, t)
            return t2

        def inv_sqrt(buf, src, scale, eps, eps_col, n, *toks):
            y, z, w = buf[:, 0:n], buf[:, n:2 * n], buf[:, 2 * n:3 * n]
            t0 = ts(V, z, src, scale, eps, ALU.mult, ALU.add, *toks)
            t = act(y, z, ACT.Ln, t0)
            t = act(y, y, ACT.Exp, t, scale=-0.5)
            t = tt(V, w, y, y, ALU.mult, t)
            t = tt(V, w, w, z, ALU.mult, t)
            t = ts(V, w, w, -0.5, 1.5, ALU.mult, ALU.add, t)
            return tt(V, y, y, w, ALU.mult, t)

        def modulated(dst, g_name, shift, scale, scratch, *toks):
            tg = stt(gain[:, :], scale, 1.0, col(g_name, 0, KD), ALU.add, ALU.mult, *toks) if scale is not None else \
                copy(V, gain[:, :], col(g_name, 0, KD), *toks)
            t = rms_rstd(xT, scratch, *toks)
            done = []
            for k in range(KD):
                tk = stt(dst[:, k, :], xT[:, k, :], gain[:, k:k + 1], rstd[:, 0:T], ALU.mult, ALU.mult, t, tg)
                if shift is not None:
                    tk = act(dst[:, k, :], dst[:, k, :], ACT.Identity, tk, bias=shift[:, k:k + 1])
                done.append(tk)
            return done

        def residual(gate):
            def read(n, ps, t):
                if gate is None:
                    return tt(V, xT[:, n, :], ps, xT[:, n, :], ALU.add, t)
                return stt(xT[:, n, :], ps, gate[:, n:n + 1], xT[:, n, :], ALU.mult, ALU.add, t)
            return read

        def swiglu(h, ready, gate):
            arena.at = 0
            hid = tiles(arena.take(KF * T), T)
            sig = [arena.take(T) for _ in range(2)]
            done, free = [], [None, None]
            for f in range(KF):
                bg, gbank, g_before = banks.take()
                bu, ubank, u_before = banks.take()
                for bank, before in ((gbank, g_before), (ubank, u_before)):
                    for k in range(KD):
                        w = feed.tile()
                        t = mm(bank[:, 0:T], w, h[:, k, :], k == 0, k == KD - 1, before, ready[k],
                               signal=k == KD - 1, weight=True)
                    if bank is gbank:
                        tg = t
                s = sig[f % 2]
                t1 = act(s, gbank[:, 0:T], ACT.Tanh, tg, free[f % 2], scale=0.5)
                t1 = stt(s, s, 1.0, gbank[:, 0:T], ALU.add, ALU.mult, t1)
                banks.reader[bg] = t1
                t1 = stt(hid[:, f, :], s, 0.5, ubank[:, 0:T], ALU.mult, ALU.mult, t1, t)
                banks.reader[bu] = free[f % 2] = t1
                done.append(t1)
            linear(KD, KF, lambda k: hid[:, k, :], lambda k: done[k], residual(gate))

        xin = tiles(arena.take(NT * D), D)
        for c0 in range(0, KD, 2):
            b, bank, before = banks.take()
            for c in (c0, c0 + 1):
                for m in range(NT):
                    t = flip(bank[:, (c - c0) * T + m * P:(c - c0) * T + (m + 1) * P], xin[:, m, c * P:(c + 1) * P],
                             x_loaded, before)
            banks.reader[b] = copy(V, xT_[:, c0 * T:(c0 + 2) * T], bank[:, :], t)

        t = sigmoid(silu_c[:, 0:KD], col("c", 0, KD))
        t_silu = tt(V, silu_c[:, 0:KD], silu_c[:, 0:KD], col("c", 0, KD), ALU.mult, t)
        PE.wait(t_silu)
        pr.all_join()
        N_LOOP = 4 * SLOTS * 4
        def mod_tiles(n, bank, before):
            for j in range(n):
                for k in range(KD):
                    w = feed.tile()
                    t = mm(bank[:, j:j + 1], w, silu_c[:, k:k + 1], k == 0, k == KD - 1,
                           before if (j, k) == (0, 0) else None, signal=(k == KD - 1), weight=True)
            return t
        with pr.repeat(4):
            read = Later()
            t = mod_tiles(24, banks.banks[0], read)
            bias_at = COLS["mod_b"][0]
            read.tok = tt(V, lambda i: mod[:, bass.ds(i * 24, 24)], banks.banks[0][:, 0:24],
                          lambda i: pk[:, bass.ds(i * 24 + bias_at, 24)], ALU.add, t)
        t = mod_tiles(16, banks.banks[1], None)
        t_mod = tt(V, mod[:, N_LOOP:112], banks.banks[1][:, 0:16], col("mod_b", N_LOOP, 16), ALU.add, t)
        pr.all_join()

        def mods(layer, j):
            return mod[:, layer * 48 + j * KD:layer * 48 + (j + 1) * KD]

        arena.at = 0
        y_br = arena.take(KL * T)
        XW = T + 3
        xpad = tiles(arena.take(KL * XW), XW)
        xc = arena.take(KL * T)
        rg = arena.take(KL * T)
        ig = arena.take(KL * T)
        cvec = arena.take(4 * KL)
        h = modulated(hT, "norm_mix0", mods(0, 0), mods(0, 1), rg[:, 0:KD * T])
        t_pad = G.do(lambda e, i: e.memset(xpad[:, :, 0:3], 0.0))

        def lru_in_read(n, ps, t):
            if n < KL:
                return copy(A, y_br[:, n * T:(n + 1) * T], ps, t)
            return copy(V, xpad[:, n - KL, 3:XW], ps, t)
        linear(2 * KL, KD, lambda k: hT[:, k, :], lambda k: h[k], lru_in_read)
        t_y = A.last()
        t_x = V.last()
        gl = rg[:, :]
        t = tt(G, gl, y_br, y_br, ALU.mult, t_y, t_x)
        t = ts(G, gl, gl, 0.044715, 1.0, ALU.mult, ALU.add, t)
        t = tt(G, gl, gl, y_br, ALU.mult, t)
        t = act(gl, gl, ACT.Tanh, t, scale=math.sqrt(2.0 / math.pi))
        t = ts(G, gl, gl, 0.5, 0.5, ALU.mult, ALU.add, t)
        t_gelu = tt(G, y_br, y_br, gl, ALU.mult, t)
        conv_done = []
        for n in range(KL):
            o = xc[:, n * T:(n + 1) * T]
            t = ts(V, o, xpad[:, n, 0:T], col("conv_w", n), col("conv_b", n), ALU.mult, ALU.add, t_x, t_pad)
            for k in range(1, 4):
                t = stt(o, xpad[:, n, k:k + T], col("conv_w", k * KL + n), o, ALU.mult, ALU.add, t)
            conv_done.append(t)
        t = act(cvec[:, 2 * KL:3 * KL], col("lambda", 0, KL), ACT.Exp, scale=-1.0)
        t = act(cvec[:, 2 * KL:3 * KL], cvec[:, 2 * KL:3 * KL], ACT.Ln, t, bias=col("one"))
        t = ts(V, cvec[:, 3 * KL:4 * KL], cvec[:, 2 * KL:3 * KL], -8.0, None, ALU.mult, None, t)
        t_cv = ts(V, cvec[:, 2 * KL:3 * KL], cvec[:, 2 * KL:3 * KL], 8.0, None, ALU.mult, None, t)
        for hh in range(LRU_HEADS):
            def gate_read(n, ps, t, hh=hh):
                dst = (rg if n < 2 else ig)[:, (2 * hh + n % 2) * T:(2 * hh + n % 2 + 1) * T]
                t1 = ts(V, dst, ps, col("b_gates", (n // 2) * KL + 2 * hh + n % 2), -80.0, ALU.add, ALU.max, t, t_gelu)
                act(dst, dst, ACT.Exp, t1, scale=-1.0)
                return t1
            linear(4, 2, lambda k: xc[:, (2 * hh + k) * T:(2 * hh + k + 1) * T], lambda k: conv_done[2 * hh + k], gate_read)
        t_e = A.last()
        t = ts(V, rg, rg, 1.0, None, ALU.add, None, t_e)
        t_r = recip(rg, rg, t)
        t = ts(V, ig, ig, 1.0, None, ALU.add, None, t_e)
        t = recip(ig, ig, t)
        t_ix = tt(G, xc, xc, ig, ALU.mult, t)
        a_buf = [xpad[:, n, 0:T] for n in range(KL)]
        ta = []
        for n in range(KL):
            s = slice(n * T, (n + 1) * T)
            ta.append(act(a_buf[n], rg[:, s], ACT.Exp, t_r, t_cv, conv_done[-1], scale=cvec[:, 3 * KL + n:3 * KL + n + 1]))
            t = act(rg[:, s], rg[:, s], ACT.Tanh, ta[-1], scale=cvec[:, 2 * KL + n:2 * KL + n + 1])
        t_th = t
        t = ts(V, ig, rg, 1.0, None, ALU.add, None, t_th, t_ix)
        t = recip(ig, ig, t)
        t = stt(rg, rg, 2.0, ig, ALU.mult, ALU.mult, t)
        t = act(rg, rg, ACT.Sqrt, t)
        t_b = tt(V, xc, xc, rg, ALU.mult, t, t_ix)
        z_done = []
        for n in range(KL):
            s = slice(n * T, (n + 1) * T)
            t = V.do(lambda e, i, n=n, s=s: e.tensor_tensor_scan(rg[:, s], a_buf[n], xc[:, s], 0.0, ALU.mult, ALU.add),
                     t_b, ta[n])
            z_done.append(tt(V, ig[:, s], rg[:, s], y_br[:, s], ALU.mult, t, t_gelu))
        linear(KD, KL, lambda k: ig[:, k * T:(k + 1) * T], lambda k: z_done[k], residual(mods(0, 2)))
        pr.all_join()

        def ffn(layer):
            arena.at = 0
            h = modulated(hT, f"norm_ffn{layer}", mods(layer, 3), mods(layer, 4), arena.take(KD * T))
            V.wait(*[x for x in h])
            pr.all_join()
            swiglu(hT, h, mods(layer, 5))
            pr.all_join()
        ffn(0)

        arena.at = 0
        KT = tiles(arena.take(KV_HEADS * T), T)
        VV = tiles(arena.take(NT * KV_HEADS * HD), KV_HEADS * HD)
        QT = tiles(arena.take(HEADS * T), T)
        OT = tiles(arena.take(HEADS * T), T)
        HB = tiles(arena.take(HEADS * T), T)
        scratch = arena.take(KD * T)
        h = modulated(hT, "kv_norm", mod[:, 96:96 + KD], mod[:, 96 + KD:112], scratch)
        linear(KV_HEADS, KD, lambda k: hT[:, k, :], lambda k: h[k], lambda n, ps, t: copy(A, KT[:, n, :], ps, t))
        (b0, v0, f0), (b1, v1, f1) = banks.take(), banks.take()
        for k in range(KD):
            w = feed.tile(4)
            t0 = mm(v0[:, :], hT[:, k, 0:P], w, k == 0, k == KD - 1, f0, h[k], signal=k == KD - 1)
            t1 = mm(v1[:, :], hT[:, k, P:T], w, k == 0, k == KD - 1, f1, signal=k == KD - 1, weight=True)
        banks.reader[b0] = copy(A, VV[:, 0, :], v0[:, :], t0)
        banks.reader[b1] = copy(V, VV[:, 1, :], v1[:, :], t1)
        t_kv = [A.last(), V.last()]
        V.wait(t1)
        A.wait(t1)
        h = modulated(hT, "norm_mix1", mods(1, 0), mods(1, 1), scratch, t1)
        linear(HEADS, KD, lambda k: hT[:, k, :], lambda k: h[k], lambda n, ps, t: copy(A, QT[:, n, :], ps, t))
        t_q = A.last()
        b, bank, before = banks.take()
        t = mm(bank[0:HEADS, :], col("rel_bias", 0, HEADS)[0:BUCKETS + 1, :], col("onehot", 0, 2 * T)[0:BUCKETS + 1, :],
               True, True, before, signal=True)
        brow = scratch[0:HEADS, 0:2 * T]
        t_brow = banks.reader[b] = copy(V, brow, bank[0:HEADS, :], t, t_q)
        s_bias_w.count = 16
        A.wait(t_brow)
        A.ops.append(("op16", lambda e, i: e.dma_start(bias_scratch, brow), s_bias_w))
        bias_written = Token(s_bias_w, 16, None)
        A.wait(bias_written)

        s_max = arena.take(8)
        pbuf = [arena.take(T) for _ in range(4)]
        ptb = [arena.take(NT * P) for _ in range(2)]
        SC = HD ** -0.5
        pt_free = [None, None]
        p_free = [None] * 4
        n_p = 0
        for m in range(NT):
            nk = (m + 1) * P
            s_bias_r.count += 16
            src = bass.AP(tensor=bias_scratch.tensor, offset=m * P, ap=[[1, P], [2 * T, HEADS], [1, T]])
            if m:
                A.wait(V.last())
            A.ops.append(("op16", lambda e, i, src=src: e.dma_start(HB, src), s_bias_r))
            t_hb = Token(s_bias_r, s_bias_r.count, None)
            for hd in range(HEADS):
                kv = hd // 2
                b, bank, before = banks.take()
                t = mm(bank[:, 0:nk], QT[:, hd, m * P:(m + 1) * P], KT[:, kv, 0:nk], True, True, before, t_q, t_kv, signal=True)
                pb = pbuf[n_p % 4][:, 0:nk]
                rev = HB[:, hd, T - nk:T][:, ::-1]
                t1 = stt(pb, bank[:, 0:nk], SC, rev, ALU.mult, ALU.add, t, t_hb, p_free[n_p % 4])
                banks.reader[b] = t1
                st = s_max[:, (n_p % 2) * 4:(n_p % 2) * 4 + 4]
                t2 = V.do(lambda e, i, st=st, pb=pb: e.tensor_reduce(st[:, 0:1], pb, AX, ALU.max), t1)
                t2 = ts(V, st[:, 1:2], st[:, 0:1], -1.0, None, ALU.mult, None, t2)
                t3 = act(pb, pb, ACT.Exp, t2, bias=st[:, 1:2], accum_out=st[:, 2:3])
                t4 = recip(st[:, 3:4], st[:, 2:3], t3)
                t4 = ts(V, pb, pb, st[:, 3:4], None, ALU.mult, None, t4)
                b, bank, before = banks.take()
                for kt in range(m + 1):
                    t5 = flip(bank[:, kt * P:(kt + 1) * P], pb[:, kt * P:(kt + 1) * P], t4, before)
                p_free[n_p % 4] = t5
                pt = ptb[n_p % 2]
                t6 = banks.reader[b] = copy(A, pt[:, 0:nk], bank[:, 0:nk], t5, pt_free[n_p % 2])
                b, bank, before = banks.take()
                for kt in range(m + 1):
                    t7 = mm(bank[:, 0:P], VV[:, kt, kv * HD:(kv + 1) * HD], pt[:, kt * P:(kt + 1) * P], kt == 0, kt == m,
                            t6, before, signal=True)
                pt_free[n_p % 2] = t7
                t8 = banks.reader[b] = copy(V, OT[:, hd, m * P:(m + 1) * P], bank[:, 0:P], t7)
                n_p += 1
        linear(KD, HEADS, lambda k: OT[:, k, :], lambda k: t8, residual(mods(1, 2)))
        pr.all_join()
        ffn(1)

        def plain_norm(dst, g_name):
            arena.at = 0
            ks = modulated(dst, g_name, None, None, arena.take(KD * T))
            pr.all_join()
            return ks
        plain_norm(xT, "final_norm")
        h = plain_norm(hT, "norm_mix_2")

        arena.at = 0
        yaT = arena.take(KR * T)
        ybT = arena.take(KR * T)
        ycT = arena.take(KR * T)
        keep = arena.at
        arena.at = KR * T
        raw = arena.take(15 * T)
        TW = T + 2
        stage = [arena.take(TW) for _ in range(2)]
        mid = arena.take(15)
        t_z = G.do(lambda e, i: e.memset(stage[0], 0.0))
        t_z = G.do(lambda e, i: e.memset(stage[1], 0.0))
        t = tt(V, mid, col("shift_prev", 0, 15), col("shift_next", 0, 15), ALU.add)
        t_mid = ts(V, mid, mid, -1.0, 1.0, ALU.mult, ALU.add, t)
        st_free = [t_z, t_z]

        def shift_read(n, ps, t):
            st = stage[n % 2]
            t1 = copy(A, st[:, 1:T + 1], ps, t, st_free[n % 2])
            o = raw[:, n * T:(n + 1) * T]
            t2 = ts(V, o, st[:, 1:T + 1], mid[:, n:n + 1], None, ALU.mult, None, t1, t_mid)
            t2 = stt(o, st[:, 0:T], col("shift_prev", n), o, ALU.mult, ALU.add, t2)
            st_free[n % 2] = stt(o, st[:, 2:T + 2], col("shift_next", n), o, ALU.mult, ALU.add, t2)
            return t1
        linear(15, KD, lambda k: hT[:, k, :], lambda k: h[k], shift_read)
        pr.all_join()

        rT, kT_, vT = raw[:, 0:KR * T], raw[:, KR * T:2 * KR * T], raw[:, 2 * KR * T:3 * KR * T]
        wd, ad, gd = [raw[:, (12 + j) * T:(13 + j) * T] for j in range(3)]
        t_wd = act(wd, wd, ACT.Tanh)
        t_gd = sigmoid(gd, gd)
        half0 = arena.take(4 * KR)
        ts(V, half0, col("w0", 0, 4 * KR), 0.5, None, ALU.mult, None)
        omk = arena.take(KR)
        ts(V, omk, col("k_a", 0, KR), -1.0, 1.0, ALU.mult, ALU.add)
        pr.all_join()

        w2s, a2s, g2s = arena.take(P), arena.take(P), arena.take(P)
        vec = arena.take(12)
        vs = arena.take(T)
        kk = arena.take(T)
        kin = arena.take(T)
        QR = [arena.take(2 * NT * P) for _ in range(2)]
        BT = [arena.take(T) for _ in range(2)]
        CT = [arena.take(T) for _ in range(2)]
        Btok, Ctok = arena.take(2 * P), arena.take(2 * P)
        sbd = [arena.take(P) for _ in range(2)]
        psc = [arena.take(1) for _ in range(2)]
        ksum = arena.take(T)
        S4 = 4 * P
        LTb, Bm, Xb, XTb, Tb = [[arena.take(S4) for _ in range(2)] for _ in range(5)]
        MBb, MCb, LCb = LTb, Bm, Tb
        Rb, Ub = [[arena.take(2 * P) for _ in range(2)] for _ in range(2)]
        tmp = [Xb[0][:, 0:T], Xb[0][:, T:2 * T], Xb[1][:, 0:T], Xb[1][:, T:2 * T],
               XTb[0][:, 0:T], XTb[0][:, T:2 * T], XTb[1][:, 0:T], XTb[1][:, T:2 * T]]
        B = banks.banks
        CW, CA, CKK, CKA, COMK, CRK, CLW, CLB = 0, 2, 4, 5, 6, 7, 8, 9

        def tile_of(ap):
            return lambda i: ap[:, bass.ds(i * T, T)]

        pr.all_join()
        with pr.repeat(KR):
            def cst(dst, base, mult=1):
                return copy(V, dst, lambda i: base[:, bass.ds(i * mult, dst.shape[1])])
            at = lambda name: pk[:, COLS[name][0]:COLS[name][0] + COLS[name][1]]
            cst(w2s, at("w2"), P); cst(a2s, at("a2"), P); cst(g2s, at("g2"), P)
            for j in range(2):
                cst(vec[:, CW + j:CW + j + 1], half0[:, j * KR:(j + 1) * KR])
                cst(vec[:, CA + j:CA + j + 1], half0[:, (2 + j) * KR:(3 + j) * KR])
            cst(vec[:, CKK:CKK + 1], at("k_k")); cst(vec[:, CKA:CKA + 1], at("k_a")); cst(vec[:, COMK:COMK + 1], omk)
            cst(vec[:, CRK:CRK + 1], at("r_k")); cst(vec[:, CLW:CLW + 1], at("ln_w"))
            t_vec = cst(vec[:, CLB:CLB + 1], at("ln_b"))
            V.wait(t_vec)
            t_v = copy(V, tmp[7], tile_of(vT))
            for m in range(NT):
                t = flip(B[0][:, m * P:(m + 1) * P], tmp[7][:, m * P:(m + 1) * P], t_v)
            t_vs = copy(A, vs, B[0][:, 0:T], t)
            t = copy(V, kin, tile_of(kT_))
            t_kin = t
            t = ts(V, kk, kin, vec[:, CKK:CKK + 1], None, ALU.mult, None, t)
            t1 = tt(V, tmp[6], kk, kk, ALU.mult, t)
            t1 = mm(B[1][:, 0:T], blk, tmp[6], True, True, t1, signal=True)
            t1 = ts(V, tmp[6], B[1][:, 0:T], 1e-24, None, ALU.max, None, t1)
            t1 = act(tmp[6], tmp[6], ACT.Sqrt, t1)
            t1 = recip(tmp[6], tmp[6], t1)
            t_kk = tt(V, kk, kk, tmp[6], ALU.mult, t1)
            t_ops = []
            for d in range(2):
                lo = 64 * d
                bw, ba = B[2 + 2 * d], B[3 + 2 * d]
                w, a, f, u = [tmp[q] for q in (0, 1, 2, 3)]
                t = mm(bw[:, 0:T], w2s[lo:lo + 64, :], wd[lo:lo + 64, :], True, True, t_vec, signal=True)
                t_a = mm(ba[:, 0:T], a2s[lo:lo + 64, :], ad[lo:lo + 64, :], True, True, signal=True)
                t = sigmoid(w, bw[:, 0:T], t, V.last(), half_bias=vec[:, CW + d:CW + d + 1])
                t_w = act(w, w, ACT.Exp, t, scale=-math.exp(-0.5))
                t_a = sigmoid(a, ba[:, 0:T], t_a, t_w, half_bias=vec[:, CA + d:CA + d + 1])
                t = ts(V, u, a, vec[:, CKA:CKA + 1], vec[:, COMK:COMK + 1], ALU.mult, ALU.add, t_a)
                t_kd = tt(V, u, u, kin, ALU.mult, t, t_kin)
                if d == 0:
                    t_ks = copy(V, ksum, u, t_kd)
                else:
                    t_ks = tt(V, ksum, ksum, u, ALU.add, t_kd, t_ks)
                zero = col("zero").to_broadcast([P, P])
                for m in range(NT):
                    ws, fs = w[:, m * P:(m + 1) * P], f[:, m * P:(m + 1) * P]
                    if d:
                        ws, fs = ws[:, ::-1], fs[:, ::-1]
                    V.do(lambda e, i, ws=ws, fs=fs: e.tensor_tensor_scan(fs, ws, zero, 1.0, ALU.mult, ALU.add), t_w)
                midc = [m * P + (63 if d == 0 else 64) for m in range(NT)]
                inv = tmp[4]
                V.wait(V.last())
                t_inv = recip(inv, f)
                first, second = (0, 1) if d == 0 else (1, 0)
                end = first * P + (P - 1 if d == 0 else 0)
                t = tt(V, psc[d], f[:, end:end + 1], inv[:, midc[first]:midc[first] + 1], ALU.mult, t_inv)
                t_ps = tt(V, psc[d], psc[d], f[:, midc[second]:midc[second] + 1], ALU.mult, t)
                t_iw = recip(tmp[5], w, t_w)
                for m in range(NT):
                    sl = slice(m * P, (m + 1) * P)
                    im, fm = inv[:, midc[m]:midc[m] + 1], f[:, midc[m]:midc[m] + 1]
                    q = QR[d][:, m * 2 * P:m * 2 * P + P]
                    rr = QR[d][:, m * 2 * P + P:(m + 1) * 2 * P]
                    t = stt(rr, f[:, sl], im, lambda i, m=m: rT[:, bass.ds(i * T + m * P, P)], ALU.mult, ALU.mult, t_inv)
                    t = stt(q, f[:, sl], im, kk[:, sl], ALU.mult, ALU.mult, t, t_kk)
                    t = tt(V, q, q, tmp[5][:, sl], ALU.mult, t, t_iw)
                    t1 = stt(BT[d][:, sl], inv[:, sl], fm, kk[:, sl], ALU.mult, ALU.mult, t)
                    t1 = tt(V, BT[d][:, sl], BT[d][:, sl], a[:, sl], ALU.mult, t1)
                    t1 = stt(CT[d][:, sl], inv[:, sl], fm, u[:, sl], ALU.mult, ALU.mult, t1)
                V.wait(t1)
                t_ops.append(t1)
            for j, (src, dst) in enumerate(((BT, Btok), (CT, Ctok))):
                for d in range(2):
                    t = flip(B[6 + j][:, d * P:(d + 1) * P], src[d][:, d * P:(d + 1) * P], t_ops[d])
                t_tok = copy(A, dst, B[6 + j][:, 0:2 * P], t)
            def tile(s, d):
                return s if d == 0 else 1 - s

            def gram(s, lhs, rhs, n, evac):
                toks = []
                for hh in range(2):
                    bb = B[2 * s + hh]
                    for d in range(2):
                        m = tile(s, d)
                        l = lhs(d, m)[64 * hh:64 * hh + 64, :]
                        rr = rhs(d, m)[64 * hh:64 * hh + 64, :]
                        t = mm(bb[:, d * n:(d + 1) * n], l, rr, True, True, V.last(), A.last(), signal=True)
                    toks.append(evac(hh, bb, t))
                return toks

            strict = tiles(col("strict", 0, 2 * P), P)
            incl = tiles(col("incl", 0, 2 * P), P)
            level = tiles(col("level", 0, LEVELS * P), P)
            t_lt, x_t, xt_t = [None] * 2, [None] * 2, [None] * 2
            v4 = lambda ap: ap.rearrange("p (d h n) -> p d h n", d=2, h=2)
            for s in range(2):
                def ev(hh, bb, t, s=s):
                    return tt(V, v4(LTb[s])[:, :, hh, :], tiles(bb[:, 0:2 * P], P), strict, ALU.mult, t)
                t_lt[s] = gram(s, lambda d, m: BT[d][:, m * P:(m + 1) * P], lambda d, m: QR[d][:, m * 2 * P:m * 2 * P + P], P, ev)
            id4 = ident.unsqueeze(1).to_broadcast([P, 4, P])
            for lv in range(LEVELS):
                tb = [None] * 2
                for s in range(2):
                    mk = level[:, lv, :].unsqueeze(1).to_broadcast([P, 4, P])
                    tb[s] = tt(G, tiles(Bm[s], P), tiles(LTb[s], P), mk, ALU.mult, t_lt[s], x_t[s], PE.last())
                if lv == 0:
                    for s in range(2):
                        xt_t[s] = tt(V, tiles(XTb[s], P), id4, tiles(Bm[s], P), ALU.subtract, tb[s])
                        bk = B[4 + s]
                        for q in range(4):
                            t = mm(bk[:, q * P:(q + 1) * P], Bm[s][:, q * P:(q + 1) * P], ident, True, True, tb[s], A.last(), V.last(),
                                   signal=q == 3)
                        x_t[s] = tt(V, tiles(Xb[s], P), id4, tiles(bk[:, :], P), ALU.subtract, t)
                    continue
                for s in range(2):
                    bk = B[s]
                    for q in range(4):
                        sl = slice(q * P, (q + 1) * P)
                        t = mm(bk[:, sl], Bm[s][:, sl], Xb[s][:, sl], True, True, tb[s], x_t[s], xt_t[s], signal=q == 3)
                    t = copy(A, Tb[s], bk[:, :], t, PE.last())
                    bx, bxt = B[2 + 2 * s], B[3 + 2 * s]
                    if lv < LEVELS - 1:
                        for q in range(4):
                            sl = slice(q * P, (q + 1) * P)
                            t1 = mm(bx[:, sl], XTb[s][:, sl], Tb[s][:, sl], True, True, t, signal=q == 3)
                    for q in range(4):
                        sl = slice(q * P, (q + 1) * P)
                        t2 = mm(bxt[:, sl], Tb[s][:, sl], XTb[s][:, sl], True, True, t, signal=q == 3)
                    if lv < LEVELS - 1:
                        x_t[s] = tt(V, Xb[s], Xb[s], bx[:, :], ALU.subtract, t1, t2)
                    xt_t[s] = tt(V, XTb[s], XTb[s], bxt[:, :], ALU.subtract, t2)
            V.wait(*xt_t)
            PE.wait(*xt_t)
            for s in range(2):
                def ev_mb(hh, bb, t, s=s):
                    return tt(V, v4(MBb[s])[:, :, hh, :], tiles(bb[:, 0:2 * P], P), incl, ALU.mult, t, tb[0], tb[1])
                t_mb = gram(s, lambda d, m: BT[d][:, m * P:(m + 1) * P], lambda d, m: QR[d][:, m * 2 * P + P:(m + 1) * 2 * P], P, ev_mb)

                def ev_c(hh, bb, t, s=s):
                    both = bb[:, :].rearrange("p (d c n) -> p d c n", d=2, c=2)
                    t1 = tt(V, v4(LCb[s])[:, :, hh, :], both[:, :, 0, :], strict, ALU.mult, t)
                    return tt(V, v4(MCb[s])[:, :, hh, :], both[:, :, 1, :], incl, ALU.mult, t, t1)
                t_c = gram(s, lambda d, m: CT[d][:, m * P:(m + 1) * P], lambda d, m: QR[d][:, m * 2 * P:(m + 1) * 2 * P], 2 * P, ev_c)
            V.wait(V.last())
            ydst = lambda m: (lambda i: yaT[:, bass.ds(i * T + m * P, P)])
            first_y = [None, None]
            for s in range(2):
                bR, bU = B[s], B[2 + s]
                PE.wait(V.last(), A.last())
                for d in range(2):
                    m = tile(s, d)
                    o = bR[:, d * P:(d + 1) * P]
                    if s:
                        mm(o, QR[d][:, m * 2 * P:m * 2 * P + P], sbd[d], True, False)
                    for hh in range(2):
                        t = mm(o[:, 64 * hh:64 * hh + 64], LCb[s][:, (2 * d + hh) * P:(2 * d + hh + 1) * P],
                               vs[:, m * P + 64 * hh:m * P + 64 * hh + 64], not s, True, t_vs, signal=True)
                t = copy(V, Rb[s], bR[:, 0:2 * P], t)
                for d in range(2):
                    for hh in range(2):
                        t1 = mm(bU[:, d * P + 64 * hh:d * P + 64 * hh + 64], XTb[s][:, (2 * d + hh) * P:(2 * d + hh + 1) * P],
                                Rb[s][:, d * P + 64 * hh:d * P + 64 * hh + 64], True, True, t, signal=True)
                t_u = ts(V, Ub[s], bU[:, 0:2 * P], -1.0, None, ALU.mult, None, t1)
                if s == 0:
                    for d in range(2):
                        m = tile(s, d)
                        o = B[6 + d][:, 0:P]
                        mm(o, Btok[:, d * P:(d + 1) * P], Ub[s][:, d * P:(d + 1) * P], True, False, t_u, t_tok)
                        t = mm(o, Ctok[:, d * P:(d + 1) * P], vs[:, m * P:(m + 1) * P], False, True, signal=True)
                        t_s = stt(sbd[d], o, psc[d], blk, ALU.mult, ALU.mult, t)
                for d in range(2):
                    m = tile(s, d)
                    bY = B[4 + d]
                    o = bY[:, 0:P]
                    if s:
                        mm(o, sbd[d], QR[d][:, m * 2 * P + P:(m + 1) * 2 * P], True, False, t_s, V.last(), A.last())
                    for hh in range(2):
                        oh = bY[64 * hh:64 * hh + 64, 0:P]
                        sl = slice((2 * d + hh) * P, (2 * d + hh + 1) * P)
                        mm(oh, Ub[s][:, d * P + 64 * hh:d * P + 64 * hh + 64], MBb[s][:, sl], not s, False, t_u)
                        t = mm(oh, vs[:, m * P + 64 * hh:m * P + 64 * hh + 64], MCb[s][:, sl], False, True, signal=True)
                    if s == 0:
                        first_y[m] = copy(V, ydst(m), o, t)
                    else:
                        t_yy = tt(V, ydst(m), o, ydst(m), ALU.add, t, first_y[m])
            yv = tile_of(yaT)
            ym, y2, bo = tmp[0], tmp[1], tmp[2]
            V.wait(t_yy); PE.wait(V.last()); A.wait(V.last())
            t = copy(V, ym, yv, PE.last())
            t = mm(B[0][:, 0:T], blk, ym, True, True, t, signal=True)
            t_m = stt(ym, B[0][:, 0:T], -1.0 / 64, ym, ALU.mult, ALU.add, t)
            t = tt(V, y2, ym, ym, ALU.mult, t_m)
            t = mm(B[1][:, 0:T], blk, y2, True, True, t, signal=True)
            t = inv_sqrt(rstd, B[1][:, 0:T], 1.0 / 64, LN_EPS, "ln_eps", T, t)
            t = tt(V, ym, ym, rstd[:, 0:T], ALU.mult, t)
            t_n = ts(V, ym, ym, vec[:, CLW:CLW + 1], vec[:, CLB:CLB + 1], ALU.mult, ALU.add, t)
            t = stt(bo, ksum, vec[:, CRK:CRK + 1], tile_of(rT), ALU.mult, ALU.mult, t_ks)
            t = mm(B[2][:, 0:T], blk, bo, True, True, t, signal=True)
            t = tt(V, bo, B[2][:, 0:T], tile_of(vT), ALU.mult, t)
            t = tt(V, ym, ym, bo, ALU.add, t, t_n)
            t1 = mm(B[3][:, 0:T], g2s, gd, True, True, signal=True)
            tt(V, yv, ym, B[3][:, 0:T], ALU.mult, t, t1)
            pr.all_join()
        pr.all_join()

        arena.at = keep
        PW = 16 + T
        zb = tiles(arena.take(4 * PW), PW)
        s1, s2 = arena.take(PW), arena.take(PW)
        pooled = tiles(arena.take(4 * T), T)
        t_z = G.do(lambda e, i: e.memset(zb[:, :, :], 0.0))
        t_z2 = G.do(lambda e, i: e.memset(s1, 0.0))
        t_z2 = G.do(lambda e, i: e.memset(s2, 0.0))
        linear(4, KD, lambda k: hT[:, k, :], lambda k: h[k], lambda n, ps, t: copy(A, zb[:, n, 8:8 + T], ps, t, t_z))
        t_zb = A.last()
        for g, w in enumerate(WINDOWS):
            cur, width = zb[:, g, :], 1
            t = t_zb
            bufs = [s1, s2]
            while width < w:
                nxt = bufs[0]
                bufs.reverse()
                t = tt(G, nxt[:, 0:PW - width], cur[:, 0:PW - width], cur[:, width:PW], ALU.add, t, t_z2)
                cur, width = nxt, 2 * width
            lo = w // 2
            t = tt(G, pooled[:, g, :], cur[:, 8 - lo:8 - lo + T], col("inv_cnt", g * T, T), ALU.mult, t)
            t = tt(G, pooled[:, g, :], pooled[:, g, :], zb[:, g, 8:8 + T], ALU.subtract, t)
            b, bank, before = banks.take()
            t1 = mm(bank[:, 0:T], col("pool_w", g * P, P), pooled[:, g, :], True, True, t, before, signal=True)
            banks.reader[b] = act(ybT[:, g * T:(g + 1) * T], bank[:, 0:T], ACT.Copy, t1, scale=col("pool_scale", g))
        t_yb = A.last()

        att = tiles(arena.take(6 * T), T)
        asq, rot = arena.take(T), arena.take(T)
        kz = [[arena.take(T) for _ in range(2)] for _ in range(2)]
        vtok = arena.take(NT * P)
        linear(6, KD, lambda k: hT[:, k, :], lambda k: h[k], lambda n, ps, t: copy(A, att[:, n, :], ps, t))
        t_att = A.last()
        t_last = None
        for n in range(5):
            p_ = att[:, n, :]
            t = tt(V, asq, p_, p_, ALU.mult, t_att, t_last, PE.last())
            b, bank, before = banks.take()
            t = mm(bank[:, 0:T], blk, asq, True, True, t, before, signal=True)
            t = banks.reader[b] = inv_sqrt(rstd, bank[:, 0:T], 1.0 / 64, EPS, "eps", T, t)
            t = stt(p_, p_, col("q_norm" if n < 4 else "k_norm"), rstd[:, 0:T], ALU.mult, ALU.mult, t)
            b, bank, before = banks.take()
            t1 = mm(bank[:, 0:T], col("pair", 0, P), p_, True, True, t, before, signal=True)
            t1 = banks.reader[b] = tt(V, rot, bank[:, 0:T], col("sin", 0, T), ALU.mult, t1)
            t = tt(V, p_, p_, col("cos", 0, T), ALU.mult, t, t1)
            t_last = tt(V, p_, p_, rot, ALU.add, t)
        kT = att[:, 4, :]
        b, bank, before = banks.take()
        t = mm(bank[:, 0:T], col("half", 0, P), kT, True, True, t_last, before, signal=True)
        for g in range(2):
            for hh in range(2):
                G.do(lambda e, i, z=kz[g][hh]: e.memset(z, 0.0))
        tz = G.last()
        copy(V, kz[0][0][0:64, :], kT[0:64, :], tz, t_last)
        copy(V, kz[1][1][64:128, :], kT[64:128, :], tz)
        copy(V, kz[0][1][64:128, :], bank[64:128, 0:T], tz, t)
        t_kz = banks.reader[b] = copy(V, kz[1][0][0:64, :], bank[0:64, 0:T], tz, t)
        b, bank, before = banks.take()
        for m in range(NT):
            t = flip(bank[:, m * P:(m + 1) * P], att[:, 5, m * P:(m + 1) * P], t_att, before)
        t_vt = banks.reader[b] = copy(A, vtok, bank[:, 0:T], t)
        pbufs = [arena.take(T) for _ in range(4)]
        stt_ = [arena.take(4) for _ in range(4)]
        ptb = [arena.take(NT * T) for _ in range(2)]
        p_free, pt_free = [None] * 4, [None] * 2
        ASC = 64 ** -0.5
        n_p = 0
        for hd in range(8):
            g, hh, ct = hd // 4, hd % 2, hd // 2
            pt = tiles(ptb[hd % 2], T)
            for m in range(NT):
                b, bank, before = banks.take()
                t = mm(bank[:, 0:T], att[:, ct, m * P:(m + 1) * P], kz[g][hh], True, True, t_kz, before, signal=True)
                pb, st = pbufs[n_p % 4], stt_[n_p % 4]
                t1 = V.do(lambda e, i, st=st, bank=bank: e.tensor_reduce(st[:, 0:1], bank[:, 0:T], AX, ALU.max), t, p_free[n_p % 4])
                t1 = ts(V, st[:, 1:2], st[:, 0:1], -ASC, None, ALU.mult, None, t1)
                t1 = banks.reader[b] = act(pb, bank[:, 0:T], ACT.Exp, t1, p_free[n_p % 4], bias=st[:, 1:2], scale=ASC, accum_out=st[:, 2:3])
                t1 = recip(st[:, 3:4], st[:, 2:3], t1)
                t1 = ts(V, pb, pb, st[:, 3:4], None, ALU.mult, None, t1)
                b, bank, before = banks.take()
                for kt in range(NT):
                    t2 = flip(bank[:, kt * P:(kt + 1) * P], pb[:, kt * P:(kt + 1) * P], t1, before)
                p_free[n_p % 4] = t2
                t3 = banks.reader[b] = copy(A, pt[:, :, m * P:(m + 1) * P], tiles(bank[:, 0:T], P), t2, pt_free[hd % 2])
                n_p += 1
            b, bank, before = banks.take()
            o = bank[64 * hh:64 * hh + 64, 0:T]
            for kt in range(NT):
                t4 = mm(o, vtok[:, kt * P + 64 * g:kt * P + 64 * g + 64], pt[:, kt, :], kt == 0, kt == NT - 1, t3, t_vt, before, signal=True)
            pt_free[hd % 2] = t4
            t_yc = banks.reader[b] = copy(V, ycT[64 * hh:64 * hh + 64, ct * T:(ct + 1) * T], o, t4)
        pr.all_join()

        arena.at = keep
        mg = tiles(arena.take(KD * T), T)
        gt = [arena.take(T) for _ in range(2)]
        g_free = [None, None]
        m_done = []
        n_g = 0
        for n in range(KD):
            tm = None
            for bi, src in enumerate((yaT, ybT, ycT)):
                st = gt[n_g % 2]

                def gate_r(_, ps, t, st=st):
                    sigmoid(st, ps, t, g_free[n_g % 2])
                    return A.last()
                linear(1, KD, lambda k: hT[:, k, :], lambda k: h[k], gate_r)
                t_g = V.last()

                def br_r(_, ps, t):
                    if bi == 0:
                        t1 = tt(V, mg[:, n, :], ps, st, ALU.mult, t, t_g)
                        g_free[n_g % 2] = t1
                        return t1
                    t1 = tt(V, st, ps, st, ALU.mult, t, t_g)
                    g_free[n_g % 2] = tt(V, mg[:, n, :], mg[:, n, :], st, ALU.add, t1, tm)
                    return t1
                linear(1, KR, lambda k: src[:, k * T:(k + 1) * T], lambda k: None, br_r)
                tm = g_free[n_g % 2]
                n_g += 1
            m_done.append(tm)
        linear(KD, KD, lambda k: mg[:, k, :], lambda k: m_done[k], residual(None))
        pr.all_join()

        h = plain_norm(hT, "norm_ffn_2")
        arena.at = 0
        htok = tiles(arena.take(NT * D), D)
        sel = arena.take(NT * EXPERTS * CAP)
        comb = arena.take(4 * T)
        yall = arena.take(KD * EXPERTS * CAP)
        work = arena.at
        aff = arena.take(NT * EXPERTS)
        st = arena.take(4 * NT)
        affT = arena.take(T)[0:EXPERTS, :]
        wk = arena.take(T)[0:EXPERTS, :]
        mk = arena.take(T)[0:EXPERTS, :]
        ps_ = arena.take(T)[0:EXPERTS, :]
        m8 = arena.take(8)[0:EXPERTS, :]
        post = arena.take(NT * EXPERTS)
        for m in range(NT):
            for q in range(2):
                b, bank, before = banks.take()
                for c in range(4):
                    t = flip(bank[:, c * P:(c + 1) * P], hT[:, 4 * q + c, m * P:(m + 1) * P], before, h[-1])
                banks.reader[b] = copy(A, htok[:, m, q * 512:(q + 1) * 512], bank[:, :], t)
        t_ht = A.last()
        for m in range(NT):
            b, bank, before = banks.take()
            for k in range(KD):
                t = mm(bank[:, 0:EXPERTS], hT[:, k, m * P:(m + 1) * P], col("router", k * EXPERTS, EXPERTS), k == 0, k == KD - 1,
                       before, signal=k == KD - 1)
            s_, af = st[:, 4 * m:4 * m + 4], aff[:, m * EXPERTS:(m + 1) * EXPERTS]
            t1 = V.do(lambda e, i, s_=s_, bank=bank: e.tensor_reduce(s_[:, 0:1], bank[:, 0:EXPERTS], AX, ALU.max), t)
            t1 = ts(V, s_[:, 1:2], s_[:, 0:1], -1.0, None, ALU.mult, None, t1)
            t1 = banks.reader[b] = act(af, bank[:, 0:EXPERTS], ACT.Exp, t1, bias=s_[:, 1:2], accum_out=s_[:, 2:3])
            t1 = recip(s_[:, 3:4], s_[:, 2:3], t1)
            t_af = ts(V, af, af, s_[:, 3:4], None, ALU.mult, None, t1)
        b, bank, before = banks.take()
        for m in range(NT):
            t = flip(bank[0:EXPERTS, m * P:(m + 1) * P], aff[:, m * EXPERTS:(m + 1) * EXPERTS], t_af, before)
        t = banks.reader[b] = copy(V, affT, bank[0:EXPERTS, 0:T], t)
        t = copy(V, wk, affT, t)
        for _ in range(CAP // 8):
            t = V.do(lambda e, i: e.max(m8, wk), t)
            t = V.do(lambda e, i: e.match_replace(out=wk, in_to_replace=m8, in_values=wk, imm_value=-1.0), t)
        t_mk = ts(V, mk, wk, 0.0, None, ALU.is_lt, None, t)
        t = V.do(lambda e, i: e.tensor_tensor_scan(ps_, mk, col("zero")[0:EXPERTS, :].to_broadcast([EXPERTS, T]), 0.0, ALU.add, ALU.add), t_mk)
        t = tt(V, ps_, ps_, mk, ALU.mult, t)
        t = ts(V, ps_, ps_, -1.0, None, ALU.add, None, t)
        b, bank, before = banks.take()
        for m in range(NT):
            t1 = flip(bank[:, m * EXPERTS:(m + 1) * EXPERTS], ps_[:, m * P:(m + 1) * P], t, before)
        t = banks.reader[b] = copy(V, post, bank[:, 0:NT * EXPERTS], t1)
        iota = col("iota", 0, CAP).unsqueeze(1).to_broadcast([P, EXPERTS, CAP])
        selv = sel.rearrange("p (m e c) -> p m e c", m=NT, e=EXPERTS)
        gsel = yall[:, 0:EXPERTS * CAP * NT]
        gselv = gsel.rearrange("p (m e c) -> p m e c", m=NT, e=EXPERTS)
        for m in range(NT):
            pv = post[:, m * EXPERTS:(m + 1) * EXPERTS].unsqueeze(2).to_broadcast([P, EXPERTS, CAP])
            av = aff[:, m * EXPERTS:(m + 1) * EXPERTS].unsqueeze(2).to_broadcast([P, EXPERTS, CAP])
            t1 = tt(V, selv[:, m], pv, iota, ALU.is_equal, t)
            t2 = tt(V, gselv[:, m], selv[:, m], av, ALU.mult, t1)
        for q in range(4):
            b, bank, before = banks.take()
            for m in range(NT):
                t = flip(bank[:, m * P:(m + 1) * P], gsel[:, m * EXPERTS * CAP + q * P:m * EXPERTS * CAP + (q + 1) * P], t2, before)
            banks.reader[b] = copy(A, comb[:, q * T:(q + 1) * T], bank[:, 0:T], t)
        pr.all_join()

        arena.at = work
        xg = tiles(arena.take(KD * CAP), CAP)
        hid = arena.take(KD * CAP)
        sg = arena.take(KD * CAP)
        yv = tiles(yall, EXPERTS * CAP)
        H2 = KD * CAP // 2
        with pr.repeat(EXPERTS):
            r_x, r_g, r_u, r_y, r_hid = Later(), Later(), Later(), Later(), Later()
            bx, bg, bu, by = B[0], [B[1], B[2]], [B[3], B[4]], [B[5], B[6]]
            for k in range(KD):
                for m in range(NT):
                    t = mm(bx[:, k * CAP:(k + 1) * CAP], htok[:, m, k * P:(k + 1) * P],
                           lambda i, m=m: sel[:, bass.ds(i * CAP + m * EXPERTS * CAP, CAP)], m == 0, m == NT - 1, r_x,
                           signal=(k, m) == (KD - 1, NT - 1))
            t_x = r_x.tok = copy(V, xg, tiles(bx[:, 0:KD * CAP], CAP), t)
            for half in range(2):
                for f in range(4):
                    for bank, before in ((bg[half], r_g if half == 0 else None), (bu[half], None)):
                        for k in range(KD):
                            w = feed.tile()
                            t = mm(bank[:, f * CAP:(f + 1) * CAP], w, xg[:, k, :], k == 0, k == KD - 1,
                                   t_x, before if f == 0 and k == 0 else None, signal=(k == KD - 1), weight=True)
                hs, ss = hid[:, half * H2:(half + 1) * H2], sg[:, half * H2:(half + 1) * H2]
                t1 = act(ss, bg[half][:, 0:H2], ACT.Tanh, t, scale=0.5)
                t1 = stt(ss, ss, 1.0, bg[half][:, 0:H2], ALU.add, ALU.mult, t1)
                t_h = stt(hs, ss, 0.5, bu[half][:, 0:H2], ALU.mult, ALU.mult, t1)
            r_g.tok = t_h
            for half in range(2):
                for dd in range(4):
                    for k in range(KD):
                        w = feed.tile()
                        t = mm(by[half][:, dd * CAP:(dd + 1) * CAP], w, hid[:, k * CAP:(k + 1) * CAP], k == 0, k == KD - 1,
                               t_h, r_y if (dd, k) == (0, 0) else None, signal=k == KD - 1, weight=True)
                t_y = copy(A, lambda i, half=half: yv[:, 4 * half:4 * half + 4, bass.ds(i * CAP, CAP)],
                           tiles(by[half][:, 0:4 * CAP], CAP), t)
            r_y.tok = t_y
        pr.all_join()
        arena.at = work
        yt = [arena.take(4 * P) for _ in range(2)]
        free = [None, None]
        for c in range(KD):
            b, bank, before = banks.take()
            for q in range(4):
                t = flip(bank[:, q * P:(q + 1) * P], yv[:, c, q * P:(q + 1) * P], before)
            t = banks.reader[b] = copy(A, yt[c % 2], bank[:, :], t, free[c % 2])
            b, bank, before = banks.take()
            for q in range(4):
                t1 = mm(bank[:, 0:T], yt[c % 2][:, q * P:(q + 1) * P], comb[:, q * T:(q + 1) * T], q == 0, q == 3, t, before, signal=True)
            free[c % 2] = t1
            banks.reader[b] = tt(V, xT[:, c, :], bank[:, 0:T], xT[:, c, :], ALU.add, t1)
        pr.all_join()
        plain_norm(hT, "norm_final")
        arena.at = 0
        res = tiles(arena.take(NT * D), D)
        for m in range(NT):
            for q in range(2):
                b, bank, before = banks.take()
                for c in range(4):
                    t = flip(bank[:, c * P:(c + 1) * P], hT[:, 4 * q + c, m * P:(m + 1) * P], before)
                banks.reader[b] = copy(V, res[:, m, q * 512:(q + 1) * 512], bank[:, :], t)
        t_res = V.last()

        assert feed.tiles == NTILES, (feed.tiles, NTILES)
        block = ctx.enter_context(nc.Block())

        @block.sync
        def _(sp):
            sp.dma_start(pk[:, :], packed).then_inc(s_in.sem, 16)
            sp.dma_start(xin, x_in.rearrange("(m p) d -> p m d", p=P)).then_inc(s_x.sem, 16)

            def fill(c, s):
                sp.dma_start(ring[:, s * TPC * P:(s + 1) * TPC * P], weights[c]).then_inc(feed.filled[s].sem, 16)
            for s in range(SLOTS):
                fill(s, s)
            full = NCHUNKS // SLOTS
            with sp.Fori(1, full) as i:
                for s in range(SLOTS):
                    sp.wait_ge(feed.freed.sem, i * SLOTS + (s + 1 - SLOTS))
                    fill(i * SLOTS + s, s)
            for c in range(full * SLOTS, NCHUNKS):
                sp.wait_ge(feed.freed.sem, c - SLOTS + 1)
                fill(c, c % SLOTS)
            sp.wait_ge(t_res.counter.sem, t_res.value)
            sp.dma_start(out.rearrange("o (m p) d -> p (o m) d", p=P), res).then_inc(s_out.sem, 16)
            sp.wait_ge(s_out.sem, 16)

        @block.tensor
        def _(e):
            PE.emit(e)

        @block.vector
        def _(e):
            V.emit(e)

        @block.scalar
        def _(e):
            A.emit(e)

        @block.gpsimd
        def _(e):
            G.emit(e)



def bucket_of(dist):
    dist = np.maximum(dist, 0)
    d = np.maximum(dist, 1).astype(np.float32)
    half = BUCKETS // 2
    large = half + (np.log(d / np.float32(half)) / np.float32(math.log(MAX_DIST / half)) * np.float32(BUCKETS - half)).astype(np.int32)
    return np.where(dist < half, dist, np.minimum(large, BUCKETS - 1))


def constants():
    c = {}
    p = np.arange(P)
    eye = np.eye(P, dtype=np.float32)
    c["ident"], c["ones"] = eye, np.ones((P, P), np.float32)
    c["blk"] = (p[:, None] // 64 == p[None, :] // 64).astype(np.float32)
    c["pair"] = eye[p ^ 1]
    c["half"] = eye[p ^ 64]
    c["eps"], c["ln_eps"] = np.full((P, 1), EPS, np.float32), np.full((P, 1), LN_EPS, np.float32)
    c["zero"], c["one"] = np.zeros((P, 1), np.float32), np.ones((P, 1), np.float32)
    c["iota"] = np.tile(np.arange(CAP, dtype=np.float32), (P, 1))
    s, t = p[:, None], p[None, :]
    c["strict"] = np.concatenate([s < t, s > t], 1).astype(np.float32)
    c["incl"] = np.concatenate([s <= t, s >= t], 1).astype(np.float32)
    c["level"] = np.concatenate([((s >> (l + 1)) == (t >> (l + 1))) & ((s >> l) != (t >> l)) for l in range(LEVELS)], 1).astype(np.float32)
    tok = np.arange(T)
    freqs = (10000.0 ** (-np.arange(0, 32, 2, dtype=np.float32) / 32)).astype(np.float32)
    ang = np.concatenate([(tok // 64)[:, None] * freqs, (tok % 64)[:, None] * freqs], 1).astype(np.float32)
    j = (p % 64) // 2
    c["cos"] = np.cos(ang)[:, j].T.astype(np.float32)
    c["sin"] = (np.sin(ang)[:, j].T * np.where(p % 2 == 0, -1.0, 1.0)[:, None]).astype(np.float32)
    rows = []
    for w in WINDOWS:
        lo, hi = w // 2, w - w // 2 - 1
        rows.append(1.0 / (np.clip(tok + hi + 1, 0, T) - np.clip(tok - lo, 0, T)))
    c["inv_cnt"] = np.tile(np.concatenate(rows).astype(np.float32), (P, 1))
    dist = np.arange(2 * T) - (T - 1)
    oh = np.zeros((P, 2 * T), np.float32)
    b = bucket_of(dist)
    oh[b[dist >= 0], np.where(dist >= 0)[0]] = 1.0
    oh[BUCKETS, dist < 0] = 1.0
    c["onehot"] = oh
    return c


def pack_columns(x):
    pk = np.zeros((P, NCOLS), np.float32)

    def put(name, a, at=0):
        s = COLS[name][0] + at
        pk[:a.shape[0], s:s + a.shape[1]] = a

    def vec(name, v, at=0):
        put(name, np.asarray(v).reshape(-1, P).T, at)
    vec("c", x["c"])
    vec("mod_b", x["mod_b"][0]); vec("mod_b", x["mod_b"][1], 48); vec("mod_b", x["kv_mod_b"], 96)
    for l in range(2):
        vec(f"norm_mix{l}", x["norm_mix"][l]); vec(f"norm_ffn{l}", x["norm_ffn"][l])
    vec("kv_norm", x["kv_norm"]); vec("final_norm", x["final_norm"])
    vec("conv_w", x["lru_conv_w"]); vec("conv_b", x["lru_conv_b"]); vec("b_gates", x["lru_b_gates"])
    vec("lambda", x["lru_lambda"]); vec("norm_mix_2", x["norm_mix_2"])
    vec("shift_prev", x["shift_prev_2"]); vec("shift_next", x["shift_next_2"])
    vec("w0", x["rwkv_w0_2"]); vec("a0", x["rwkv_a0_2"])
    for n, m in (("k_k", "k_k"), ("k_a", "k_a"), ("r_k", "r_k"), ("ln_w", "ln_w"), ("ln_b", "ln_b")):
        vec(n, x[f"rwkv_{m}_2"])
    vec("pool_scale", x["pool_scale_2"])
    for n in ("q_norm", "k_norm"):
        put(n, np.tile(x[f"{n}_2"].reshape(-1, 1), (2, 1)))
    vec("norm_ffn_2", x["norm_ffn_2"]); vec("norm_final", x["norm_final_2"])
    put("rel_bias", x["rel_bias"].T)
    pk[BUCKETS, COLS["rel_bias"][0]:COLS["rel_bias"][0] + HEADS] = NEG
    put("w2", x["rwkv_w2_2"].reshape(P, RW)); put("a2", x["rwkv_a2_2"].reshape(P, RW)); put("g2", x["rwkv_g2_2"][0])
    put("pool_w", x["pool_w_2"][0].transpose(1, 0, 2).reshape(P, 4 * P))
    put("router", x["router_2"][0].reshape(KD, P, EXPERTS).transpose(1, 0, 2).reshape(P, -1))
    for n, a in constants().items():
        put(n, a)
    return pk


def pack_weights(x):
    out = np.empty((NTILES, P, P), np.float32)
    at = 0

    def grid(w):
        k, n = w.shape
        return w.reshape(k // P, P, n // P, P).transpose(0, 2, 1, 3)

    def put(a):
        nonlocal at
        a = a.reshape(-1, P, P) if a.ndim > 3 else a
        out[at:at + len(a)] = a
        at += len(a)

    def by_n(w):
        put(grid(w).transpose(1, 0, 2, 3))

    by_n(x["mod_w"][0]); by_n(x["mod_w"][1]); by_n(x["kv_mod_w"])
    by_n(x["lru_w_in"][0])
    for h in range(LRU_HEADS):
        by_n(x["lru_w_gates"][0, h])
    by_n(x["lru_w_out"][0])

    def ffn(l):
        both = np.stack([grid(x["ffn_w_gate"][l]), grid(x["ffn_w_up"][l])])
        put(both.transpose(2, 0, 1, 3, 4))
        by_n(x["ffn_w_down"][l])
    ffn(0)
    kv = x["w_kv"]
    by_n(kv[:, :512])
    put(grid(kv[:, 512:]))
    by_n(x["attn_w_q"][0]); by_n(x["attn_w_o"][0])
    ffn(1)
    w = x["w_in_2"][0]
    by_n(w[:, :RWKV_COLS + POOL_W + ATT_COLS])
    gates = grid(w[:, RWKV_COLS + POOL_W + ATT_COLS:])
    br = [grid(x[f"w_branch_{n}_2"][0]) for n in ("rwkv", "pool", "attn")]
    for n in range(KD):
        for b in range(3):
            put(gates[:, b * KD + n])
            put(br[b][:, n])
    by_n(x["w_out_2"][0])
    for e in range(EXPERTS):
        both = np.stack([grid(x["exp_gate_2"][0, e]), grid(x["exp_up_2"][0, e])])
        put(both.transpose(2, 0, 1, 3, 4))
        by_n(x["exp_down_2"][0, e])
    assert at == NTILES
    return np.ascontiguousarray(out.reshape(NCHUNKS, TPC, P, P).transpose(0, 2, 1, 3)).reshape(NCHUNKS, P, TPC * P)


def kernel(**inputs):
    import concourse.bacc as bacc
    from concourse.bass_utils import run_bass_kernel_spmd

    x = {k: np.asarray(v) for k, v in inputs.items()}
    arrays = {"weights": pack_weights(x), "packed": pack_columns(x), "x": np.ascontiguousarray(x["x"][0])}
    nc = bacc.Bacc("TRN2", target_bir_lowering=False, num_devices=1)
    aps = {n: nc.dram_tensor(n, a.shape, F32, kind="ExternalInput").ap() for n, a in arrays.items()}
    scratch = nc.dram_tensor("bias_by_distance", (HEADS, 2 * T), F32, kind="Internal").ap()
    out = nc.dram_tensor("out", (1, T, D), F32, kind="ExternalOutput").ap()
    build(nc, aps["weights"], aps["packed"], aps["x"], scratch, out)
    return run_bass_kernel_spmd(nc, [arrays], core_ids=[0]).results[0]["out"]
```

```python
import contextlib
import math

import numpy as np
import concourse.bass as bass
from concourse import mybir

F32 = mybir.dt.float32
ALU = mybir.AluOpType
ACT = mybir.ActivationFunctionType
AX = mybir.AxisListType.X

P = 128
T = 256
NT = T // P
D = 1024
KD = D // P
LRU = 1280
KL = LRU // P
LRU_HEADS = 5
FF = 2816
KF = FF // P
HEADS, KV_HEADS, HD = 8, 4, 128
BUCKETS, MAX_DIST = 32, 128
NEG = -1e30
RW = 512
KR = RW // P
RWKV_COLS, POOL_W, ATT_COLS, GATE_COLS = 1920, 512, 768, 3072
WINDOWS = (2, 4, 8, 16)
EXPERTS, EFF, CAP = 16, 1024, 32
EPS = 1e-6
LN_EPS = 64e-5

SLOTS = 6
TPC = 16
FIRST, LAST = 4, 3
LEVELS = 7



def columns():
    sizes = [
        ("c", KD), ("mod_b", 112), ("norm_mix0", KD), ("norm_mix1", KD), ("norm_ffn0", KD), ("norm_ffn1", KD),
        ("kv_norm", KD), ("final_norm", KD), ("conv_w", 4 * KL), ("conv_b", KL), ("b_gates", 2 * KL),
        ("lambda", KL), ("norm_mix_2", KD), ("shift_prev", 15), ("shift_next", 15), ("w0", 2 * KR),
        ("a0", 2 * KR), ("k_k", KR), ("k_a", KR), ("r_k", KR), ("ln_w", KR), ("ln_b", KR), ("pool_scale", KR),
        ("q_norm", 1), ("k_norm", 1), ("norm_ffn_2", KD), ("norm_final", KD), ("rel_bias", HEADS),
        ("w2", RW), ("a2", RW), ("g2", RW), ("pool_w", 4 * P), ("router", KD * EXPERTS),
        ("eps", 1), ("ln_eps", 1), ("zero", 1), ("one", 1), ("iota", CAP),
        ("ident", P), ("ones", P), ("blk", P), ("pair", P), ("half", P),
        ("cos", T), ("sin", T), ("inv_cnt", 4 * T), ("onehot", 2 * T),
        ("strict", 2 * P), ("incl", 2 * P), ("level", LEVELS * P),
    ]
    at, out = 0, {}
    for name, n in sizes:
        out[name] = (at, n)
        at += n
    return out, at


COLS, NCOLS = columns()
SEGMENTS = [
    ("mods_0", 16 * KD), ("lru_in_mods_1_2", (20 + 32) * KD), ("lru_gates", LRU_HEADS * 8), ("lru_out", KD * KL),
    ("ffn0_gu_mods_3_6", (2 * KF + 64) * KD), ("ffn0_down", KD * KF), ("k", KV_HEADS * KD), ("v", KV_HEADS * KD),
    ("q", HEADS * KD), ("o", KD * HEADS), ("ffn1_gu", 2 * KF * KD), ("ffn1_down", KD * KF),
    ("in2_main", 25 * KD), ("gates", 24 * KD), ("branches", 24 * KR), ("out2", KD * KD), ("experts", EXPERTS * 3 * KD * KD),
]


def mod_steps(n, n_all, blocks):
    return blocks * KD * (n + 1) // n_all - blocks * KD * n // n_all


NTILES = sum(n for _, n in SEGMENTS)
NCHUNKS = NTILES // TPC
assert NTILES % TPC == 0



class Counter:
    def __init__(self, sem):
        self.sem, self.count = sem, 0


class Loop:
    def __init__(self, n):
        self.n, self.entry, self.per = n, {}, {}


class Token:

    def __init__(self, counter, value, loop):
        self.counter, self.value, self.loop = counter, value, loop


class Later:

    def __init__(self):
        self.tok = None


class Engine:

    def __init__(self, prog, name, counter):
        self.prog, self.name, self.c = prog, name, counter
        self.ops, self.seen = [], {}

    def wait(self, *toks):
        for t in toks:
            if t is None:
                continue
            if isinstance(t, (list, tuple)):
                self.wait(*t)
                continue
            if isinstance(t, Later):
                self.ops.append(("wait", t, self.prog.loop))
                continue
            key = (id(t.counter), id(t.loop))
            if self.seen.get(key, -1) < t.value:
                self.seen[key] = t.value
                self.ops.append(("wait", t, self.prog.loop))

    def do(self, fn, *toks, counter=None):
        self.wait(*toks)
        c = counter or self.c
        c.count += 1
        self.ops.append(("op", fn, c))
        return Token(c, c.count, self.prog.loop)

    def run(self, fn, *toks):
        self.wait(*toks)
        self.ops.append(("op", fn, None))

    def last(self):
        return Token(self.c, self.c.count, self.prog.loop) if self.c.count else None

    def emit(self, e, ops=None, i=None):
        for op in self.ops if ops is None else ops:
            if op[0] == "wait":
                _, t, here = op
                late = isinstance(t, Later)
                t = t.tok if late else t
                v = t.value
                if t.loop is not None:
                    per = t.loop.per[t.counter]
                    if t.loop is here:
                        v = (v - per if late else v) + i * per
                    else:
                        v = v + (t.loop.n - 1) * per
                e.wait_ge(t.counter.sem, v)
            elif op[0] == "op16":
                op[1](e, i).then_inc(op[2].sem, 16)
            elif op[0] == "op":
                ins = op[1](e, i)
                if op[2] is not None:
                    ins.then_inc(op[2].sem, 1)
            else:
                with e.Fori(0, op[1]) as j:
                    self.emit(e, op[2], j)


class Program:
    def __init__(self, nc, ctx):
        self.nc, self.ctx, self.loop = nc, ctx, None
        self.counters = []
        self.pe, self.dve, self.act, self.pool = [
            Engine(self, n, self.counter(n)) for n in ("pe_done", "dve_done", "act_done", "pool_done")]
        self.engines = [self.pe, self.dve, self.act, self.pool]

    def counter(self, name):
        c = Counter(self.ctx.enter_context(self.nc.semaphore(name)))
        self.counters.append(c)
        return c

    def all_join(self):
        last = [e.last() for e in self.engines]
        for e in self.engines:
            e.wait(*last)

    @contextlib.contextmanager
    def repeat(self, n):
        loop = Loop(n)
        loop.entry = {c: c.count for c in self.counters}
        outer = [(e.ops, e.seen) for e in self.engines]
        for e in self.engines:
            e.ops, e.seen = [], {}
        self.loop = loop
        first_tile = self.feed.tiles
        yield loop
        self.loop = None
        taken = self.feed.tiles - first_tile
        assert taken % (SLOTS * TPC) == 0, "a chunk's slot is the same in every iteration"
        self.feed.tiles = first_tile + n * taken
        for c in self.counters:
            loop.per[c] = c.count - loop.entry[c]
            c.count = loop.entry[c] + n * loop.per[c]
        for e, (ops, seen) in zip(self.engines, outer):
            body = e.ops
            e.ops, e.seen = ops, seen
            if body:
                e.ops.append(("loop", n, body))


class Banks:

    def __init__(self, banks):
        self.banks, self.reader, self.at, self.held = banks, [None] * len(banks), 0, set()

    def take(self, hold=False):
        while self.at in self.held:
            self.at = (self.at + 1) % len(self.banks)
        b = self.at
        self.at = (b + 1) % len(self.banks)
        if hold:
            self.held.add(b)
        return b, self.banks[b], self.reader[b]

    def release(self, b, reader):
        self.held.discard(b)
        self.reader[b] = reader


class Feed:

    def __init__(self, prog, ring):
        self.prog, self.ring = prog, ring
        self.filled = [prog.counter(f"filled{s}") for s in range(SLOTS)]
        self.freed = prog.counter("freed")
        self.tiles = 0

    def tile(self, n=1):
        k = self.tiles % TPC
        assert k + n <= TPC
        s = self.tiles // TPC % SLOTS
        if k == 0:
            c = self.filled[s]
            c.count += 16
            self.prog.pe.wait(Token(c, c.count, self.prog.loop))
        self.tiles += n
        return self.ring[:, (s * TPC + k) * P:(s * TPC + k + n) * P]

    def ends_chunk(self):
        return self.tiles % TPC == 0


class Arena:
    def __init__(self, t, n):
        self.t, self.n, self.at, self.high = t, n, 0, 0

    def take(self, n):
        a = self.t[:, self.at:self.at + n]
        self.at += n
        self.high = max(self.high, self.at)
        assert self.at <= self.n, (self.at, self.n)
        return a


def tiles(ap, n):
    return ap.rearrange("p (a b) -> p a b", b=n)


def build(nc, weights, packed, x_in, bias_scratch, out):
    with contextlib.ExitStack() as ctx:
        pr = Program(nc, ctx)
        PE, V, A, G = pr.pe, pr.dve, pr.act, pr.pool

        def sbuf(name, n):
            return ctx.enter_context(nc.sbuf_tensor(name, [P, n], F32))

        ring = sbuf("weight_ring", SLOTS * TPC * P)
        pk = sbuf("packed_consts", NCOLS)
        xT_ = sbuf("residual_T", KD * T)
        hT_ = sbuf("normed_T", KD * T)
        mod = sbuf("modulation", 112)
        gain = sbuf("norm_gain", KD)
        silu_c = sbuf("silu_c", KD)
        silu32 = sbuf("silu_c_copies", 32 * KD)
        mod_rows = sbuf("modulation_rows", 512)
        rstd = sbuf("rstd", 3 * T)
        NAR = (nc.sbuf_bytes_remaining // 4 - 64) if not callable(nc.sbuf_bytes_remaining) else nc.sbuf_bytes_remaining() // 4 - 64
        arena = Arena(sbuf("arena", NAR), NAR)
        banks = Banks([ctx.enter_context(nc.psum_tensor(f"bank{b}", [P, 512], F32)) for b in range(8)])
        feed = pr.feed = Feed(pr, ring)
        s_in, s_x, s_bias_w, s_out = [pr.counter(n) for n in ("in", "x_in", "bias_w", "out")]
        s_bias_r = [pr.counter(f"bias_r{m}") for m in range(NT)]
        packed_in = Token(s_in, 16, None)
        x_loaded = Token(s_x, 16, None)

        xT, hT = tiles(xT_[:, :], T), tiles(hT_[:, :], T)

        def col(name, j=0, n=1):
            a = COLS[name][0] + j
            return pk[:, a:a + n]

        ident, ones, blk = col("ident", 0, P), col("ones", 0, P), col("blk", 0, P)

        for e in pr.engines:
            e.wait(packed_in)

        def mm(out, lhsT, rhs, start, stop, *toks, signal=False, weight=False):
            fn = lambda e, i: e.matmul(out(i) if callable(out) else out, lhsT, rhs(i) if callable(rhs) else rhs,
                                       start=start, stop=stop, skip_group_check=True)
            if weight and feed.ends_chunk():
                return PE.do(fn, *toks, counter=feed.freed)
            if signal:
                return PE.do(fn, *toks)
            PE.run(fn, *toks)

        def flip(out, in_, *toks, signal=True):
            n = in_.shape[0]
            fn = lambda e, i: e.transpose(out, in_, ident[0:n, 0:n])
            if signal:
                return PE.do(fn, *toks)
            PE.run(fn, *toks)

        def r(x, i):
            return x(i) if callable(x) else x

        def tt(eng, out, a, b, op, *toks):
            return eng.do(lambda e, i: e.tensor_tensor(r(out, i), r(a, i), r(b, i), op), *toks)

        def ts(eng, out, a, s1, s2, op0, op1, *toks):
            return eng.do(lambda e, i: e.tensor_scalar(r(out, i), r(a, i), r(s1, i), r(s2, i), op0, op1)
                          if s2 is not None else e.tensor_scalar(r(out, i), r(a, i), r(s1, i), None, op0), *toks)

        def stt(out, a, s, b, op0, op1, *toks):
            return V.do(lambda e, i: e.scalar_tensor_tensor(out=r(out, i), in0=r(a, i), scalar=r(s, i), in1=r(b, i),
                                                           op0=op0, op1=op1), *toks)

        def act(out, in_, f, *toks, **kw):
            return A.do(lambda e, i: e.activation(r(out, i), r(in_, i), f, **{k: r(v, i) for k, v in kw.items()}), *toks)

        def copy(eng, out, in_, *toks):
            if eng is A:
                return act(out, in_, ACT.Copy, *toks)
            if callable(out) or callable(in_):
                return eng.do(lambda e, i: e.tensor_scalar(r(out, i), r(in_, i), 1.0, None, ALU.mult), *toks)
            return eng.do(lambda e, i: e.tensor_copy(out, in_), *toks)

        def recip(out, in_, *toks):
            return V.do(lambda e, i: e.reciprocal(r(out, i), r(in_, i)), *toks)

        def sigmoid(out, in_, *toks, half_bias=None):
            kw = {"scale": 0.5}
            if half_bias is not None:
                kw["bias"] = half_bias
            t = act(out, in_, ACT.Tanh, *toks, **kw)
            return ts(V, out, out, 0.5, 0.5, ALU.mult, ALU.add, t)

        def linear(n_tiles, kt, rhs, ready, read):
            for n in range(n_tiles):
                b, bank, before = banks.take()
                for k in range(kt):
                    w = feed.tile()
                    t = mm(bank[:, 0:T], w, rhs(k), k == 0, k == kt - 1, before if k == 0 else None, ready(k),
                           signal=k == kt - 1, weight=True)
                banks.reader[b] = read(n, bank[:, 0:T], t)
            return t

        def linear_steps(n_tiles, kt, rhs, ready, read, b):
            for n in range(n_tiles):
                for k in range(kt):
                    t = mm(banks.banks[b][:, 0:T], feed.tile(), rhs(k), k == 0, k == kt - 1, banks.reader[b] if k == 0 else None,
                           ready(k), signal=k == kt - 1, weight=True)
                    if k == kt - 1:
                        banks.reader[b] = read(n, banks.banks[b][:, 0:T], t)
                    yield

        def squares(*toks):
            b, bank, before = banks.take(hold=True)
            for k in range(KD):
                q = act(hT[:, k, :], xT[:, k, :], ACT.Square, *toks) if k % 2 else \
                    tt(V, hT[:, k, :], xT[:, k, :], xT[:, k, :], ALU.mult, *toks)
                t = mm(bank[:, 0:T], ones, hT[:, k, :], k == 0, k == KD - 1, before, q, signal=k == KD - 1)
            return b, t

        def inv_sqrt(buf, src, scale, eps, eps_col, n, *toks):
            y, z, w = buf[:, 0:n], buf[:, n:2 * n], buf[:, 2 * n:3 * n]
            t0 = ts(V, z, src, scale, eps, ALU.mult, ALU.add, *toks)
            t = act(y, z, ACT.Ln, t0)
            t = act(y, y, ACT.Exp, t, scale=-0.5)
            t = tt(V, w, y, y, ALU.mult, t)
            t = tt(V, w, w, z, ALU.mult, t)
            t = ts(V, w, w, -0.5, 1.5, ALU.mult, ALU.add, t)
            return tt(V, y, y, w, ALU.mult, t)

        def modulated(dst, g_name, shift, scale, sums):
            b, t = sums
            tg = stt(gain[:, :], scale, 1.0, col(g_name, 0, KD), ALU.add, ALU.mult, PE.last()) if scale is not None else \
                copy(V, gain[:, :], col(g_name, 0, KD))
            t = inv_sqrt(rstd, banks.banks[b][:, 0:T], 1.0 / D, EPS, "eps", T, t)
            banks.release(b, t)
            done = []
            for k in range(KD):
                tk = stt(dst[:, k, :], xT[:, k, :], gain[:, k:k + 1], rstd[:, 0:T], ALU.mult, ALU.mult, t, tg)
                if shift is not None:
                    tk = act(dst[:, k, :], dst[:, k, :], ACT.Identity, tk, bias=shift[:, k:k + 1])
                done.append(tk)
            return done

        def linear_residual(kt, rhs, ready, gate):
            sb_, sbank, s_before = banks.take(hold=True)
            pending = []

            def add_square():
                n, q = pending.pop(0)
                return mm(sbank[:, 0:T], ones, hT[:, n, :], n == 0, n == KD - 1, s_before, q, signal=True)

            def read(n, ps, t):
                g = gate if isinstance(gate, float) else gate[:, n:n + 1]
                t = t_new = stt(xT[:, n, :], ps, g, xT[:, n, :], ALU.mult, ALU.add, t)
                pending.append((n, act(hT[:, n, :], xT[:, n, :], ACT.Square, t)))
                if n:
                    add_square()
                return t_new
            linear(KD, kt, rhs, ready, read)
            return sb_, add_square()

        def swiglu(h, ready, gate, fill=None):
            arena.at = 0
            hid = tiles(arena.take(KF * T), T)
            sig = [arena.take(T) for _ in range(2)]
            done, free = [], [None, None]
            for f in range(KF):
                bg, gbank, g_before = banks.take()
                bu, ubank, u_before = banks.take()
                for bank, before in ((gbank, g_before), (ubank, u_before)):
                    for k in range(KD):
                        w = feed.tile()
                        t = mm(bank[:, 0:T], w, h[:, k, :], k == 0, k == KD - 1, before, ready[k],
                               signal=k == KD - 1, weight=True)
                    if bank is gbank:
                        tg = t
                s = sig[f % 2]
                t1 = act(s, gbank[:, 0:T], ACT.Tanh, tg, free[f % 2], scale=0.5)
                t1 = stt(s, s, 1.0, gbank[:, 0:T], ALU.add, ALU.mult, t1)
                banks.reader[bg] = t1
                t1 = stt(hid[:, f, :], s, 0.5, ubank[:, 0:T], ALU.mult, ALU.mult, t1, t)
                banks.reader[bu] = free[f % 2] = t1
                done.append(t1)
                if fill:
                    fill(f)
            return linear_residual(KF, lambda k: hid[:, k, :], lambda k: done[k], gate)

        def staggered(n, *stages):
            for i in range(n + max(o for o, _ in stages)):
                for o, f in stages:
                    if 0 <= i - o < n:
                        f(i - o)

        xin = tiles(arena.take(NT * D), D)
        for c0 in range(0, KD, 2):
            b, bank, before = banks.take()
            for c in (c0, c0 + 1):
                for m in range(NT):
                    t = flip(bank[:, (c - c0) * T + m * P:(c - c0) * T + (m + 1) * P], xin[:, m, c * P:(c + 1) * P],
                             x_loaded, before)
            banks.reader[b] = t_xT = copy(V, xT_[:, c0 * T:(c0 + 2) * T], bank[:, :], t)

        t = sigmoid(silu_c[:, :], col("c", 0, KD))
        t = tt(V, silu_c[:, :], silu_c[:, :], col("c", 0, KD), ALU.mult, t)
        wide = silu_c[:, :].unsqueeze(2).to_broadcast([P, KD, 32])
        t_silu = copy(V, tiles(silu32[:, :], 32), wide, t)
        PE.wait(t_silu)

        def mod_blocks(*blocks):
            for b in blocks:
                bk, bank, before = banks.take(hold=True)
                for k in range(KD):
                    for j in range(4):
                        w = feed.tile(4)
                        t = mm(bank[32 * j:32 * j + 32, :], silu32[:, 32 * k:32 * k + 32], w, k == 0, k == KD - 1,
                               before, signal=(k, j) == (KD - 1, 3), weight=True)
                    if k < KD - 1:
                        yield
                t = copy(A, mod_rows[:, :], bank[:, :], t, V.last())
                banks.release(bk, t)
                bk, bank, before = banks.take()
                for c in range(4):
                    t1 = flip(bank[:, c * P:(c + 1) * P], mod_rows[:, c * P:(c + 1) * P], t, before)
                cols = bank[:, :].rearrange("p (c j r) -> p j c r", c=4, j=4)[:, :, :, 0]
                pick = lambda ap: ap.rearrange("p (j c) -> p j c", j=4)
                banks.reader[bk] = tt(V, pick(mod[:, 16 * b:16 * b + 16]), cols, pick(col("mod_b", 16 * b, 16)), ALU.add, t1)
                V.wait(V.last())
                yield

        def steps(gen, n):
            for _ in range(n):
                next(gen)
        steps(mod_blocks(0), KD)

        def mods(layer, j):
            return mod[:, layer * 48 + j * KD:layer * 48 + (j + 1) * KD]

        arena.at = 0
        y_br = arena.take(KL * T)
        XW = T + 3
        xpad = tiles(arena.take(KL * XW), XW)
        xc = arena.take(KL * T)
        rg = arena.take(KL * T)
        ig = arena.take(KL * T)
        aa = arena.take(KL * T)
        gs = [arena.take(T) for _ in range(2)]
        cvec = arena.take(4 * KL)
        t_pad = G.do(lambda e, i: e.memset(xpad[:, :, 0:3], 0.0))
        t = act(cvec[:, 0:KL], col("lambda", 0, KL), ACT.Exp, scale=-1.0)
        t = act(cvec[:, 0:KL], cvec[:, 0:KL], ACT.Ln, t, bias=col("one"))
        ts(V, cvec[:, 2 * KL:3 * KL], col("b_gates", KL, KL), 0.5, None, ALU.mult, None)
        t = ts(V, cvec[:, KL:2 * KL], cvec[:, 0:KL], 8.0, None, ALU.mult, None, t)
        t_cv = ts(V, cvec[:, 0:KL], cvec[:, 0:KL], -8.0, None, ALU.mult, None, t)
        h = modulated(hT, "norm_mix0", mods(0, 0), mods(0, 1), squares(t_xT))
        conv_done, gelu_done, gs_free = [], [], [None, None]
        early = mod_blocks(1, 2)

        def lru_in_read(n, ps, t):
            steps(early, mod_steps(n, 2 * KL, 2))
            if n < KL:
                t1 = copy(A, xpad[:, n, 3:XW], ps, t)
                o = xc[:, n * T:(n + 1) * T]
                t2 = ts(V, o, xpad[:, n, 0:T], col("conv_w", n), col("conv_b", n), ALU.mult, ALU.add, t1, t_pad)
                for k in range(1, 4):
                    t2 = stt(o, xpad[:, n, k:k + T], col("conv_w", k * KL + n), o, ALU.mult, ALU.add, t2)
                conv_done.append(t2)
                return t1
            n -= KL
            y, g = y_br[:, n * T:(n + 1) * T], gs[n % 2]
            t1 = copy(A, y, ps, t)
            t2 = tt(G, g, y, y, ALU.mult, t1, gs_free[n % 2])
            t2 = ts(G, g, g, 0.044715, 1.0, ALU.mult, ALU.add, t2)
            t2 = tt(G, g, g, y, ALU.mult, t2)
            t2 = act(g, g, ACT.Tanh, t2, scale=math.sqrt(2.0 / math.pi))
            gs_free[n % 2] = stt(y, g, 1.0, y, ALU.add, ALU.mult, t2)
            gelu_done.append(gs_free[n % 2])
            return t1
        linear(2 * KL, KD, lambda k: hT[:, k, :], lambda k: h[k], lru_in_read)
        for hh in range(LRU_HEADS):
            s = slice(2 * hh * T, (2 * hh + 2) * T)
            t_pre = {}

            def gate_read(n, ps, t):
                c = 2 * hh + n % 2
                o = slice(c * T, (c + 1) * T)
                if n < 2:
                    t1 = ts(V, rg[:, o], ps, col("b_gates", c), -80.0, ALU.add, ALU.max, t)
                    t_pre["r"] = act(rg[:, o], rg[:, o], ACT.Exp, t1, scale=-1.0)
                    return t1
                t1 = t_pre["i"] = act(ig[:, o], ps, ACT.Tanh, t, t_cv, scale=0.5, bias=cvec[:, 2 * KL + c:2 * KL + c + 1])
                return t1
            linear(4, 2, lambda k: xc[:, (2 * hh + k) * T:(2 * hh + k + 1) * T], lambda k: conv_done[2 * hh + k], gate_read)
            t = ts(V, rg[:, s], rg[:, s], 1.0, None, ALU.add, None, t_pre["r"])
            t_r = recip(rg[:, s], rg[:, s], t)
            t_ix = stt(ig[:, s], ig[:, s], 1.0, xc[:, s], ALU.add, ALU.mult, t_pre["i"], PE.last())
            for c in (2 * hh, 2 * hh + 1):
                o = slice(c * T, (c + 1) * T)
                act(aa[:, o], rg[:, o], ACT.Exp, t_r, scale=cvec[:, c:c + 1])
                t = act(rg[:, o], rg[:, o], ACT.Tanh, A.last(), scale=cvec[:, KL + c:KL + c + 1])
            t1 = tt(G, xc[:, s], aa[:, s], aa[:, s], ALU.mult, t, t_ix)
            t_w = stt(rg[:, s], xc[:, s], 1.0, rg[:, s], ALU.add, ALU.mult, t1)
        t_a = A.last()
        t_sq = act(rg, rg, ACT.Sqrt, t_w, scale=0.25)
        z_done = []
        for n in range(KL):
            s = slice(n * T, (n + 1) * T)
            t = tt(V, ig[:, s], ig[:, s], rg[:, s], ALU.mult, t_sq, t_ix)
            t = V.do(lambda e, i, s=s: e.tensor_tensor_scan(xc[:, s], aa[:, s], ig[:, s], 0.0, ALU.mult, ALU.add), t, t_a)
            z_done.append(stt(ig[:, s], xc[:, s], 0.5, y_br[:, s], ALU.mult, ALU.mult, t, gelu_done[n]))
        sums = linear_residual(KL, lambda k: ig[:, k * T:(k + 1) * T], lambda k: z_done[k], mods(0, 2))
        pr.all_join()

        def ffn(layer, sums, fill=None):
            h = modulated(hT, f"norm_ffn{layer}", mods(layer, 3), mods(layer, 4), sums)
            sums = swiglu(hT, h, mods(layer, 5), fill)
            pr.all_join()
            return sums
        later = mod_blocks(3, 4, 5, 6)
        sums = ffn(0, sums, lambda f: steps(later, mod_steps(f, KF, 4)))

        arena.at = 0
        KT = tiles(arena.take(KV_HEADS * T), T)
        VV = tiles(arena.take(NT * KV_HEADS * HD), KV_HEADS * HD)
        QT = tiles(arena.take(HEADS * T), T)
        OT = tiles(arena.take(HEADS * T), T)
        HB = [tiles(arena.take(HEADS * T), T) for _ in range(NT)]
        brow = arena.take(2 * T)[0:HEADS, :]
        b, bank, before = banks.take()
        t = mm(bank[0:HEADS, :], col("rel_bias", 0, HEADS)[0:BUCKETS + 1, :], col("onehot", 0, 2 * T)[0:BUCKETS + 1, :],
               True, True, before, signal=True)
        banks.reader[b] = copy(A, brow, bank[0:HEADS, :], t)
        A.wait(A.last())
        s_bias_w.count = 16
        A.ops.append(("op16", lambda e, i: e.dma_start(bias_scratch, brow), s_bias_w))
        A.wait(Token(s_bias_w, 16, None))
        t_hb = []
        for m in range(NT):
            src = bass.AP(tensor=bias_scratch.tensor, offset=m * P, ap=[[1, P], [2 * T, HEADS], [1, T]])
            s_bias_r[m].count = 16
            A.ops.append(("op16", lambda e, i, src=src, m=m: e.dma_start(HB[m], src), s_bias_r[m]))
            t_hb.append(Token(s_bias_r[m], 16, None))
        kvT = tiles(arena.take(KD * T), T)
        h = modulated(kvT, "kv_norm", mod[:, 96:96 + KD], mod[:, 96 + KD:112], sums)
        stt(gain[:, :], mods(1, 1), 1.0, col("norm_mix1", 0, KD), ALU.add, ALU.mult, V.last())
        tg = V.last()
        hq = []
        for k in range(KD):
            tk = stt(hT[:, k, :], xT[:, k, :], gain[:, k:k + 1], rstd[:, 0:T], ALU.mult, ALU.mult, tg)
            hq.append(act(hT[:, k, :], hT[:, k, :], ACT.Identity, tk, bias=mods(1, 0)[:, k:k + 1]))
        linear(KV_HEADS, KD, lambda k: kvT[:, k, :], lambda k: h[k], lambda n, ps, t: copy(A, KT[:, n, :], ps, t))
        (b0, v0, f0), (b1, v1, f1) = banks.take(), banks.take()
        for k in range(KD):
            w = feed.tile(4)
            t0 = mm(v0[:, :], kvT[:, k, 0:P], w, k == 0, k == KD - 1, f0, h[k], signal=k == KD - 1)
            t1 = mm(v1[:, :], kvT[:, k, P:T], w, k == 0, k == KD - 1, f1, signal=k == KD - 1, weight=True)
        banks.reader[b0] = copy(A, VV[:, 0, :], v0[:, :], t0)
        banks.reader[b1] = copy(V, VV[:, 1, :], v1[:, :], t1)
        t_kv = [A.last(), V.last()]
        t_q = []
        linear(HEADS, KD, lambda k: hT[:, k, :], lambda k: hq[k],
               lambda n, ps, t: t_q.append(copy(A, QT[:, n, :], ps, t)) or t_q[-1])
        SC = HD ** -0.5
        NBUF = 4
        pbuf, ptb, stat = [[arena.take(n) for _ in range(NBUF)] for n in (T, T, 4)]
        items = [(hd, m) for hd in range(HEADS) for m in range(NT)]
        t_exp, t_pt, p_free, pt_free, t_o = {}, {}, {}, {}, [None] * HEADS

        def scores(i):
            hd, m = items[i]
            nk = (m + 1) * P
            b, bank, before = banks.take()
            t = mm(bank[:, 0:nk], QT[:, hd, m * P:(m + 1) * P], KT[:, hd // 2, 0:nk], True, True, before, t_q[hd], t_kv, signal=True)
            pb, st = pbuf[i % NBUF][:, 0:nk], stat[i % NBUF]
            t = banks.reader[b] = stt(pb, bank[:, 0:nk], SC, HB[m][:, hd, T - nk:T][:, ::-1], ALU.mult, ALU.add, t, t_hb[m],
                                      p_free.get(i - NBUF))
            t = V.do(lambda e, i: e.tensor_reduce(st[:, 0:1], pb, AX, ALU.max, negate=True), t)
            t_exp[i] = act(pb, pb, ACT.Exp, t, bias=st[:, 0:1], accum_out=st[:, 1:2])

        def to_keys(i):
            hd, m = items[i]
            nk = (m + 1) * P
            pb, pt, st = pbuf[i % NBUF][:, 0:nk], ptb[i % NBUF], stat[i % NBUF]
            t = recip(st[:, 2:3], st[:, 1:2], t_exp[i])
            t = ts(V, pb, pb, st[:, 2:3], None, ALU.mult, None, t)
            b, bank, before = banks.take()
            for kt in range(m + 1):
                t1 = flip(bank[:, kt * P:(kt + 1) * P], pb[:, kt * P:(kt + 1) * P], t, before)
            p_free[i] = t1
            t_pt[i] = banks.reader[b] = copy(A, pt[:, 0:nk], bank[:, 0:nk], t1, pt_free.get(i - NBUF))

        def values(i):
            hd, m = items[i]
            pt = ptb[i % NBUF]
            b, bank, before = banks.take()
            for kt in range(m + 1):
                t = mm(bank[:, 0:P], VV[:, kt, hd // 2 * HD:(hd // 2 + 1) * HD], pt[:, kt * P:(kt + 1) * P], kt == 0, kt == m,
                       t_pt[i], before, signal=True)
            pt_free[i] = t
            t_o[hd] = banks.reader[b] = copy(V, OT[:, hd, m * P:(m + 1) * P], bank[:, 0:P], t)
        staggered(len(items), (0, scores), (2, to_keys), (3, values))
        sums = linear_residual(HEADS, lambda k: OT[:, k, :], lambda k: t_o[k], mods(1, 2))
        pr.all_join()
        sums = ffn(1, sums)

        t = modulated(xT, "final_norm", None, None, sums)
        h = modulated(hT, "norm_mix_2", None, None, squares(t))

        arena.at = 0
        yaT = arena.take(KR * T)
        ybT = arena.take(KR * T)
        ycT = arena.take(KR * T)
        keep = arena.at
        arena.at = KR * T
        raw = arena.take(15 * T)
        TW = T + 2
        stage = [arena.t[:, arena.n - (2 - j) * TW:arena.n - (1 - j) * TW] for j in range(2)]
        mid = arena.take(15)
        t_z = G.do(lambda e, i: e.memset(stage[0], 0.0))
        t_z = G.do(lambda e, i: e.memset(stage[1], 0.0))
        t = tt(V, mid, col("shift_prev", 0, 15), col("shift_next", 0, 15), ALU.add)
        t_mid = ts(V, mid, mid, -1.0, 1.0, ALU.mult, ALU.add, t)
        st_free = [t_z, t_z]

        def shift_read(n, ps, t):
            st = stage[n % 2]
            t1 = copy(A, st[:, 1:T + 1], ps, t, st_free[n % 2])
            o = raw[:, n * T:(n + 1) * T]
            t2 = ts(V, o, st[:, 1:T + 1], mid[:, n:n + 1], None, ALU.mult, None, t1, t_mid)
            t2 = stt(o, st[:, 0:T], col("shift_prev", n), o, ALU.mult, ALU.add, t2)
            st_free[n % 2] = stt(o, st[:, 2:T + 2], col("shift_next", n), o, ALU.mult, ALU.add, t2)
            return t1
        linear(15, KD, lambda k: hT[:, k, :], lambda k: h[k], shift_read)
        pr.all_join()

        rT, kT_, vT = raw[:, 0:KR * T], raw[:, KR * T:2 * KR * T], raw[:, 2 * KR * T:3 * KR * T]
        wd, ad, gd = [raw[:, (12 + j) * T:(13 + j) * T] for j in range(3)]
        half0 = arena.take(4 * KR)
        omk = arena.take(KR)
        ts(V, half0, col("w0", 0, 4 * KR), 0.5, None, ALU.mult, None)
        ts(V, omk, col("k_a", 0, KR), -1.0, 1.0, ALU.mult, ALU.add)
        act(wd, wd, ACT.Tanh)
        t_gd = sigmoid(gd, gd)
        pr.all_join()

        class Unit:
            def __init__(self):
                self.QR = [arena.take(2 * NT * P) for _ in range(2)]
                self.BT = [arena.take(T) for _ in range(2)]
                self.CT = [arena.take(T) for _ in range(2)]
                self.BCtok = arena.take(4 * P)
                self.Btok, self.Ctok = self.BCtok[:, 0:2 * P], self.BCtok[:, 2 * P:4 * P]
                self.psc = [arena.take(1) for _ in range(2)]
                self.ksum, self.vs = arena.take(T), arena.take(T)
                self.XT = [arena.take(4 * P) for _ in range(2)]
                self.MB = [arena.take(4 * P) for _ in range(2)]
        units = [Unit(), Unit()]
        LTb, Bm, Xb, Tb, LCb, MCb = [[arena.take(4 * P) for _ in range(2)] for _ in range(6)]
        Rb, Ub = arena.take(2 * P), arena.take(2 * P)
        sbd = [arena.take(P) for _ in range(2)]
        kk, sq, w_, a_, f_, u_, inv_, iw_ = [arena.take(T) for _ in range(8)]
        ym, y2, bo = [arena.take(T) for _ in range(3)]
        zero = col("zero").to_broadcast([P, P])
        strict, incl = tiles(col("strict", 0, 2 * P), P), tiles(col("incl", 0, 2 * P), P)
        level = tiles(col("level", 0, LEVELS * P), P)
        id4 = ident.unsqueeze(1).to_broadcast([P, 4, P])
        v4 = lambda ap: ap.rearrange("p (d h n) -> p d h n", d=2, h=2)
        B = banks.banks
        tail_done = [None] * KR

        att_ = arena.take(6 * T)
        att = tiles(att_, T)
        PW = 16 + T
        zb = tiles(arena.take(4 * PW), PW)
        t_zb0 = G.do(lambda e, i: e.memset(zb[:, :, :], 0.0))
        gates = [arena.take(T), mod_rows[:, 0:T], mod_rows[:, T:2 * T], silu32[:, :], stage[0][:, 0:T], stage[1][:, 0:T]]
        n_early = len(gates)
        assert arena.at <= arena.n - 2 * TW
        for j in range(24 - n_early):
            gates.append(arena.t[:, keep + j * T:keep + (j + 1) * T])
        keep += (24 - n_early) * T
        t_att, t_zb, t_gates = [], [], []
        FILL = 7
        banks.held.add(FILL)

        def keep_token(toks, t):
            toks.append(t)
            return t

        def background():
            src, ready = (lambda k: hT[:, k, :]), (lambda k: h[k])
            yield from linear_steps(6, KD, src, ready, lambda n, ps, t: keep_token(t_att, copy(A, att[:, n, :], ps, t)), FILL)
            yield from linear_steps(4, KD, src, ready, lambda n, ps, t: keep_token(t_zb, copy(A, zb[:, n, 8:8 + T], ps, t, t_zb0)), FILL)
            yield from linear_steps(24, KD, src, ready, lambda n, ps, t: keep_token(t_gates, act(gates[n], ps, ACT.Tanh, t, scale=0.5)), FILL)
        filler = background()
        left = [(10 + n_early) * KD]

        def fill(n):
            for _ in range(min(n, left[0])):
                next(filler)
                left[0] -= 1

        def tile(s, d):
            return s if d == 0 else 1 - s

        def bank(b):
            return B[b], banks.reader[b]

        def prepare(ct, un):
            sl = slice(ct * T, (ct + 1) * T)
            k_, r_, v_ = kT_[:, sl], rT[:, sl], vT[:, sl]
            if ct >= 1:
                A.wait(units[(ct - 1) % 2].t_ops)
            if ct >= 2:
                for e in (V, A):
                    e.wait(tail_done[ct - 2])
            t = ts(V, kk, k_, col("k_k", ct), None, ALU.mult, None)
            t_sq = tt(V, sq, kk, kk, ALU.mult, t)
            b6, before = bank(6)
            for m in range(NT):
                t = flip(b6[:, m * P:(m + 1) * P], v_[:, m * P:(m + 1) * P], before)
            un.t_vs = banks.reader[6] = copy(A, un.vs, b6[:, 0:T], t)
            w2, a2 = col("w2", ct * P, P), col("a2", ct * P, P)
            yield
            b6, before = bank(6)
            t = mm(b6[:, 0:T], blk, sq, True, True, t_sq, before, signal=True)
            t = banks.reader[6] = ts(V, sq, b6[:, 0:T], 1e-24, None, ALU.max, None, t)
            t = act(sq, sq, ACT.Sqrt, t)
            t = recip(sq, sq, t)
            t_kk = tt(V, kk, kk, sq, ALU.mult, t)
            un.t_ops = []
            for d in range(2):
                lo = 64 * d
                yield
                b6, before = bank(6)
                mm(b6[:, 0:T], w2[lo:lo + 64, :], wd[lo:lo + 64, :], True, True, before)
                t = mm(b6[:, T:2 * T], a2[lo:lo + 64, :], ad[lo:lo + 64, :], True, True, signal=True)
                t_a = act(w_, b6[:, 0:T], ACT.Tanh, t, *un.t_ops, scale=0.5, bias=half0[:, d * KR + ct:d * KR + ct + 1])
                t, t_a = t_a, act(a_, b6[:, T:2 * T], ACT.Tanh, scale=0.5, bias=half0[:, (2 + d) * KR + ct:(2 + d) * KR + ct + 1])
                banks.reader[6] = t_a
                t = ts(V, w_, w_, 0.5, 0.5, ALU.mult, ALU.add, t)
                t_w = act(w_, w_, ACT.Exp, t, scale=-math.exp(-0.5))
                t_a = ts(V, a_, a_, 0.5, 0.5, ALU.mult, ALU.add, t_a)
                t = ts(V, u_, a_, col("k_a", ct), omk[:, ct:ct + 1], ALU.mult, ALU.add, t_a)
                t_kd = tt(V, u_, u_, k_, ALU.mult, t)
                if d == 0:
                    t_ks = copy(V, un.ksum, u_, t_kd)
                else:
                    t_ks = tt(V, un.ksum, un.ksum, u_, ALU.add, t_kd, t_ks)
                yield
                for m in range(NT):
                    ws, fs = w_[:, m * P:(m + 1) * P], f_[:, m * P:(m + 1) * P]
                    if d:
                        ws, fs = ws[:, ::-1], fs[:, ::-1]
                    t = V.do(lambda e, i, ws=ws, fs=fs: e.tensor_tensor_scan(fs, ws, zero, 1.0, ALU.mult, ALU.add), t_w)
                t_inv = recip(inv_, f_, t)
                t_iw = recip(iw_, w_, t_w)
                yield
                mid_ = [m * P + (63 if d == 0 else 64) for m in range(NT)]
                first, second = (0, 1) if d == 0 else (1, 0)
                end = first * P + (P - 1 if d == 0 else 0)
                t = tt(V, un.psc[d], f_[:, end:end + 1], inv_[:, mid_[first]:mid_[first] + 1], ALU.mult, t_inv)
                un.t_ps = tt(V, un.psc[d], un.psc[d], f_[:, mid_[second]:mid_[second] + 1], ALU.mult, t)
                last = []
                for m in range(NT):
                    ms = slice(m * P, (m + 1) * P)
                    im, fm = inv_[:, mid_[m]:mid_[m] + 1], f_[:, mid_[m]:mid_[m] + 1]
                    q, rr = un.QR[d][:, 2 * m * P:(2 * m + 1) * P], un.QR[d][:, (2 * m + 1) * P:(2 * m + 2) * P]
                    t_r = stt(rr, f_[:, ms], im, r_[:, ms], ALU.mult, ALU.mult, t_inv)
                    t1 = stt(q, f_[:, ms], im, kk[:, ms], ALU.mult, ALU.mult, t_kk)
                    t2 = stt(un.BT[d][:, ms], inv_[:, ms], fm, kk[:, ms], ALU.mult, ALU.mult)
                    last.append(stt(un.CT[d][:, ms], inv_[:, ms], fm, u_[:, ms], ALU.mult, ALU.mult))
                    last.append(tt(V, q, q, iw_[:, ms], ALU.mult, t1, t_iw))
                    last.append(tt(V, un.BT[d][:, ms], un.BT[d][:, ms], a_[:, ms], ALU.mult, t2))
                    if m == 0:
                        yield
                un.t_ops.append(last[-1])
            yield
            b6, before = bank(6)
            for j, src in enumerate((un.BT, un.CT)):
                for d in range(2):
                    m = tile(0, d)
                    t = flip(b6[:, (2 * j + d) * P:(2 * j + d + 1) * P], src[d][:, m * P:(m + 1) * P], *un.t_ops, before)
            un.t_tok = banks.reader[6] = copy(A, un.BCtok, b6[:, :], t)

        def gram(bb, un, left, s, hh, *toks):
            for d in range(2):
                m = tile(s, d)
                t = mm(bb[:, 2 * d * P:2 * (d + 1) * P], left[d][64 * hh:64 * hh + 64, m * P:(m + 1) * P],
                       un.QR[d][64 * hh:64 * hh + 64, 2 * m * P:2 * (m + 1) * P], True, True, *toks, signal=True)
            return t, bb[:, :].rearrange("p (d c n) -> p d c n", d=2, c=2)

        def finish(ct, un):
            sl = slice(ct * T, (ct + 1) * T)
            first_y = [None, None]
            t_s = t_yy = None
            for s in range(2):
                for hh in range(2):
                    bb, before = bank(4 + hh)
                    t, both = gram(bb, un, un.CT, s, hh, before)
                    t1 = tt(V, v4(LCb[s])[:, :, hh, :], both[:, :, 0, :], strict, ALU.mult, t)
                    t_c = banks.reader[4 + hh] = tt(V, v4(MCb[s])[:, :, hh, :], both[:, :, 1, :], incl, ALU.mult)
                yield
            for s in range(2):
                bR, before = bank(4)
                for d in range(2):
                    m = tile(s, d)
                    o = bR[:, d * P:(d + 1) * P]
                    if s:
                        mm(o, un.QR[d][:, 2 * m * P:(2 * m + 1) * P], sbd[d], True, False, before, t_s)
                    for hh in range(2):
                        t = mm(o[:, 64 * hh:64 * hh + 64], LCb[s][:, (2 * d + hh) * P:(2 * d + hh + 1) * P],
                               un.vs[:, m * P + 64 * hh:m * P + 64 * hh + 64], not s, True, before, t_c, un.t_vs, signal=True)
                t_R = banks.reader[4] = copy(V, Rb, bR[:, 0:2 * P], t)
                yield
                bU, before = bank(5)
                for d in range(2):
                    for hh in range(2):
                        c = slice(d * P + 64 * hh, d * P + 64 * hh + 64)
                        t1 = mm(bU[:, c], un.XT[s][:, (2 * d + hh) * P:(2 * d + hh + 1) * P], Rb[:, c], True, True, t_R, un.t_x, before,
                                signal=True)
                t_u = banks.reader[5] = ts(V, Ub, bU[:, 0:2 * P], -1.0, None, ALU.mult, None, t1)
                yield
                if s == 0:
                    toks = []
                    for d in range(2):
                        m = tile(s, d)
                        bS, before = bank(4 + d)
                        mm(bS[:, 0:P], un.Btok[:, d * P:(d + 1) * P], Ub[:, d * P:(d + 1) * P], True, False, t_u, un.t_tok, before)
                        t = mm(bS[:, 0:P], un.Ctok[:, d * P:(d + 1) * P], un.vs[:, m * P:(m + 1) * P], False, True, signal=True)
                        t_s = banks.reader[4 + d] = stt(sbd[d], bS[:, 0:P], un.psc[d], blk, ALU.mult, ALU.mult, t, un.t_ps)
                    yield
                for d in range(2):
                    m = tile(s, d)
                    bY, before = bank(4 + d)
                    o = bY[:, 0:P]
                    if s:
                        mm(o, sbd[d], un.QR[d][:, (2 * m + 1) * P:(2 * m + 2) * P], True, False, t_s, before)
                    for hh in range(2):
                        oh = bY[64 * hh:64 * hh + 64, 0:P]
                        q = slice((2 * d + hh) * P, (2 * d + hh + 1) * P)
                        mm(oh, Ub[:, d * P + 64 * hh:d * P + 64 * hh + 64], un.MB[s][:, q], not s, False, t_u, before)
                        t = mm(oh, un.vs[:, m * P + 64 * hh:m * P + 64 * hh + 64], MCb[s][:, q], False, True, signal=True)
                    y = yaT[:, ct * T + m * P:ct * T + (m + 1) * P]
                    if s == 0:
                        first_y[m] = banks.reader[4 + d] = copy(V, y, o, t)
                    else:
                        t_yy = banks.reader[4 + d] = tt(V, y, o, y, ALU.add, t, first_y[m])
                yield
            yv = yaT[:, sl]
            t_bo = stt(bo, un.ksum, col("r_k", ct), rT[:, sl], ALU.mult, ALU.mult)
            bb, before = bank(4)
            t = mm(bb[:, 0:T], blk, yv, True, True, t_yy, before, signal=True)
            t_m = banks.reader[4] = stt(ym, bb[:, 0:T], -1.0 / 64, yv, ALU.mult, ALU.add, t)
            t = tt(V, y2, ym, ym, ALU.mult, t_m)
            yield
            bb, before = bank(4)
            bb2, before2 = bank(5)
            t = mm(bb[:, 0:T], blk, y2, True, True, t, before, signal=True)
            t2 = mm(bb2[:, 0:T], blk, bo, True, True, t_bo, before2, signal=True)
            t_bo = banks.reader[5] = tt(V, bo, bb2[:, 0:T], vT[:, sl], ALU.mult, t2)
            t = banks.reader[4] = inv_sqrt(rstd, bb[:, 0:T], 1.0 / 64, LN_EPS, "ln_eps", T, t)
            t = tt(V, ym, ym, rstd[:, 0:T], ALU.mult, t)
            t = ts(V, ym, ym, col("ln_w", ct), col("ln_b", ct), ALU.mult, ALU.add, t)
            t = tt(V, ym, ym, bo, ALU.add, t, t_bo)
            yield
            bb, before = bank(5)
            t1 = mm(bb[:, 0:T], col("g2", ct * P, P), gd, True, True, before, signal=True)
            t = banks.reader[5] = tt(V, yv, ym, bb[:, 0:T], ALU.mult, t, t1)
            tail_done[ct] = [PE.last(), t]

        def invert(un, others):
            def between():
                fill(1)
                for g in others:
                    if next(g, self_) is not self_:
                        return
            self_ = object()
            t_lt, t_x, t_xt, t_bm = [None] * 2, [None] * 2, [None] * 2, [None] * 2
            for s in range(2):
                for hh in range(2):
                    b = 2 * s + hh
                    bb, before = bank(b)
                    t, both = gram(bb, un, un.BT, s, hh, before, *un.t_ops)
                    tt(V, v4(LTb[s])[:, :, hh, :], both[:, :, 0, :], strict, ALU.mult, t)
                    t_lt[s] = banks.reader[b] = tt(V, v4(un.MB[s])[:, :, hh, :], both[:, :, 1, :], incl, ALU.mult)

            def blocks_of(lv, s, *toks):
                mk = level[:, lv, :].unsqueeze(1).to_broadcast([P, 4, P])
                return tt(G, tiles(Bm[s], P), tiles(LTb[s], P), mk, ALU.mult, *toks)
            for s in range(2):
                t_bm[s] = blocks_of(0, s, t_lt[s], PE.last())
            for lv in range(LEVELS):
                if lv == 0:
                    for s in range(2):
                        t_xt[s] = tt(V, tiles(un.XT[s], P), id4, tiles(Bm[s], P), ALU.subtract, t_bm[s])
                        t_bm[s] = blocks_of(1, s, t_xt[s])
                else:
                    for s in range(2):
                        bb, before = bank(2 * s)
                        for q in range(4):
                            c = slice(q * P, (q + 1) * P)
                            t = mm(bb[:, c], Bm[s][:, c], Xb[s][:, c], True, True, t_bm[s], t_x[s], before, signal=q == 3)
                        t_x[s] = banks.reader[2 * s] = copy(A, Tb[s], bb[:, :], t)
                        if lv < LEVELS - 1:
                            t_bm[s] = blocks_of(lv + 1, s, t)
                    between()
                    for s in range(2):
                        bb, before = bank(2 * s + 1)
                        for q in range(4):
                            c = slice(q * P, (q + 1) * P)
                            t = mm(bb[:, c], Tb[s][:, c], un.XT[s][:, c], True, True, t_x[s], t_xt[s], before, signal=q == 3)
                        t_xt[s] = banks.reader[2 * s + 1] = tt(V, un.XT[s], un.XT[s], bb[:, :], ALU.subtract, t)
                    between()
                if lv < LEVELS - 1:
                    for s in range(2):
                        bb, before = bank(2 * s)
                        for q in range(4):
                            c = slice(q * P, (q + 1) * P)
                            t = flip(bb[:, c], un.XT[s][:, c], t_xt[s], before)
                        t_x[s] = banks.reader[2 * s] = copy(A, Xb[s], bb[:, :], t)
                    between()
            un.t_x = t_xt
            for g in others:
                for _ in g:
                    pass

        for _ in prepare(0, units[0]):
            fill(FIRST)
        tail = iter(())
        for ct in range(KR):
            un = units[ct % 2]
            ahead = prepare(ct + 1, units[(ct + 1) % 2]) if ct + 1 < KR else iter(())
            invert(un, [tail, ahead])
            tail = finish(ct, un)
        for _ in tail:
            fill(LAST)
        fill(left[0])
        pr.all_join()
        left[0] = (24 - n_early) * KD

        arena.at = keep
        asq, arot = arena.take(5 * T), arena.take(5 * T)
        arstd = arena.take(3 * 5 * T)
        kz = [[arena.take(T) for _ in range(2)] for _ in range(2)]
        vtok = arena.take(NT * P)
        qk_gain = arena.take(2)
        ts(V, qk_gain[:, 0:1], col("q_norm"), 64 ** -0.5, None, ALU.mult, None)
        copy(V, qk_gain[:, 1:2], col("k_norm"))
        t_kz0 = [G.do(lambda e, i, z=kz[g][hh]: e.memset(z, 0.0)) for g in range(2) for hh in range(2)]
        t_s = [tt(V, asq[:, n * T:(n + 1) * T], att[:, n, :], att[:, n, :], ALU.mult, t_att[n]) for n in range(5)]
        stat_banks = []
        for n in range(5):
            if n % 2 == 0:
                b, bank, before = banks.take(hold=True)
                stat_banks.append((b, bank))
            t = mm(bank[:, n % 2 * T:(n % 2 + 1) * T], blk, asq[:, n * T:(n + 1) * T], True, True, t_s[n], before, signal=True)
            if n % 2 or n == 4:
                c0, c1 = n // 2 * 2 * T, (n + 1) * T
                t = ts(V, arstd[:, 5 * T + c0:5 * T + c1], bank[:, 0:c1 - c0], 1.0 / 64, EPS, ALU.mult, ALU.add, t)
                banks.release(b, t)
        fill(16)
        y, z, w = arstd[:, 0:5 * T], arstd[:, 5 * T:10 * T], arstd[:, 10 * T:15 * T]
        t = act(y, z, ACT.Ln, t)
        t = act(y, y, ACT.Exp, t, scale=-0.5)
        t = tt(V, w, y, y, ALU.mult, t)
        t = tt(V, w, w, z, ALU.mult, t)
        t = ts(V, w, w, -0.5, 1.5, ALU.mult, ALU.add, t)
        t = tt(V, y, y, w, ALU.mult, t)
        t1 = stt(att_[:, 0:4 * T], att_[:, 0:4 * T], qk_gain[:, 0:1], y[:, 0:4 * T], ALU.mult, ALU.mult, t)
        t1 = stt(att[:, 4, :], att[:, 4, :], qk_gain[:, 1:2], y[:, 4 * T:5 * T], ALU.mult, ALU.mult, t)
        for n in range(5):
            b, bank, before = banks.take()
            t = mm(bank[:, 0:T], col("pair", 0, P), att[:, n, :], True, True, t1, before, signal=True)
            banks.reader[b] = tt(V, arot[:, n * T:(n + 1) * T], bank[:, 0:T], col("sin", 0, T), ALU.mult, t)
        fill(12)
        t_rot = V.last()
        t = tt(V, tiles(att_[:, 0:5 * T], T), tiles(att_[:, 0:5 * T], T), col("cos", 0, T).unsqueeze(1).to_broadcast([P, 5, T]),
               ALU.mult, t_rot)
        t_rope = tt(V, att_[:, 0:5 * T], att_[:, 0:5 * T], arot, ALU.add, t)
        kT = att[:, 4, :]
        b, bank, before = banks.take()
        t = mm(bank[:, 0:T], col("half", 0, P), kT, True, True, t_rope, before, signal=True)
        copy(V, kz[0][0][0:64, :], kT[0:64, :], t_kz0, t_rope)
        copy(V, kz[1][1][64:128, :], kT[64:128, :])
        copy(V, kz[0][1][64:128, :], bank[64:128, 0:T], t)
        t_kz = banks.reader[b] = copy(V, kz[1][0][0:64, :], bank[0:64, 0:T])
        fill(4)
        b, bank, before = banks.take()
        for m in range(NT):
            t = flip(bank[:, m * P:(m + 1) * P], att[:, 5, m * P:(m + 1) * P], t_att[5], before)
        t_vt = banks.reader[b] = copy(A, vtok, bank[:, 0:T], t)

        s1, s2 = arena.take(PW), arena.take(PW)
        pooled = tiles(arena.take(4 * T), T)
        t_z2 = G.do(lambda e, i: e.memset(s1, 0.0))
        t_z2 = G.do(lambda e, i: e.memset(s2, 0.0))
        t_pooled = []
        for g, w in enumerate(WINDOWS):
            cur, width = zb[:, g, :], 1
            t = t_zb[g]
            bufs = [s1, s2]
            while width < w:
                nxt = bufs[0]
                bufs.reverse()
                t = tt(G, nxt[:, 0:PW - width], cur[:, 0:PW - width], cur[:, width:PW], ALU.add, t, t_z2)
                cur, width = nxt, 2 * width
            lo = w // 2
            t = tt(G, pooled[:, g, :], cur[:, 8 - lo:8 - lo + T], col("inv_cnt", g * T, T), ALU.mult, t)
            t_pooled.append(tt(G, pooled[:, g, :], pooled[:, g, :], zb[:, g, 8:8 + T], ALU.subtract, t))

        pbuf, ptb, stat = [[arena.take(n) for _ in range(NBUF)] for n in (T, NT * P, 4)]
        items = [(hd, m) for hd in range(8) for m in range(NT)]
        t_exp, t_pt, p_free, pt_free = {}, {}, {}, {}

        def scores2(i):
            hd, m = items[i]
            b, bank, before = banks.take()
            t = mm(bank[:, 0:T], att[:, hd // 2, m * P:(m + 1) * P], kz[hd // 4][hd % 2], True, True, t_kz, before, signal=True)
            pb, st = pbuf[i % NBUF], stat[i % NBUF]
            t = V.do(lambda e, i: e.tensor_reduce(st[:, 0:1], bank[:, 0:T], AX, ALU.max, negate=True), t, p_free.get(i - NBUF))
            t_exp[i] = banks.reader[b] = act(pb, bank[:, 0:T], ACT.Exp, t, bias=st[:, 0:1], accum_out=st[:, 1:2])

        def to_keys2(i):
            hd, m = items[i]
            pb, pt, st = pbuf[i % NBUF], ptb[i % NBUF], stat[i % NBUF]
            t = recip(st[:, 2:3], st[:, 1:2], t_exp[i])
            t = ts(V, pb, pb, st[:, 2:3], None, ALU.mult, None, t)
            b, bank, before = banks.take()
            for kt in range(NT):
                t1 = flip(bank[:, kt * P:(kt + 1) * P], pb[:, kt * P:(kt + 1) * P], t, before)
            p_free[i] = t1
            t_pt[i] = banks.reader[b] = copy(A, pt, bank[:, 0:T], t1, pt_free.get(i - NBUF))

        def values2(i):
            hd, m = items[i]
            g, lo, pt = hd // 4, 64 * (hd % 2), ptb[i % NBUF]
            b, bank, before = banks.take()
            o = bank[lo:lo + 64, 0:P]
            for kt in range(NT):
                t = mm(o, vtok[:, kt * P + 64 * g:kt * P + 64 * g + 64], pt[:, kt * P:(kt + 1) * P], kt == 0, kt == NT - 1,
                       t_pt[i], t_vt, before, signal=True)
            pt_free[i] = t
            at_ = hd // 2 * T + m * P
            banks.reader[b] = copy(V, ycT[lo:lo + 64, at_:at_ + P], o, t)
        staggered(len(items), (0, scores2), (0, lambda i: fill(4)), (2, to_keys2), (2, lambda i: fill(4)), (3, values2))
        fill(left[0])
        banks.release(FILL, banks.reader[FILL])
        for g in range(4):
            b, bank, before = banks.take()
            t1 = mm(bank[:, 0:T], col("pool_w", g * P, P), pooled[:, g, :], True, True, t_pooled[g], before, signal=True)
            banks.reader[b] = act(ybT[:, g * T:(g + 1) * T], bank[:, 0:T], ACT.Copy, t1, scale=col("pool_scale", g))
        pr.all_join()

        arena.at = keep
        mg = tiles(arena.take(KD * T), T)
        part = [arena.take(T) for _ in range(2)]
        part_free = [None, None]
        m_done = []
        for n in range(KD):
            for bi, src in enumerate((yaT, ybT, ycT)):
                gate = gates[3 * n + bi]

                def branch_read(_, ps, t):
                    if bi == 0:
                        return stt(mg[:, n, :], gate, 1.0, ps, ALU.add, ALU.mult, t)
                    p = part[bi - 1]
                    t1 = stt(p, gate, 1.0, ps, ALU.add, ALU.mult, t, part_free[bi - 1])
                    part_free[bi - 1] = tt(V, mg[:, n, :], mg[:, n, :], p, ALU.add, t1)
                    return t1
                linear(1, KR, lambda k: src[:, k * T:(k + 1) * T], lambda k: None, branch_read)
            m_done.append(V.last())
        sums = linear_residual(KD, lambda k: mg[:, k, :], lambda k: m_done[k], 0.5)
        pr.all_join()

        h = modulated(hT, "norm_ffn_2", None, None, sums)
        arena.at = 0
        htok = tiles(arena.take(NT * D), D)
        sel = arena.take(NT * EXPERTS * CAP)
        gsel = arena.take(NT * EXPERTS * CAP)
        xall = arena.take(KD * EXPERTS * CAP)
        work = arena.at
        aff = arena.take(NT * EXPERTS)
        st = arena.take(4 * NT)
        affT = arena.take(T)[0:EXPERTS, :]
        wk = arena.take(T)[0:EXPERTS, :]
        mk = arena.take(T)[0:EXPERTS, :]
        ps_ = arena.take(T)[0:EXPERTS, :]
        m8 = arena.take(8)[0:EXPERTS, :]
        post = arena.take(NT * EXPERTS)
        for m in range(NT):
            for q in range(2):
                b, bank, before = banks.take()
                for c in range(4):
                    t = flip(bank[:, c * P:(c + 1) * P], hT[:, 4 * q + c, m * P:(m + 1) * P], before, h[-1])
                banks.reader[b] = copy(A, htok[:, m, q * 512:(q + 1) * 512], bank[:, :], t)
        t_ht = A.last()
        for m in range(NT):
            b, bank, before = banks.take()
            for k in range(KD):
                t = mm(bank[:, 0:EXPERTS], hT[:, k, m * P:(m + 1) * P], col("router", k * EXPERTS, EXPERTS), k == 0, k == KD - 1,
                       before, signal=k == KD - 1)
            s_, af = st[:, 4 * m:4 * m + 4], aff[:, m * EXPERTS:(m + 1) * EXPERTS]
            t1 = V.do(lambda e, i, s_=s_, bank=bank: e.tensor_reduce(s_[:, 0:1], bank[:, 0:EXPERTS], AX, ALU.max), t)
            t1 = ts(V, s_[:, 1:2], s_[:, 0:1], -1.0, None, ALU.mult, None, t1)
            t1 = banks.reader[b] = act(af, bank[:, 0:EXPERTS], ACT.Exp, t1, bias=s_[:, 1:2], accum_out=s_[:, 2:3])
            t1 = recip(s_[:, 3:4], s_[:, 2:3], t1)
            t_af = ts(V, af, af, s_[:, 3:4], None, ALU.mult, None, t1)
        b, bank, before = banks.take()
        for m in range(NT):
            t = flip(bank[0:EXPERTS, m * P:(m + 1) * P], aff[:, m * EXPERTS:(m + 1) * EXPERTS], t_af, before)
        t = banks.reader[b] = copy(V, affT, bank[0:EXPERTS, 0:T], t)
        t = copy(V, wk, affT, t)
        for _ in range(CAP // 8):
            t = V.do(lambda e, i: e.max(m8, wk), t)
            t = V.do(lambda e, i: e.match_replace(out=wk, in_to_replace=m8, in_values=wk, imm_value=-1.0), t)
        t_mk = ts(V, mk, wk, 0.0, None, ALU.is_lt, None, t)
        t = V.do(lambda e, i: e.tensor_tensor_scan(ps_, mk, col("zero")[0:EXPERTS, :].to_broadcast([EXPERTS, T]), 0.0, ALU.add, ALU.add), t_mk)
        t = tt(V, ps_, ps_, mk, ALU.mult, t)
        t = ts(V, ps_, ps_, -1.0, None, ALU.add, None, t)
        b, bank, before = banks.take()
        for m in range(NT):
            t1 = flip(bank[:, m * EXPERTS:(m + 1) * EXPERTS], ps_[:, m * P:(m + 1) * P], t, before)
        t = banks.reader[b] = copy(V, post, bank[:, 0:NT * EXPERTS], t1)
        iota = col("iota", 0, CAP).unsqueeze(1).to_broadcast([P, EXPERTS, CAP])
        selv = sel.rearrange("p (m e c) -> p m e c", m=NT, e=EXPERTS)
        gselv = gsel.rearrange("p (m e c) -> p m e c", m=NT, e=EXPERTS)
        for m in range(NT):
            pv = post[:, m * EXPERTS:(m + 1) * EXPERTS].unsqueeze(2).to_broadcast([P, EXPERTS, CAP])
            av = aff[:, m * EXPERTS:(m + 1) * EXPERTS].unsqueeze(2).to_broadcast([P, EXPERTS, CAP])
            t1 = tt(V, selv[:, m], pv, iota, ALU.is_equal, t)
            t2 = tt(V, gselv[:, m], selv[:, m], av, ALU.mult, t1)
        for k in range(KD):
            b, bank, before = banks.take()
            for m in range(NT):
                t = mm(bank[:, :], htok[:, m, k * P:(k + 1) * P], sel[:, m * 512:(m + 1) * 512], m == 0, m == NT - 1,
                       before, t2, t_ht, signal=m == NT - 1)
            banks.reader[b] = copy(A if k % 2 else V, xall[:, k * 512:(k + 1) * 512], bank[:, :], t)
        pr.all_join()

        arena.at = work
        xg, g4 = arena.take(KD * CAP), arena.take(NT * P)
        act_, hid, hidT, ye, comb = [arena.take(T) for _ in range(5)]
        zeros = arena.take(P)
        bG, bU, bT, bY, acc = B[0], B[1], B[2], B[3], B[4:8]
        xv = tiles(xall, EXPERTS * CAP)
        gv = tiles(gsel, EXPERTS * CAP)
        QW = D // 4
        t = G.do(lambda e, i: e.memset(zeros, 0.0))
        for j in range(4):
            mm(acc[j][:, :], zeros, xall[:, 0:512], True, False, t)
        pr.all_join()
        with pr.repeat(EXPERTS):
            mix_before, up_before, hidT_before, ye_before = Later(), Later(), Later(), Later()
            t_x = ts(V, tiles(xg, CAP), lambda i: xv[:, :, bass.ds(i * CAP, CAP)], 1.0, None, ALU.mult, None, up_before)
            for m in range(NT):
                t_g4 = ts(V, g4[:, m * P:(m + 1) * P].rearrange("p (j c) -> p j c", j=4),
                          lambda i, m=m: gv[:, m:m + 1, bass.ds(i * CAP, CAP)].to_broadcast([P, 4, CAP]),
                          1.0, None, ALU.mult, None)

            def quarters(bank, lhs, ready, before):
                for k in range(KD):
                    for j in range(4):
                        w = feed.tile(2)
                        t = mm(bank[32 * j:32 * j + 32, 0:QW], lhs(k), w, k == 0, k == KD - 1, ready, before if (k, j) == (0, 0) else None,
                               signal=(k, j) == (KD - 1, 3), weight=True)
                return t
            t_gate = quarters(bG, lambda k: xg[:, k * CAP:(k + 1) * CAP], t_x, hidT_before)
            for m in range(NT):
                t = flip(bT[:, m * P:(m + 1) * P], g4[:, m * P:(m + 1) * P], t_g4, ye_before)
            t_comb = copy(A, comb, bT[:, 0:T], t, mix_before)
            t1 = act(act_, bG[:, 0:QW], ACT.Tanh, t_gate, scale=0.5)
            t_up = up_before.tok = quarters(bU, lambda k: xg[:, k * CAP:(k + 1) * CAP], None, None)
            t1 = stt(act_, act_, 1.0, bG[:, 0:QW], ALU.add, ALU.mult, t1)
            t_hid = stt(hid, act_, 0.5, bU[:, 0:QW], ALU.mult, ALU.mult, t1, t_up)
            for a in range(2):
                t = flip(bT[:, a * P:(a + 1) * P], hid[:, a * P:(a + 1) * P], t_hid, t_comb)
            t_hT = hidT_before.tok = copy(V, hidT, bT[:, 0:T], t)
            t_y = quarters(bY, lambda k: hidT[:, (k % 2) * P + (k // 2) * 32:(k % 2) * P + (k // 2) * 32 + 32], t_hT, None)
            t_ye = ye_before.tok = copy(V, ye, bY[:, 0:QW], t_y)
            for j in range(4):
                for a in range(2):
                    t = mm(acc[j][:, a * T:(a + 1) * T], ye[32 * j:32 * j + 32, a * P:(a + 1) * P], comb[32 * j:32 * j + 32, :],
                           False, False, t_ye, t_comb, signal=(j, a) == (3, 1))
            mix_before.tok = t
        for j in range(4):
            sl = xT_[:, 2 * j * T:(2 * j + 2) * T]
            t_x2 = tt(V, sl, acc[j][:, :], sl, ALU.add, t)
        pr.all_join()
        h = modulated(hT, "norm_final", None, None, squares(t_x2))
        arena.at = 0
        res = tiles(arena.take(NT * D), D)
        for m in range(NT):
            for q in range(2):
                b, bank, before = banks.take()
                for c in range(4):
                    t = flip(bank[:, c * P:(c + 1) * P], hT[:, 4 * q + c, m * P:(m + 1) * P], before, h[4 * q + c])
                banks.reader[b] = copy(V, res[:, m, q * 512:(q + 1) * 512], bank[:, :], t)
        t_res = V.last()

        assert feed.tiles == NTILES, (feed.tiles, NTILES)
        block = ctx.enter_context(nc.Block())

        @block.sync
        def _(sp):
            sp.dma_start(pk[:, :], packed).then_inc(s_in.sem, 16)
            sp.dma_start(xin, x_in.rearrange("(m p) d -> p m d", p=P)).then_inc(s_x.sem, 16)

            def fill(c, s):
                sp.dma_start(ring[:, s * TPC * P:(s + 1) * TPC * P], weights[c]).then_inc(feed.filled[s].sem, 16)
            for s in range(SLOTS):
                fill(s, s)
            full = NCHUNKS // SLOTS
            with sp.Fori(1, full) as i:
                for s in range(SLOTS):
                    sp.wait_ge(feed.freed.sem, i * SLOTS + (s + 1 - SLOTS))
                    fill(i * SLOTS + s, s)
            for c in range(full * SLOTS, NCHUNKS):
                sp.wait_ge(feed.freed.sem, c - SLOTS + 1)
                fill(c, c % SLOTS)
            sp.wait_ge(t_res.counter.sem, t_res.value)
            sp.dma_start(out.rearrange("o (m p) d -> p (o m) d", p=P), res).then_inc(s_out.sem, 16)
            sp.wait_ge(s_out.sem, 16)

        @block.tensor
        def _(e):
            PE.emit(e)

        @block.vector
        def _(e):
            V.emit(e)

        @block.scalar
        def _(e):
            A.emit(e)

        @block.gpsimd
        def _(e):
            G.emit(e)



def bucket_of(dist):
    dist = np.maximum(dist, 0)
    d = np.maximum(dist, 1).astype(np.float32)
    half = BUCKETS // 2
    large = half + (np.log(d / np.float32(half)) / np.float32(math.log(MAX_DIST / half)) * np.float32(BUCKETS - half)).astype(np.int32)
    return np.where(dist < half, dist, np.minimum(large, BUCKETS - 1))


def constants():
    c = {}
    p = np.arange(P)
    eye = np.eye(P, dtype=np.float32)
    c["ident"], c["ones"] = eye, np.ones((P, P), np.float32)
    c["blk"] = (p[:, None] // 64 == p[None, :] // 64).astype(np.float32)
    c["pair"] = eye[p ^ 1]
    c["half"] = eye[p ^ 64]
    c["eps"], c["ln_eps"] = np.full((P, 1), EPS, np.float32), np.full((P, 1), LN_EPS, np.float32)
    c["zero"], c["one"] = np.zeros((P, 1), np.float32), np.ones((P, 1), np.float32)
    c["iota"] = np.tile(np.arange(CAP, dtype=np.float32), (P, 1))
    s, t = p[:, None], p[None, :]
    c["strict"] = np.concatenate([s < t, s > t], 1).astype(np.float32)
    c["incl"] = np.concatenate([s <= t, s >= t], 1).astype(np.float32)
    c["level"] = np.concatenate([((s >> (l + 1)) == (t >> (l + 1))) & ((s >> l) != (t >> l)) for l in range(LEVELS)], 1).astype(np.float32)
    tok = np.arange(T)
    freqs = (10000.0 ** (-np.arange(0, 32, 2, dtype=np.float32) / 32)).astype(np.float32)
    ang = np.concatenate([(tok // 64)[:, None] * freqs, (tok % 64)[:, None] * freqs], 1).astype(np.float32)
    j = (p % 64) // 2
    c["cos"] = np.cos(ang)[:, j].T.astype(np.float32)
    c["sin"] = (np.sin(ang)[:, j].T * np.where(p % 2 == 0, -1.0, 1.0)[:, None]).astype(np.float32)
    rows = []
    for w in WINDOWS:
        lo, hi = w // 2, w - w // 2 - 1
        rows.append(1.0 / (np.clip(tok + hi + 1, 0, T) - np.clip(tok - lo, 0, T)))
    c["inv_cnt"] = np.tile(np.concatenate(rows).astype(np.float32), (P, 1))
    dist = np.arange(2 * T) - (T - 1)
    oh = np.zeros((P, 2 * T), np.float32)
    b = bucket_of(dist)
    oh[b[dist >= 0], np.where(dist >= 0)[0]] = 1.0
    oh[BUCKETS, dist < 0] = 1.0
    c["onehot"] = oh
    return c


def pack_columns(x):
    pk = np.zeros((P, NCOLS), np.float32)

    def put(name, a, at=0):
        s = COLS[name][0] + at
        pk[:a.shape[0], s:s + a.shape[1]] = a

    def vec(name, v, at=0):
        put(name, np.asarray(v).reshape(-1, P).T, at)
    vec("c", x["c"])
    vec("mod_b", x["mod_b"][0]); vec("mod_b", x["mod_b"][1], 48); vec("mod_b", x["kv_mod_b"], 96)
    for l in range(2):
        vec(f"norm_mix{l}", x["norm_mix"][l]); vec(f"norm_ffn{l}", x["norm_ffn"][l])
    vec("kv_norm", x["kv_norm"]); vec("final_norm", x["final_norm"])
    vec("conv_w", x["lru_conv_w"]); vec("conv_b", x["lru_conv_b"]); vec("b_gates", x["lru_b_gates"])
    vec("lambda", x["lru_lambda"]); vec("norm_mix_2", x["norm_mix_2"])
    vec("shift_prev", x["shift_prev_2"]); vec("shift_next", x["shift_next_2"])
    vec("w0", x["rwkv_w0_2"]); vec("a0", x["rwkv_a0_2"])
    for n, m in (("k_k", "k_k"), ("k_a", "k_a"), ("r_k", "r_k"), ("ln_w", "ln_w"), ("ln_b", "ln_b")):
        vec(n, x[f"rwkv_{m}_2"])
    vec("pool_scale", x["pool_scale_2"])
    for n in ("q_norm", "k_norm"):
        put(n, np.tile(x[f"{n}_2"].reshape(-1, 1), (2, 1)))
    vec("norm_ffn_2", x["norm_ffn_2"]); vec("norm_final", x["norm_final_2"])
    put("rel_bias", x["rel_bias"].T)
    pk[BUCKETS, COLS["rel_bias"][0]:COLS["rel_bias"][0] + HEADS] = NEG
    put("w2", x["rwkv_w2_2"].reshape(P, RW)); put("a2", x["rwkv_a2_2"].reshape(P, RW)); put("g2", x["rwkv_g2_2"][0])
    put("pool_w", x["pool_w_2"][0].transpose(1, 0, 2).reshape(P, 4 * P))
    put("router", x["router_2"][0].reshape(KD, P, EXPERTS).transpose(1, 0, 2).reshape(P, -1))
    for n, a in constants().items():
        put(n, a)
    return pk


def pack_weights(x):
    out = np.empty((NTILES, P, P), np.float32)
    at = 0

    def grid(w):
        k, n = w.shape
        return w.reshape(k // P, P, n // P, P).transpose(0, 2, 1, 3)

    def put(a):
        nonlocal at
        a = a.reshape(-1, P, P) if a.ndim > 3 else a
        out[at:at + len(a)] = a
        at += len(a)

    def by_n(w):
        put(grid(w).transpose(1, 0, 2, 3))

    mods = [grid(x["mod_w"][0]), grid(x["mod_w"][1]), grid(x["kv_mod_w"])]
    mods = np.concatenate(mods, 1)

    def mod_blocks(*bs):
        for b in bs:
            for k in range(KD):
                put(mods[k, 16 * b:16 * b + 16])
                yield

    def steps(gen, n):
        for _ in range(n):
            next(gen)
    steps(mod_blocks(0), KD)
    early, later = mod_blocks(1, 2), mod_blocks(3, 4, 5, 6)
    w = grid(x["lru_w_in"][0])
    for n in range(2 * KL):
        put(w[:, (n + KL) % (2 * KL)])
        steps(early, mod_steps(n, 2 * KL, 2))
    for h in range(LRU_HEADS):
        by_n(x["lru_w_gates"][0, h])
    by_n(x["lru_w_out"][0])

    def ffn(l):
        gate, up = grid(x["ffn_w_gate"][l]), grid(x["ffn_w_up"][l])
        for f in range(KF):
            put(gate[:, f])
            put(up[:, f])
            if l == 0:
                steps(later, mod_steps(f, KF, 4))
        by_n(x["ffn_w_down"][l])
    ffn(0)
    kv = x["w_kv"]
    by_n(kv[:, :512])
    put(grid(kv[:, 512:]))
    by_n(x["attn_w_q"][0]); by_n(x["attn_w_o"][0])
    ffn(1)
    w = x["w_in_2"][0]
    by_n(w[:, :RWKV_COLS])
    by_n(w[:, RWKV_COLS + POOL_W:RWKV_COLS + POOL_W + ATT_COLS])
    by_n(w[:, RWKV_COLS:RWKV_COLS + POOL_W])
    gates = grid(w[:, RWKV_COLS + POOL_W + ATT_COLS:])
    br = [grid(x[f"w_branch_{n}_2"][0]) for n in ("rwkv", "pool", "attn")]
    for n in range(KD):
        for b in range(3):
            put(gates[:, b * KD + n])
    for n in range(KD):
        for b in range(3):
            put(br[b][:, n])
    by_n(x["w_out_2"][0])
    for e in range(EXPERTS):
        for n in ("gate", "up", "down"):
            put(grid(x[f"exp_{n}_2"][0, e]))
    assert at == NTILES
    return np.ascontiguousarray(out.reshape(NCHUNKS, TPC, P, P).transpose(0, 2, 1, 3)).reshape(NCHUNKS, P, TPC * P)


def kernel(**inputs):
    import concourse.bacc as bacc
    from concourse.bass_utils import run_bass_kernel_spmd

    x = {k: np.asarray(v) for k, v in inputs.items()}
    arrays = {"weights": pack_weights(x), "packed": pack_columns(x), "x": np.ascontiguousarray(x["x"][0])}
    nc = bacc.Bacc("TRN2", target_bir_lowering=False, num_devices=1)
    aps = {n: nc.dram_tensor(n, a.shape, F32, kind="ExternalInput").ap() for n, a in arrays.items()}
    scratch = nc.dram_tensor("bias_by_distance", (HEADS, 2 * T), F32, kind="Internal").ap()
    out = nc.dram_tensor("out", (1, T, D), F32, kind="ExternalOutput").ap()
    build(nc, aps["weights"], aps["packed"], aps["x"], scratch, out)
    return run_bass_kernel_spmd(nc, [arrays], core_ids=[0]).results[0]["out"]
```

```python
import contextlib
import itertools
import math

import numpy as np
import concourse.bass as bass
from concourse import mybir

F32 = mybir.dt.float32
ALU = mybir.AluOpType
ACT = mybir.ActivationFunctionType
AX = mybir.AxisListType.X

P = 128
T = 256
NT = T // P
D = 1024
KD = D // P
LRU = 1280
KL = LRU // P
LRU_HEADS = 5
FF = 2816
KF = FF // P
HEADS, KV_HEADS, HD = 8, 4, 128
BUCKETS, MAX_DIST = 32, 128
NEG = -1e30
RW = 512
KR = RW // P
RWKV_COLS, POOL_W, ATT_COLS = 1920, 512, 768
WINDOWS = (2, 4, 8, 16)
EXPERTS, CAP = 16, 32
EPS = 1e-6
LN_EPS = 64e-5

SLOTS = 6
TPC = 16
AHEAD = 8
MODS_PER_HEAD = 1
FIRST, LAST = 3, 2
START, EVERY = 6, 3
AT_NORM, AT_SCORES, AT_KEYS = 20, 4, 4
LEVELS = 7



def columns():
    early = [
        ("c", KD), ("mod_b", 112), ("norm_mix0", KD), ("norm_mix1", KD), ("norm_ffn0", KD), ("norm_ffn1", KD),
        ("kv_norm", KD), ("final_norm", KD), ("conv_w", 4 * KL), ("conv_b", KL), ("b_gates", 2 * KL),
        ("lambda", KL), ("eps", 1), ("ln_eps", 1), ("zero", 1), ("one", 1), ("ident", P), ("ones", P),
    ]
    late = [
        ("norm_mix_2", KD), ("shift_prev", 15), ("shift_next", 15), ("w0", 2 * KR),
        ("a0", 2 * KR), ("k_k", KR), ("k_a", KR), ("r_k", KR), ("ln_w", KR), ("ln_b", KR), ("pool_scale", KR),
        ("q_norm", 1), ("k_norm", 1), ("norm_ffn_2", KD), ("norm_final", KD), ("rel_bias", HEADS),
        ("w2", RW), ("a2", RW), ("g2", RW), ("pool_w", 4 * P), ("router", KD * EXPERTS),
        ("iota", CAP), ("blk", P), ("pair", P), ("half", P),
        ("cos", T), ("sin", T), ("inv_cnt", 4 * T), ("onehot", 2 * T),
        ("strict", 2 * P), ("incl", 2 * P), ("level", LEVELS * P),
    ]
    at, out = 0, {}
    for name, n in early + late:
        out[name] = (at, n)
        at += n
    return out, at, sum(n for _, n in early)


COLS, NCOLS, EARLY_COLS = columns()
SEGMENTS = [
    ("mods_0", 16 * KD), ("lru_in_mods_1_2", (20 + 32) * KD), ("lru_gates_mods_3_4", LRU_HEADS * 8 + 32 * KD), ("lru_out", KD * KL),
    ("ffn0_gu_mods_6", (2 * KF + 16) * KD), ("ffn0_down", KD * KF), ("k", KV_HEADS * KD), ("v", KV_HEADS * KD),
    ("q", HEADS * KD), ("mods_5", 16 * KD), ("o", KD * HEADS), ("ffn1_gu", 2 * KF * KD), ("ffn1_down", KD * KF),
    ("in2_main", 25 * KD), ("gates", 24 * KD), ("branches", 24 * KR), ("out2", KD * KD), ("experts", EXPERTS * 3 * KD * KD),
]


def mod_steps(n, n_all, blocks):
    return blocks * KD * (n + 1) // n_all - blocks * KD * n // n_all


NTILES = sum(n for _, n in SEGMENTS)
NCHUNKS = NTILES // TPC
RING_CHUNKS = NCHUNKS - AHEAD
assert NTILES % TPC == 0



class Counter:
    def __init__(self, sem):
        self.sem, self.count = sem, 0


class Loop:
    def __init__(self, n):
        self.n, self.entry, self.per = n, {}, {}


class Token:

    def __init__(self, counter, value, loop):
        self.counter, self.value, self.loop = counter, value, loop


class Later:

    def __init__(self):
        self.tok = None


class Engine:

    def __init__(self, prog, name, counter):
        self.prog, self.name, self.c = prog, name, counter
        self.ops, self.seen = [], {}

    def wait(self, *toks):
        for t in toks:
            if t is None:
                continue
            if isinstance(t, (list, tuple)):
                self.wait(*t)
                continue
            if isinstance(t, Later):
                self.ops.append(("wait", t, self.prog.loop))
                continue
            key = (id(t.counter), id(t.loop))
            if self.seen.get(key, -1) < t.value:
                self.seen[key] = t.value
                self.ops.append(("wait", t, self.prog.loop))

    def do(self, fn, *toks, counter=None):
        self.wait(*toks)
        c = counter or self.c
        c.count += 1
        self.ops.append(("op", fn, c))
        return Token(c, c.count, self.prog.loop)

    def run(self, fn, *toks):
        self.wait(*toks)
        self.ops.append(("op", fn, None))

    def last(self):
        return Token(self.c, self.c.count, self.prog.loop) if self.c.count else None

    def emit(self, e, ops=None, i=None):
        for op in self.ops if ops is None else ops:
            if op[0] == "wait":
                _, t, here = op
                late = isinstance(t, Later)
                t = t.tok if late else t
                v = t.value
                if t.loop is not None:
                    per = t.loop.per[t.counter]
                    if t.loop is here:
                        v = (v - per if late else v) + i * per
                    else:
                        v = v + (t.loop.n - 1) * per
                e.wait_ge(t.counter.sem, v)
            elif op[0] == "op16":
                op[1](e, i).then_inc(op[2].sem, 16)
            elif op[0] == "op":
                ins = op[1](e, i)
                if op[2] is not None:
                    ins.then_inc(op[2].sem, 1)
            else:
                with e.Fori(0, op[1]) as j:
                    self.emit(e, op[2], j)


class Program:
    def __init__(self, nc, ctx):
        self.nc, self.ctx, self.loop = nc, ctx, None
        self.counters = []
        self.pe, self.dve, self.act, self.pool = [
            Engine(self, n, self.counter(n)) for n in ("pe_done", "dve_done", "act_done", "pool_done")]
        self.engines = [self.pe, self.dve, self.act, self.pool]

    def counter(self, name):
        c = Counter(self.ctx.enter_context(self.nc.semaphore(name)))
        self.counters.append(c)
        return c

    def all_join(self):
        last = [e.last() for e in self.engines]
        for e in self.engines:
            e.wait(*last)

    @contextlib.contextmanager
    def repeat(self, n):
        loop = Loop(n)
        loop.entry = {c: c.count for c in self.counters}
        outer = [(e.ops, e.seen) for e in self.engines]
        for e in self.engines:
            e.ops, e.seen = [], {}
        self.loop = loop
        first_tile = self.feed.tiles
        yield loop
        self.loop = None
        taken = self.feed.tiles - first_tile
        assert taken % (SLOTS * TPC) == 0, "a chunk's slot is the same in every iteration"
        self.feed.tiles = first_tile + n * taken
        for c in self.counters:
            loop.per[c] = c.count - loop.entry[c]
            c.count = loop.entry[c] + n * loop.per[c]
        for e, (ops, seen) in zip(self.engines, outer):
            body = e.ops
            e.ops, e.seen = ops, seen
            if body:
                e.ops.append(("loop", n, body))


class Banks:

    def __init__(self, banks):
        self.banks, self.reader, self.at, self.held = banks, [None] * len(banks), 0, set()

    def take(self, hold=False):
        while self.at in self.held:
            self.at = (self.at + 1) % len(self.banks)
        b = self.at
        self.at = (b + 1) % len(self.banks)
        if hold:
            self.held.add(b)
        return b, self.banks[b], self.reader[b]

    def release(self, b, reader):
        self.held.discard(b)
        self.reader[b] = reader


class Feed:

    def __init__(self, prog, ring):
        self.prog, self.ring = prog, ring
        self.filled = [prog.counter(f"filled{s}") for s in range(SLOTS)]
        self.freed = prog.counter("freed")
        self.tiles = 0
        self.from_ring = True

    def load_ahead(self, buf, dram, engine):
        self.buf, self.ahead_in = buf, [self.prog.counter(f"ahead{c}") for c in range(AHEAD)]
        for c, done in enumerate(self.ahead_in):
            done.count = 16
            engine.ops.append(("op16", lambda e, i, c=c: e.dma_start(buf[:, c * TPC * P:(c + 1) * TPC * P], dram[c]), done))

    def tile(self, n=1):
        k = self.tiles - RING_CHUNKS * TPC
        self.from_ring = k < 0
        if not self.from_ring:
            if k % TPC == 0:
                self.prog.pe.wait(Token(self.ahead_in[k // TPC], 16, None))
            self.tiles += n
            return self.buf[:, k * P:(k + n) * P]
        k = self.tiles % TPC
        assert k + n <= TPC
        s = self.tiles // TPC % SLOTS
        if k == 0:
            c = self.filled[s]
            c.count += 16
            self.prog.pe.wait(Token(c, c.count, self.prog.loop))
        self.tiles += n
        return self.ring[:, (s * TPC + k) * P:(s * TPC + k + n) * P]

    def ends_chunk(self):
        return self.from_ring and self.tiles % TPC == 0


class Arena:
    def __init__(self, t, n):
        self.t, self.n, self.at, self.high = t, n, 0, 0

    def take(self, n):
        a = self.t[:, self.at:self.at + n]
        self.at += n
        self.high = max(self.high, self.at)
        assert self.at <= self.n, (self.at, self.n)
        return a


def tiles(ap, n):
    return ap.rearrange("p (a b) -> p a b", b=n)


def build(nc, weights, last_expert, packed, x_in, bias_scratch, out):
    with contextlib.ExitStack() as ctx:
        pr = Program(nc, ctx)
        PE, V, A, G = pr.pe, pr.dve, pr.act, pr.pool

        def sbuf(name, n):
            return ctx.enter_context(nc.sbuf_tensor(name, [P, n], F32))

        ring = sbuf("weight_ring", SLOTS * TPC * P)
        pk = sbuf("packed_consts", NCOLS)
        xT_ = sbuf("residual_T", KD * T)
        hT_ = sbuf("normed_T", KD * T)
        mod = sbuf("modulation", 112)
        gain = sbuf("norm_gain", KD)
        silu_c = sbuf("silu_c", KD)
        silu32 = sbuf("silu_c_copies", 32 * KD)
        mod_rows = sbuf("modulation_rows", 512)
        rstd = sbuf("rstd", T)
        table_probe = sbuf("table_probe", 1)
        NAR = (nc.sbuf_bytes_remaining // 4 - 64) if not callable(nc.sbuf_bytes_remaining) else nc.sbuf_bytes_remaining() // 4 - 64
        arena = Arena(sbuf("arena", NAR), NAR)
        banks = Banks([ctx.enter_context(nc.psum_tensor(f"bank{b}", [P, 512], F32)) for b in range(8)])
        feed = pr.feed = Feed(pr, ring)
        s_in, s_late, s_x, s_bias_w, s_out = [pr.counter(n) for n in ("in", "late_in", "x_in", "bias_w", "out")]
        s_bias_r = [pr.counter(f"bias_r{m}") for m in range(NT)]
        packed_in, late_in = Token(s_in, 16, None), Token(s_late, 16, None)
        x_loaded = Token(s_x, 16, None)

        xT, hT = tiles(xT_[:, :], T), tiles(hT_[:, :], T)

        def col(name, j=0, n=1):
            a = COLS[name][0] + j
            return pk[:, a:a + n]

        ident, ones, blk = col("ident", 0, P), col("ones", 0, P), col("blk", 0, P)

        for e in pr.engines:
            e.wait(packed_in)

        def mm(out, lhsT, rhs, start, stop, *toks, signal=False, weight=False):
            fn = lambda e, i: e.matmul(out(i) if callable(out) else out, lhsT, rhs(i) if callable(rhs) else rhs,
                                       start=start, stop=stop, skip_group_check=True)
            if weight and feed.ends_chunk():
                return PE.do(fn, *toks, counter=feed.freed)
            if signal:
                return PE.do(fn, *toks)
            PE.run(fn, *toks)

        def flip(out, in_, *toks, signal=True):
            n = in_.shape[0]
            fn = lambda e, i: e.transpose(out, in_, ident[0:n, 0:n])
            if signal:
                return PE.do(fn, *toks)
            PE.run(fn, *toks)

        def r(x, i):
            return x(i) if callable(x) else x

        def tt(eng, out, a, b, op, *toks):
            return eng.do(lambda e, i: e.tensor_tensor(r(out, i), r(a, i), r(b, i), op), *toks)

        def ts(eng, out, a, s1, s2, op0, op1, *toks):
            return eng.do(lambda e, i: e.tensor_scalar(r(out, i), r(a, i), r(s1, i), r(s2, i), op0, op1)
                          if s2 is not None else e.tensor_scalar(r(out, i), r(a, i), r(s1, i), None, op0), *toks)

        def stt(out, a, s, b, op0, op1, *toks):
            return V.do(lambda e, i: e.scalar_tensor_tensor(out=r(out, i), in0=r(a, i), scalar=r(s, i), in1=r(b, i),
                                                           op0=op0, op1=op1), *toks)

        def act(out, in_, f, *toks, **kw):
            return A.do(lambda e, i: e.activation(r(out, i), r(in_, i), f, **{k: r(v, i) for k, v in kw.items()}), *toks)

        def copy(eng, out, in_, *toks):
            if eng is A:
                return act(out, in_, ACT.Copy, *toks)
            if callable(out) or callable(in_):
                return eng.do(lambda e, i: e.tensor_scalar(r(out, i), r(in_, i), 1.0, None, ALU.mult), *toks)
            return eng.do(lambda e, i: e.tensor_copy(out, in_), *toks)

        def recip(out, in_, *toks):
            return V.do(lambda e, i: e.reciprocal(r(out, i), r(in_, i)), *toks)

        def sigmoid(out, in_, *toks, half_bias=None):
            kw = {"scale": 0.5}
            if half_bias is not None:
                kw["bias"] = half_bias
            t = act(out, in_, ACT.Tanh, *toks, **kw)
            return ts(V, out, out, 0.5, 0.5, ALU.mult, ALU.add, t)

        def linear(n_tiles, kt, rhs, ready, read):
            for n in range(n_tiles):
                b, bank, before = banks.take()
                for k in range(kt):
                    w = feed.tile()
                    t = mm(bank[:, 0:T], w, rhs(k), k == 0, k == kt - 1, before if k == 0 else None, ready(k),
                           signal=k == kt - 1, weight=True)
                banks.reader[b] = read(n, bank[:, 0:T], t)
            return t

        def linear_steps(n_tiles, kt, rhs, ready, read, b):
            for n in range(n_tiles):
                for k in range(kt):
                    t = mm(banks.banks[b][:, 0:T], feed.tile(), rhs(k), k == 0, k == kt - 1, banks.reader[b] if k == 0 else None,
                           ready(k), signal=k == kt - 1, weight=True)
                    if k == kt - 1:
                        banks.reader[b] = read(n, banks.banks[b][:, 0:T], t)
                    yield

        def squares(*toks):
            b, bank, before = banks.take(hold=True)
            load_sqrt_table()
            for k in range(KD):
                x_ready = toks[k]
                q = act(hT[:, k, :], xT[:, k, :], ACT.Square, x_ready) if k % 2 else \
                    tt(V, hT[:, k, :], xT[:, k, :], xT[:, k, :], ALU.mult, x_ready)
                t = mm(bank[:, 0:T], ones, hT[:, k, :], k == 0, k == KD - 1, before, q, signal=k == KD - 1)
            return b, t

        def load_sqrt_table():
            table_used[0] = act(table_probe[:, :], col("one"), ACT.Sqrt, table_used[0])
        table_used = [None]

        def inv_sqrt(buf, src, scale, eps_col, *toks):
            t = act(buf, src, ACT.Sqrt, *toks, scale=scale, bias=col(eps_col))
            return t, recip(buf, buf, t)

        def modulated(dst, g_name, shift, scale, sums):
            b, t = sums
            g = col(g_name, 0, KD) if scale is None else gain
            tg = None if scale is None else stt(gain[:, :], scale, 1.0, col(g_name, 0, KD), ALU.add, ALU.mult, V.last())
            t_src, t = inv_sqrt(rstd[:, :], banks.banks[b][:, 0:T], 1.0 / D, "eps", t, V.last())
            banks.release(b, t_src)
            done = []
            for k in range(KD):
                tk = stt(dst[:, k, :], xT[:, k, :], g[:, k:k + 1], rstd[:, 0:T], ALU.mult, ALU.mult, t, tg)
                if shift is not None:
                    tk = act(dst[:, k, :], dst[:, k, :], ACT.Identity, tk, bias=shift[:, k:k + 1])
                done.append(tk)
            return done

        def linear_residual(kt, rhs, ready, gate):
            sb_, sbank, s_before = banks.take(hold=True)
            pending = []

            def add_square():
                n, q = pending.pop(0)
                return mm(sbank[:, 0:T], ones, hT[:, n, :], n == 0, n == KD - 1, s_before, q, signal=True)

            def read(n, ps, t):
                g = gate if isinstance(gate, float) else gate[:, n:n + 1]
                t = t_new = stt(xT[:, n, :], ps, g, xT[:, n, :], ALU.mult, ALU.add, t)
                pending.append((n, act(hT[:, n, :], xT[:, n, :], ACT.Square, t)))
                if n:
                    add_square()
                else:
                    load_sqrt_table()
                return t_new
            linear(KD, kt, rhs, ready, read)
            return sb_, add_square()

        def swiglu(h, ready, gate, fill=None):
            arena.at = 0
            hid = tiles(arena.take(KF * T), T)
            sig = [arena.take(T) for _ in range(2)]
            done, free = [], [None, None]
            for f in range(KF):
                bg, gbank, g_before = banks.take()
                bu, ubank, u_before = banks.take()
                for bank, before in ((gbank, g_before), (ubank, u_before)):
                    for k in range(KD):
                        w = feed.tile()
                        t = mm(bank[:, 0:T], w, h[:, k, :], k == 0, k == KD - 1, before, ready[k],
                               signal=k == KD - 1, weight=True)
                    if bank is gbank:
                        tg = t
                s = sig[f % 2]
                t1 = act(s, gbank[:, 0:T], ACT.Tanh, tg, free[f % 2], scale=0.5)
                t1 = stt(s, s, 1.0, gbank[:, 0:T], ALU.add, ALU.mult, t1)
                banks.reader[bg] = t1
                t1 = stt(hid[:, f, :], s, 0.5, ubank[:, 0:T], ALU.mult, ALU.mult, t1, t)
                banks.reader[bu] = free[f % 2] = t1
                done.append(t1)
                if fill:
                    fill(f)
            return linear_residual(KF, lambda k: hid[:, k, :], lambda k: done[k], gate)

        def staggered(n, *stages):
            for i in range(n + max(o for o, _ in stages)):
                for o, f in stages:
                    if 0 <= i - o < n:
                        f(i - o)

        xin = tiles(arena.take(NT * D), D)
        t_xT = []
        for c0 in range(0, KD, 2):
            b, bank, before = banks.take()
            for c in (c0, c0 + 1):
                for m in range(NT):
                    t = flip(bank[:, (c - c0) * T + m * P:(c - c0) * T + (m + 1) * P], xin[:, m, c * P:(c + 1) * P],
                             x_loaded, before)
            banks.reader[b] = copy(V, xT_[:, c0 * T:(c0 + 2) * T], bank[:, :], t)
            t_xT += 2 * [banks.reader[b]]

        t = sigmoid(silu_c[:, :], col("c", 0, KD))
        t = tt(V, silu_c[:, :], silu_c[:, :], col("c", 0, KD), ALU.mult, t)
        wide = silu_c[:, :].unsqueeze(2).to_broadcast([P, KD, 32])
        t_silu = copy(V, tiles(silu32[:, :], 32), wide, t)
        PE.wait(t_silu)

        def mod_blocks(*blocks):
            ends = []

            def rows_to_columns():
                b, bk, bank, t = ends.pop(0)
                t = copy(A, mod_rows[:, :], bank[:, :], t, PE.last())
                banks.release(bk, t)
                bk, bank, before = banks.take()
                for c in range(4):
                    t1 = flip(bank[:, c * P:(c + 1) * P], mod_rows[:, c * P:(c + 1) * P], t, before)
                cols = bank[:, :].rearrange("p (c j r) -> p j c r", c=4, j=4)[:, :, :, 0]
                pick = lambda ap: ap.rearrange("p (j c) -> p j c", j=4)
                banks.reader[bk] = tt(V, pick(mod[:, 16 * b:16 * b + 16]), cols, pick(col("mod_b", 16 * b, 16)), ALU.add, t1)
                V.wait(V.last())
            for b in blocks:
                bk, bank, before = banks.take(hold=True)
                for k in range(KD):
                    for j in range(4):
                        w = feed.tile(4)
                        t = mm(bank[32 * j:32 * j + 32, :], silu32[:, 32 * k:32 * k + 32], w, k == 0, k == KD - 1,
                               before, signal=(k, j) == (KD - 1, 3), weight=True)
                    if k == KD // 2 and ends:
                        rows_to_columns()
                    if k < KD - 1:
                        yield
                ends.append((b, bk, bank, t))
                if b in (6, blocks[-1]):
                    while ends:
                        rows_to_columns()
                yield

        def steps(gen, n):
            for _ in range(n):
                next(gen)
        steps(mod_blocks(0), KD)

        def mods(layer, j):
            return mod[:, layer * 48 + j * KD:layer * 48 + (j + 1) * KD]

        arena.at = 0
        y_br = arena.take(KL * T)
        XW = T + 3
        xpad = tiles(arena.take(KL * XW), XW)
        xc = arena.take(KL * T)
        rg = arena.take(KL * T)
        ig = arena.take(KL * T)
        aa = arena.take(KL * T)
        gs = [arena.take(T) for _ in range(2)]
        cvec = arena.take(4 * KL)
        t_pad = G.do(lambda e, i: e.memset(xpad[:, :, 0:3], 0.0))
        t = act(cvec[:, 0:KL], col("lambda", 0, KL), ACT.Exp, scale=-1.0)
        t = act(cvec[:, 0:KL], cvec[:, 0:KL], ACT.Ln, t, bias=col("one"))
        ts(V, cvec[:, 2 * KL:3 * KL], col("b_gates", KL, KL), 0.5, None, ALU.mult, None)
        t = ts(V, cvec[:, KL:2 * KL], cvec[:, 0:KL], 8.0, None, ALU.mult, None, t)
        t_cv = ts(V, cvec[:, 0:KL], cvec[:, 0:KL], -8.0, None, ALU.mult, None, t)
        h = modulated(hT, "norm_mix0", mods(0, 0), mods(0, 1), squares(*t_xT))
        conv_done, gelu_done, gs_free = [], [], [None, None]
        early = mod_blocks(1, 2)

        def lru_in_read(n, ps, t):
            steps(early, mod_steps(n, 2 * KL, 2))
            if n < KL:
                t1 = copy(A, xpad[:, n, 3:XW], ps, t)
                o = xc[:, n * T:(n + 1) * T]
                t2 = ts(V, o, xpad[:, n, 0:T], col("conv_w", n), col("conv_b", n), ALU.mult, ALU.add, t1, t_pad)
                for k in range(1, 4):
                    t2 = stt(o, xpad[:, n, k:k + T], col("conv_w", k * KL + n), o, ALU.mult, ALU.add, t2)
                conv_done.append(t2)
                return t1
            n -= KL
            y, g = y_br[:, n * T:(n + 1) * T], gs[n % 2]
            t1 = copy(A, y, ps, t)
            t2 = tt(G, g, y, y, ALU.mult, t1, gs_free[n % 2])
            t2 = ts(G, g, g, 0.044715, 1.0, ALU.mult, ALU.add, t2)
            t2 = tt(G, g, g, y, ALU.mult, t2)
            t2 = act(g, g, ACT.Tanh, t2, scale=math.sqrt(2.0 / math.pi))
            gs_free[n % 2] = stt(y, g, 1.0, y, ALU.add, ALU.mult, t2)
            gelu_done.append(gs_free[n % 2])
            return t1
        linear(2 * KL, KD, lambda k: hT[:, k, :], lambda k: h[k], lru_in_read)
        s_late.count = 16
        A.ops.append(("op16", lambda e, i: e.dma_start(pk[:, EARLY_COLS:NCOLS], packed[:, EARLY_COLS:NCOLS]), s_late))
        later = mod_blocks(3, 4, 6, 5)
        for hh in range(LRU_HEADS):
            s = slice(2 * hh * T, (2 * hh + 2) * T)
            t_pre = {}

            def gate_read(n, ps, t):
                c = 2 * hh + n % 2
                o = slice(c * T, (c + 1) * T)
                if n < 2:
                    t1 = ts(V, rg[:, o], ps, col("b_gates", c), -80.0, ALU.add, ALU.max, t)
                    t_pre["r"] = act(rg[:, o], rg[:, o], ACT.Exp, t1, scale=-1.0)
                    return t1
                t1 = t_pre["i"] = act(ig[:, o], ps, ACT.Tanh, t, t_cv, scale=0.5, bias=cvec[:, 2 * KL + c:2 * KL + c + 1])
                return t1
            steps(later, MODS_PER_HEAD)
            linear(4, 2, lambda k: xc[:, (2 * hh + k) * T:(2 * hh + k + 1) * T], lambda k: conv_done[2 * hh + k], gate_read)
            t = ts(V, rg[:, s], rg[:, s], 1.0, None, ALU.add, None, t_pre["r"])
            t_r = recip(rg[:, s], rg[:, s], t)
            t_ix = stt(ig[:, s], ig[:, s], 1.0, xc[:, s], ALU.add, ALU.mult, t_pre["i"], PE.last())
            for c in (2 * hh, 2 * hh + 1):
                o = slice(c * T, (c + 1) * T)
                act(aa[:, o], rg[:, o], ACT.Exp, t_r, scale=cvec[:, c:c + 1])
                t = act(rg[:, o], rg[:, o], ACT.Tanh, A.last(), scale=cvec[:, KL + c:KL + c + 1])
            t1 = tt(G, xc[:, s], aa[:, s], aa[:, s], ALU.mult, t, t_ix)
            t_w = stt(rg[:, s], xc[:, s], 1.0, rg[:, s], ALU.add, ALU.mult, t1)
        t_a = A.last()
        t_sq = act(rg, rg, ACT.Sqrt, t_w, scale=0.25)
        z_done = []
        for n in range(KL):
            s = slice(n * T, (n + 1) * T)
            t = tt(V, ig[:, s], ig[:, s], rg[:, s], ALU.mult, t_sq, t_ix)
            t = V.do(lambda e, i, s=s: e.tensor_tensor_scan(xc[:, s], aa[:, s], ig[:, s], 0.0, ALU.mult, ALU.add), t, t_a)
            z_done.append(stt(ig[:, s], xc[:, s], 0.5, y_br[:, s], ALU.mult, ALU.mult, t, gelu_done[n]))
        steps(later, 2 * KD - LRU_HEADS * MODS_PER_HEAD)
        sums = linear_residual(KL, lambda k: ig[:, k * T:(k + 1) * T], lambda k: z_done[k], mods(0, 2))
        pr.all_join()

        def ffn(layer, sums, fill=None):
            h = modulated(hT, f"norm_ffn{layer}", mods(layer, 3), mods(layer, 4), sums)
            sums = swiglu(hT, h, mods(layer, 5), fill)
            pr.all_join()
            return sums
        sums = ffn(0, sums, lambda f: steps(later, mod_steps(f, KF, 1)))

        for e in pr.engines:
            e.wait(late_in)
        arena.at = 0
        KT = tiles(arena.take(KV_HEADS * T), T)
        VV = tiles(arena.take(NT * KV_HEADS * HD), KV_HEADS * HD)
        QT = tiles(arena.take(HEADS * T), T)
        OT = tiles(arena.take(HEADS * T), T)
        HB = [tiles(arena.take(HEADS * T), T) for _ in range(NT)]
        brow = arena.take(2 * T)[0:HEADS, :]
        b, bank, before = banks.take()
        t = mm(bank[0:HEADS, :], col("rel_bias", 0, HEADS)[0:BUCKETS + 1, :], col("onehot", 0, 2 * T)[0:BUCKETS + 1, :],
               True, True, before, signal=True)
        banks.reader[b] = copy(A, brow, bank[0:HEADS, :], t)
        A.wait(A.last())
        s_bias_w.count = 16
        A.ops.append(("op16", lambda e, i: e.dma_start(bias_scratch, brow), s_bias_w))
        A.wait(Token(s_bias_w, 16, None))
        t_hb = []
        for m in range(NT):
            src = bass.AP(tensor=bias_scratch.tensor, offset=m * P, ap=[[1, P], [2 * T, HEADS], [1, T]])
            s_bias_r[m].count = 16
            A.ops.append(("op16", lambda e, i, src=src, m=m: e.dma_start(HB[m], src), s_bias_r[m]))
            t_hb.append(Token(s_bias_r[m], 16, None))
        kvT = tiles(arena.take(KD * T), T)
        h = modulated(kvT, "kv_norm", mod[:, 96:96 + KD], mod[:, 96 + KD:112], sums)
        stt(gain[:, :], mods(1, 1), 1.0, col("norm_mix1", 0, KD), ALU.add, ALU.mult, V.last())
        tg = V.last()
        hq = []
        for k in range(KD):
            tk = stt(hT[:, k, :], xT[:, k, :], gain[:, k:k + 1], rstd[:, 0:T], ALU.mult, ALU.mult, tg)
            hq.append(act(hT[:, k, :], hT[:, k, :], ACT.Identity, tk, bias=mods(1, 0)[:, k:k + 1]))
        linear(KV_HEADS, KD, lambda k: kvT[:, k, :], lambda k: h[k], lambda n, ps, t: copy(A, KT[:, n, :], ps, t))
        (b0, v0, f0), (b1, v1, f1) = banks.take(), banks.take()
        for k in range(KD):
            w = feed.tile(4)
            t0 = mm(v0[:, :], kvT[:, k, 0:P], w, k == 0, k == KD - 1, f0, h[k], signal=k == KD - 1)
            t1 = mm(v1[:, :], kvT[:, k, P:T], w, k == 0, k == KD - 1, f1, signal=k == KD - 1, weight=True)
        banks.reader[b0] = copy(A, VV[:, 0, :], v0[:, :], t0)
        banks.reader[b1] = copy(V, VV[:, 1, :], v1[:, :], t1)
        t_kv = [A.last(), V.last()]
        t_q = []
        linear(HEADS, KD, lambda k: hT[:, k, :], lambda k: hq[k],
               lambda n, ps, t: t_q.append(copy(A, QT[:, n, :], ps, t)) or t_q[-1])
        SC = HD ** -0.5
        NBUF = 4
        pbuf, ptb, stat = [[arena.take(n) for _ in range(NBUF)] for n in (T, T, 4)]
        items = [(hd, m) for hd in range(HEADS) for m in range(NT)]
        t_exp, t_pt, p_free, pt_free, t_o = {}, {}, {}, {}, [None] * HEADS

        def scores(i):
            hd, m = items[i]
            nk = (m + 1) * P
            b, bank, before = banks.take()
            t = mm(bank[:, 0:nk], QT[:, hd, m * P:(m + 1) * P], KT[:, hd // 2, 0:nk], True, True, before, t_q[hd], t_kv, signal=True)
            pb, st = pbuf[i % NBUF][:, 0:nk], stat[i % NBUF]
            t = banks.reader[b] = stt(pb, bank[:, 0:nk], SC, HB[m][:, hd, T - nk:T][:, ::-1], ALU.mult, ALU.add, t, t_hb[m],
                                      p_free.get(i - NBUF))
            t = V.do(lambda e, i: e.tensor_reduce(st[:, 0:1], pb, AX, ALU.max, negate=True), t)
            t_exp[i] = act(pb, pb, ACT.Exp, t, bias=st[:, 0:1], accum_out=st[:, 1:2])

        def to_keys(i):
            hd, m = items[i]
            nk = (m + 1) * P
            pb, pt, st = pbuf[i % NBUF][:, 0:nk], ptb[i % NBUF], stat[i % NBUF]
            t = recip(st[:, 2:3], st[:, 1:2], t_exp[i])
            t = ts(V, pb, pb, st[:, 2:3], None, ALU.mult, None, t)
            b, bank, before = banks.take()
            for kt in range(m + 1):
                t1 = flip(bank[:, kt * P:(kt + 1) * P], pb[:, kt * P:(kt + 1) * P], t, before)
            p_free[i] = t1
            t_pt[i] = banks.reader[b] = copy(A, pt[:, 0:nk], bank[:, 0:nk], t1, pt_free.get(i - NBUF))

        def values(i):
            hd, m = items[i]
            pt = ptb[i % NBUF]
            b, bank, before = banks.take()
            for kt in range(m + 1):
                t = mm(bank[:, 0:P], VV[:, kt, hd // 2 * HD:(hd // 2 + 1) * HD], pt[:, kt * P:(kt + 1) * P], kt == 0, kt == m,
                       t_pt[i], before, signal=True)
            pt_free[i] = t
            t_o[hd] = banks.reader[b] = copy(V, OT[:, hd, m * P:(m + 1) * P], bank[:, 0:P], t)
        staggered(len(items), (0, scores), (2, to_keys), (3, values),
                  (3, lambda i: steps(later, 1) if i % 2 else None))
        sums = linear_residual(HEADS, lambda k: OT[:, k, :], lambda k: t_o[k], mods(1, 2))
        pr.all_join()
        sums = ffn(1, sums)

        t = modulated(xT, "final_norm", None, None, sums)
        h = modulated(hT, "norm_mix_2", None, None, squares(*t))

        arena.at = 0
        yaT = arena.take(KR * T)
        ybT = arena.take(KR * T)
        ycT = arena.take(KR * T)
        keep = arena.at
        arena.at = KR * T
        raw = arena.take(15 * T)
        TW = T + 2
        stage = [arena.t[:, arena.n - (2 - j) * TW:arena.n - (1 - j) * TW] for j in range(2)]
        mid = arena.take(15)
        t_z = G.do(lambda e, i: e.memset(stage[0], 0.0))
        t_z = G.do(lambda e, i: e.memset(stage[1], 0.0))
        t = tt(V, mid, col("shift_prev", 0, 15), col("shift_next", 0, 15), ALU.add)
        t_mid = ts(V, mid, mid, -1.0, 1.0, ALU.mult, ALU.add, t)
        st_free = [t_z, t_z]

        def shift_read(n, ps, t):
            st = stage[n % 2]
            t1 = copy(A, st[:, 1:T + 1], ps, t, st_free[n % 2])
            o = raw[:, n * T:(n + 1) * T]
            t2 = ts(V, o, st[:, 1:T + 1], mid[:, n:n + 1], None, ALU.mult, None, t1, t_mid)
            t2 = stt(o, st[:, 0:T], col("shift_prev", n), o, ALU.mult, ALU.add, t2)
            st_free[n % 2] = stt(o, st[:, 2:T + 2], col("shift_next", n), o, ALU.mult, ALU.add, t2)
            return t1
        linear(15, KD, lambda k: hT[:, k, :], lambda k: h[k], shift_read)
        pr.all_join()

        rT, kT_, vT = raw[:, 0:KR * T], raw[:, KR * T:2 * KR * T], raw[:, 2 * KR * T:3 * KR * T]
        wd, ad, gd = [raw[:, (12 + j) * T:(13 + j) * T] for j in range(3)]
        half0 = arena.take(4 * KR)
        omk = arena.take(KR)
        ts(V, half0, col("w0", 0, 4 * KR), 0.5, None, ALU.mult, None)
        ts(V, omk, col("k_a", 0, KR), -1.0, 1.0, ALU.mult, ALU.add)
        act(wd, wd, ACT.Tanh)
        sigmoid(gd, gd)
        pr.all_join()

        class Unit:
            def __init__(self):
                self.QR = [arena.take(2 * NT * P) for _ in range(2)]
                self.BT = [arena.take(T) for _ in range(2)]
                self.CT = [arena.take(T) for _ in range(2)]
                self.BCtok = arena.take(4 * P)
                self.Btok, self.Ctok = self.BCtok[:, 0:2 * P], self.BCtok[:, 2 * P:4 * P]
                self.psc = [arena.take(1) for _ in range(2)]
                self.ksum, self.vs = arena.take(T), arena.take(T)
                self.XT = [arena.take(4 * P) for _ in range(2)]
                self.MB = [arena.take(4 * P) for _ in range(2)]
        units = [Unit(), Unit()]
        LTb, Bm, Xb, Tb, LCb, MCb = [[arena.take(4 * P) for _ in range(2)] for _ in range(6)]
        Rb, Ub = arena.take(2 * P), arena.take(2 * P)
        sbd = [arena.take(P) for _ in range(2)]
        kk, sq, w_, a_, u_, inv_ = [arena.take(T) for _ in range(6)]
        f2 = [arena.take(NT * (P + 1)) for _ in range(2)]
        t_one = [G.do(lambda e, i, f=f: e.memset(f, 1.0)) for f in f2]
        V.wait(t_one)
        ym, y2, bo = [arena.take(T) for _ in range(3)]
        zero = col("zero").to_broadcast([P, P])
        strict, incl = tiles(col("strict", 0, 2 * P), P), tiles(col("incl", 0, 2 * P), P)
        level = tiles(col("level", 0, LEVELS * P), P)
        id4 = ident.unsqueeze(1).to_broadcast([P, 4, P])
        v4 = lambda ap: ap.rearrange("p (d h n) -> p d h n", d=2, h=2)
        B = banks.banks
        tail_done = [None] * KR

        att_ = arena.take(6 * T)
        att = tiles(att_, T)
        PW = 16 + T
        zb = tiles(arena.take(4 * PW), PW)
        t_zb0 = G.do(lambda e, i: e.memset(zb[:, :, :], 0.0))
        gates = [arena.take(T), mod_rows[:, 0:T], mod_rows[:, T:2 * T], silu32[:, :], stage[0][:, 0:T], stage[1][:, 0:T]]
        n_early = len(gates)
        AHEAD_LO = arena.at - T - AHEAD * TPC * P
        assert arena.at <= arena.n - 2 * TW
        for j in range(24 - n_early):
            gates.append(arena.t[:, keep + j * T:keep + (j + 1) * T])
        keep += (24 - n_early) * T
        t_att, t_zb, t_gates = [], [], []
        FILL = 7
        banks.held.add(FILL)

        def keep_token(toks, t):
            toks.append(t)
            return t

        def background():
            src, ready = (lambda k: hT[:, k, :]), (lambda k: h[k])
            yield from linear_steps(6, KD, src, ready, lambda n, ps, t: keep_token(t_att, copy(A, att[:, n, :], ps, t)), FILL)
            yield from linear_steps(4, KD, src, ready, lambda n, ps, t: keep_token(t_zb, copy(A, zb[:, n, 8:8 + T], ps, t, t_zb0)), FILL)
            yield from linear_steps(24, KD, src, ready, lambda n, ps, t: keep_token(t_gates, act(gates[n], ps, ACT.Tanh, t, scale=0.5)), FILL)

        def branch(src, gate0, ready):
            def read(n, ps, t):
                gate = gates[3 * n + gate0]
                if gate0 == 0:
                    t1 = stt(mg[:, n, :], gate, 1.0, ps, ALU.add, ALU.mult, t, t_gates[3 * n + gate0])
                    m_done.append(t1)
                    return t1
                p = part[n % 2]
                t1 = stt(p, gate, 1.0, ps, ALU.add, ALU.mult, t, part_free[n % 2], t_gates[3 * n + gate0])
                m_done[n] = part_free[n % 2] = tt(V, mg[:, n, :], mg[:, n, :], p, ALU.add, t1, m_done[n])
                return t1
            return KD, KR, lambda k: src[:, k * T:(k + 1) * T], ready, read
        m_done, part_free = [], [None, None]

        def background2():
            yield from linear_steps(*branch(yaT, 0, lambda k: None), FILL)
            yield from linear_steps(*branch(ybT, 1, lambda k: t_yb[k]), FILL)
        filler = itertools.chain(background(), background2())
        left = [(10 + n_early) * KD]

        def fill(n):
            for _ in range(min(n, left[0])):
                next(filler)
                left[0] -= 1

        def tile(s, d):
            return s if d == 0 else 1 - s

        def bank(b):
            return B[b], banks.reader[b]

        def prepare(ct, un):
            sl = slice(ct * T, (ct + 1) * T)
            k_, r_, v_ = kT_[:, sl], rT[:, sl], vT[:, sl]
            if ct >= 1:
                A.wait(units[(ct - 1) % 2].t_ops)
            if ct >= 2:
                for e in (V, A):
                    e.wait(tail_done[ct - 2])
            t = ts(V, kk, k_, col("k_k", ct), None, ALU.mult, None)
            t_sq = tt(V, sq, kk, kk, ALU.mult, t)
            b6, before = bank(6)
            for m in range(NT):
                t = flip(b6[:, m * P:(m + 1) * P], v_[:, m * P:(m + 1) * P], before)
            un.t_vs = banks.reader[6] = copy(A, un.vs, b6[:, 0:T], t)
            w2, a2 = col("w2", ct * P, P), col("a2", ct * P, P)
            yield
            b6, before = bank(6)
            t = mm(b6[:, 0:T], blk, sq, True, True, t_sq, before, signal=True)
            t = banks.reader[6] = ts(V, sq, b6[:, 0:T], 1e-24, None, ALU.max, None, t)
            t = act(sq, sq, ACT.Sqrt, t)
            yield
            t = recip(sq, sq, t)
            t_kk = tt(V, kk, kk, sq, ALU.mult, t)
            un.t_ops = []
            for d in range(2):
                lo = 64 * d
                yield
                b6, before = bank(6)
                mm(b6[:, 0:T], w2[lo:lo + 64, :], wd[lo:lo + 64, :], True, True, before)
                t = mm(b6[:, T:2 * T], a2[lo:lo + 64, :], ad[lo:lo + 64, :], True, True, signal=True)
                t_a = act(w_, b6[:, 0:T], ACT.Tanh, t, *un.t_ops, scale=0.5, bias=half0[:, d * KR + ct:d * KR + ct + 1])
                t, t_a = t_a, act(a_, b6[:, T:2 * T], ACT.Tanh, scale=0.5, bias=half0[:, (2 + d) * KR + ct:(2 + d) * KR + ct + 1])
                banks.reader[6] = t_a
                yield
                t = ts(V, w_, w_, 0.5, 0.5, ALU.mult, ALU.add, t)
                t_w = act(w_, w_, ACT.Exp, t, scale=-math.exp(-0.5))
                t_a = ts(V, a_, a_, 0.5, 0.5, ALU.mult, ALU.add, t_a)
                t = ts(V, u_, a_, col("k_a", ct), omk[:, ct:ct + 1], ALU.mult, ALU.add, t_a)
                t_kd = tt(V, u_, u_, k_, ALU.mult, t)
                if d == 0:
                    t_ks = copy(V, un.ksum, u_, t_kd)
                else:
                    t_ks = tt(V, un.ksum, un.ksum, u_, ALU.add, t_kd, t_ks)
                yield
                F, F_prev = tiles(f2[d], P + 1)[:, :, 1 - d:P + 1 - d], tiles(f2[d], P + 1)[:, :, d:P + d]
                for m in range(NT):
                    ws, fs = w_[:, m * P:(m + 1) * P], F[:, m, :]
                    if d:
                        ws, fs = ws[:, ::-1], fs[:, ::-1]
                    t = V.do(lambda e, i, ws=ws, fs=fs: e.tensor_tensor_scan(fs, ws, zero, 1.0, ALU.mult, ALU.add), t_w)
                t_inv = recip(tiles(inv_, P), F, t)
                yield
                mid_ = [m * P + 63 + d for m in range(NT)]
                first, second = (0, 1) if d == 0 else (1, 0)
                end, middle = P - 1 if d == 0 else 0, 63 + d
                t = tt(V, un.psc[d], F[:, first, end:end + 1], inv_[:, mid_[first]:mid_[first] + 1], ALU.mult, t_inv)
                un.t_ps = tt(V, un.psc[d], un.psc[d], F[:, second, middle:middle + 1], ALU.mult, t)
                last = []
                for m in range(NT):
                    ms = slice(m * P, (m + 1) * P)
                    im, fm = inv_[:, mid_[m]:mid_[m] + 1], F[:, m, middle:middle + 1]
                    q, rr = un.QR[d][:, 2 * m * P:(2 * m + 1) * P], un.QR[d][:, (2 * m + 1) * P:(2 * m + 2) * P]
                    stt(rr, F[:, m, :], im, r_[:, ms], ALU.mult, ALU.mult, t_inv)
                    stt(q, F_prev[:, m, :], im, kk[:, ms], ALU.mult, ALU.mult, t_kk)
                    t2 = stt(un.BT[d][:, ms], inv_[:, ms], fm, kk[:, ms], ALU.mult, ALU.mult)
                    last.append(stt(un.CT[d][:, ms], inv_[:, ms], fm, u_[:, ms], ALU.mult, ALU.mult))
                    last.append(tt(V, un.BT[d][:, ms], un.BT[d][:, ms], a_[:, ms], ALU.mult, t2))
                    if m == 0:
                        yield
                un.t_ops.append(last[-1])
            yield
            b6, before = bank(6)
            for j, src in enumerate((un.BT, un.CT)):
                for d in range(2):
                    m = tile(0, d)
                    t = flip(b6[:, (2 * j + d) * P:(2 * j + d + 1) * P], src[d][:, m * P:(m + 1) * P], *un.t_ops, before)
            un.t_tok = banks.reader[6] = copy(A, un.BCtok, b6[:, :], t)

        def gram(bb, un, left, s, hh, *toks):
            for d in range(2):
                m = tile(s, d)
                t = mm(bb[:, 2 * d * P:2 * (d + 1) * P], left[d][64 * hh:64 * hh + 64, m * P:(m + 1) * P],
                       un.QR[d][64 * hh:64 * hh + 64, 2 * m * P:2 * (m + 1) * P], True, True, *toks, signal=True)
            return t, bb[:, :].rearrange("p (d c n) -> p d c n", d=2, c=2)

        def finish(ct, un):
            sl = slice(ct * T, (ct + 1) * T)
            first_y = [None, None]
            t_s = t_yy = None
            for s in range(2):
                for hh in range(2):
                    bb, before = bank(4 + hh)
                    t, both = gram(bb, un, un.CT, s, hh, before)
                    t1 = tt(V, v4(LCb[s])[:, :, hh, :], both[:, :, 0, :], strict, ALU.mult, t)
                    t_c = banks.reader[4 + hh] = tt(V, v4(MCb[s])[:, :, hh, :], both[:, :, 1, :], incl, ALU.mult)
                yield
            for s in range(2):
                bR, before = bank(4)
                for d in range(2):
                    m = tile(s, d)
                    o = bR[:, d * P:(d + 1) * P]
                    if s:
                        mm(o, un.QR[d][:, 2 * m * P:(2 * m + 1) * P], sbd[d], True, False, before, t_s)
                    for hh in range(2):
                        t = mm(o[:, 64 * hh:64 * hh + 64], LCb[s][:, (2 * d + hh) * P:(2 * d + hh + 1) * P],
                               un.vs[:, m * P + 64 * hh:m * P + 64 * hh + 64], not s, True, before, t_c, un.t_vs, signal=True)
                t_R = banks.reader[4] = copy(V, Rb, bR[:, 0:2 * P], t)
                yield
                bU, before = bank(5)
                for d in range(2):
                    for hh in range(2):
                        c = slice(d * P + 64 * hh, d * P + 64 * hh + 64)
                        t1 = mm(bU[:, c], un.XT[s][:, (2 * d + hh) * P:(2 * d + hh + 1) * P], Rb[:, c], True, True, t_R, un.t_x, before,
                                signal=True)
                t_u = banks.reader[5] = ts(V, Ub, bU[:, 0:2 * P], -1.0, None, ALU.mult, None, t1)
                yield
                if s == 0:
                    toks = []
                    for d in range(2):
                        m = tile(s, d)
                        bS, before = bank(4 + d)
                        mm(bS[:, 0:P], un.Btok[:, d * P:(d + 1) * P], Ub[:, d * P:(d + 1) * P], True, False, t_u, un.t_tok, before)
                        t = mm(bS[:, 0:P], un.Ctok[:, d * P:(d + 1) * P], un.vs[:, m * P:(m + 1) * P], False, True, signal=True)
                        t_s = banks.reader[4 + d] = stt(sbd[d], bS[:, 0:P], un.psc[d], blk, ALU.mult, ALU.mult, t, un.t_ps)
                    yield
                for d in range(2):
                    m = tile(s, d)
                    bY, before = bank(4 + d)
                    o = bY[:, 0:P]
                    if s:
                        mm(o, sbd[d], un.QR[d][:, (2 * m + 1) * P:(2 * m + 2) * P], True, False, t_s, before)
                    for hh in range(2):
                        oh = bY[64 * hh:64 * hh + 64, 0:P]
                        q = slice((2 * d + hh) * P, (2 * d + hh + 1) * P)
                        mm(oh, Ub[:, d * P + 64 * hh:d * P + 64 * hh + 64], un.MB[s][:, q], not s, False, t_u, before)
                        t = mm(oh, un.vs[:, m * P + 64 * hh:m * P + 64 * hh + 64], MCb[s][:, q], False, True, signal=True)
                    y = yaT[:, ct * T + m * P:ct * T + (m + 1) * P]
                    if s == 0:
                        first_y[m] = banks.reader[4 + d] = copy(V, y, o, t)
                    else:
                        t_yy = banks.reader[4 + d] = tt(V, y, o, y, ALU.add, t, first_y[m])
                yield
            yv = yaT[:, sl]
            t_bo = stt(bo, un.ksum, col("r_k", ct), rT[:, sl], ALU.mult, ALU.mult)
            bb, before = bank(4)
            t = mm(bb[:, 0:T], blk, yv, True, True, t_yy, before, signal=True)
            t_m = banks.reader[4] = stt(ym, bb[:, 0:T], -1.0 / 64, yv, ALU.mult, ALU.add, t)
            t = tt(V, y2, ym, ym, ALU.mult, t_m)
            yield
            bb, before = bank(4)
            bb2, before2 = bank(5)
            t = mm(bb[:, 0:T], blk, y2, True, True, t, before, signal=True)
            t2 = mm(bb2[:, 0:T], blk, bo, True, True, t_bo, before2, signal=True)
            t_bo = banks.reader[5] = tt(V, bo, bb2[:, 0:T], vT[:, sl], ALU.mult, t2)
            banks.reader[4] = t = act(rstd[:, :], bb[:, 0:T], ACT.Sqrt, t, V.last(), scale=1.0 / 64, bias=col("ln_eps"))
            yield
            t = recip(rstd[:, :], rstd[:, :], t)
            t = tt(V, ym, ym, rstd[:, 0:T], ALU.mult, t)
            t = ts(V, ym, ym, col("ln_w", ct), col("ln_b", ct), ALU.mult, ALU.add, t)
            t = tt(V, ym, ym, bo, ALU.add, t, t_bo)
            yield
            bb, before = bank(5)
            t1 = mm(bb[:, 0:T], col("g2", ct * P, P), gd, True, True, before, signal=True)
            t = banks.reader[5] = tt(V, yv, ym, bb[:, 0:T], ALU.mult, t, t1)
            tail_done[ct] = [PE.last(), t]

        def invert(un, others):
            def between():
                slot[0] += 1
                if slot[0] % EVERY == 0:
                    fill(1)
                while others and next(others[0], ended) is ended:
                    others.pop(0)
            ended, slot = object(), [0]
            t_lt, t_x, t_xt, t_bm = [None] * 2, [None] * 2, [None] * 2, [None] * 2
            for s in range(2):
                for hh in range(2):
                    b = 2 * s + hh
                    bb, before = bank(b)
                    t, both = gram(bb, un, un.BT, s, hh, before, *un.t_ops)
                    tt(V, v4(LTb[s])[:, :, hh, :], both[:, :, 0, :], strict, ALU.mult, t)
                    t_lt[s] = banks.reader[b] = tt(V, v4(un.MB[s])[:, :, hh, :], both[:, :, 1, :], incl, ALU.mult)

            def blocks_of(lv, s, *toks):
                mk = level[:, lv, :].unsqueeze(1).to_broadcast([P, 4, P])
                return tt(G, tiles(Bm[s], P), tiles(LTb[s], P), mk, ALU.mult, *toks)
            for s in range(2):
                t_bm[s] = blocks_of(0, s, t_lt[s], PE.last())
            fill(START)
            for lv in range(LEVELS):
                if lv == 0:
                    for s in range(2):
                        t_xt[s] = tt(V, tiles(un.XT[s], P), id4, tiles(Bm[s], P), ALU.subtract, t_bm[s])
                        t_bm[s] = blocks_of(1, s, t_xt[s])
                else:
                    for s in range(2):
                        bb, before = bank(2 * s)
                        for q in range(4):
                            c = slice(q * P, (q + 1) * P)
                            t = mm(bb[:, c], Bm[s][:, c], Xb[s][:, c], True, True, t_bm[s], t_x[s], before, signal=q == 3)
                        t_x[s] = banks.reader[2 * s] = copy(A, Tb[s], bb[:, :], t)
                        if lv < LEVELS - 1:
                            t_bm[s] = blocks_of(lv + 1, s, t)
                        between()
                    for s in range(2):
                        bb, before = bank(2 * s + 1)
                        for q in range(4):
                            c = slice(q * P, (q + 1) * P)
                            t = mm(bb[:, c], Tb[s][:, c], un.XT[s][:, c], True, True, t_x[s], t_xt[s], before, signal=q == 3)
                        t_xt[s] = banks.reader[2 * s + 1] = tt(V, un.XT[s], un.XT[s], bb[:, :], ALU.subtract, t)
                        between()
                if lv < LEVELS - 1:
                    for s in range(2):
                        bb, before = bank(2 * s)
                        for q in range(4):
                            c = slice(q * P, (q + 1) * P)
                            t = flip(bb[:, c], un.XT[s][:, c], t_xt[s], before)
                        t_x[s] = banks.reader[2 * s] = copy(A, Xb[s], bb[:, :], t)
                    between()
            un.t_x = t_xt
            while others:
                between()

        for _ in prepare(0, units[0]):
            fill(FIRST)
        tail = iter(())
        for ct in range(KR):
            un = units[ct % 2]
            ahead = prepare(ct + 1, units[(ct + 1) % 2]) if ct + 1 < KR else iter(())
            invert(un, [tail, ahead])
            tail = finish(ct, un)
        for _ in tail:
            fill(LAST)
        fill(left[0])
        pr.all_join()
        left[0] = (24 - n_early) * KD + 2 * KD * KR

        arena.at = keep
        mg = tiles(arena.take(KD * T), T)
        part = [arena.take(T) for _ in range(2)]
        asq, arot = arena.take(5 * T), arena.take(5 * T)
        arstd = arena.take(3 * 5 * T)
        kz = [[arena.take(T) for _ in range(2)] for _ in range(2)]
        vtok = arena.take(NT * P)
        qk_gain = arena.take(2)
        ts(V, qk_gain[:, 0:1], col("q_norm"), 64 ** -0.5, None, ALU.mult, None)
        copy(V, qk_gain[:, 1:2], col("k_norm"))
        t_kz0 = [G.do(lambda e, i, z=kz[g][hh]: e.memset(z, 0.0)) for g in range(2) for hh in range(2)]
        t_s = [tt(V, asq[:, n * T:(n + 1) * T], att[:, n, :], att[:, n, :], ALU.mult, t_att[n]) for n in range(5)]
        stat_banks = []
        for n in range(5):
            if n % 2 == 0:
                b, bank, before = banks.take(hold=True)
                stat_banks.append((b, bank))
            t = mm(bank[:, n % 2 * T:(n % 2 + 1) * T], blk, asq[:, n * T:(n + 1) * T], True, True, t_s[n], before, signal=True)
            if n % 2 or n == 4:
                c0, c1 = n // 2 * 2 * T, (n + 1) * T
                t = ts(V, arstd[:, 5 * T + c0:5 * T + c1], bank[:, 0:c1 - c0], 1.0 / 64, EPS, ALU.mult, ALU.add, t)
                banks.release(b, t)
        y, z, w = [arstd[:, j * 5 * T:(j + 1) * 5 * T] for j in range(3)]
        t = act(y, z, ACT.Ln, t)
        t = act(y, y, ACT.Exp, t, scale=-0.5)
        t = tt(V, w, y, y, ALU.mult, t)
        t = tt(V, w, w, z, ALU.mult, t)
        t = ts(V, w, w, -0.5, 1.5, ALU.mult, ALU.add, t)
        t = tt(V, y, y, w, ALU.mult, t)
        t1 = stt(att_[:, 0:4 * T], att_[:, 0:4 * T], qk_gain[:, 0:1], y[:, 0:4 * T], ALU.mult, ALU.mult, t)
        t1 = stt(att[:, 4, :], att[:, 4, :], qk_gain[:, 1:2], y[:, 4 * T:5 * T], ALU.mult, ALU.mult, t)
        fill(2 * AT_NORM)
        for n in range(5):
            b, bank, before = banks.take()
            t = mm(bank[:, 0:T], col("pair", 0, P), att[:, n, :], True, True, t1, before, signal=True)
            banks.reader[b] = tt(V, arot[:, n * T:(n + 1) * T], bank[:, 0:T], col("sin", 0, T), ALU.mult, t)
        fill(AT_NORM)
        t_rot = V.last()
        t = tt(V, tiles(att_[:, 0:5 * T], T), tiles(att_[:, 0:5 * T], T), col("cos", 0, T).unsqueeze(1).to_broadcast([P, 5, T]),
               ALU.mult, t_rot)
        t_rope = tt(V, att_[:, 0:5 * T], att_[:, 0:5 * T], arot, ALU.add, t)
        kT = att[:, 4, :]
        b, bank, before = banks.take()
        t = mm(bank[:, 0:T], col("half", 0, P), kT, True, True, t_rope, before, signal=True)
        copy(V, kz[0][0][0:64, :], kT[0:64, :], t_kz0, t_rope)
        copy(V, kz[1][1][64:128, :], kT[64:128, :])
        copy(V, kz[0][1][64:128, :], bank[64:128, 0:T], t)
        t_kz = banks.reader[b] = copy(V, kz[1][0][0:64, :], bank[0:64, 0:T])
        fill(4)
        b, bank, before = banks.take()
        for m in range(NT):
            t = flip(bank[:, m * P:(m + 1) * P], att[:, 5, m * P:(m + 1) * P], t_att[5], before)
        t_vt = banks.reader[b] = copy(A, vtok, bank[:, 0:T], t)

        s1, s2 = arena.take(PW), arena.take(PW)
        pooled = tiles(arena.take(4 * T), T)
        t_z2 = G.do(lambda e, i: e.memset(s1, 0.0))
        t_z2 = G.do(lambda e, i: e.memset(s2, 0.0))
        t_pooled = []
        for g, w in enumerate(WINDOWS):
            cur, width = zb[:, g, :], 1
            t = t_zb[g]
            bufs = [s1, s2]
            while width < w:
                nxt = bufs[0]
                bufs.reverse()
                t = tt(G, nxt[:, 0:PW - width], cur[:, 0:PW - width], cur[:, width:PW], ALU.add, t, t_z2)
                cur, width = nxt, 2 * width
            lo = w // 2
            t = tt(G, pooled[:, g, :], cur[:, 8 - lo:8 - lo + T], col("inv_cnt", g * T, T), ALU.mult, t)
            t_pooled.append(tt(G, pooled[:, g, :], pooled[:, g, :], zb[:, g, 8:8 + T], ALU.subtract, t))

        pbuf, ptb, stat = [[arena.take(n) for _ in range(NBUF)] for n in (T, NT * P, 4)]
        items = [(hd, m) for hd in range(8) for m in range(NT)]
        t_exp, t_pt, p_free, pt_free = {}, {}, {}, {}

        def scores2(i):
            hd, m = items[i]
            b, bank, before = banks.take()
            t = mm(bank[:, 0:T], att[:, hd // 2, m * P:(m + 1) * P], kz[hd // 4][hd % 2], True, True, t_kz, before, signal=True)
            pb, st = pbuf[i % NBUF], stat[i % NBUF]
            t = V.do(lambda e, i: e.tensor_reduce(st[:, 0:1], bank[:, 0:T], AX, ALU.max, negate=True), t, p_free.get(i - NBUF))
            t_exp[i] = banks.reader[b] = act(pb, bank[:, 0:T], ACT.Exp, t, bias=st[:, 0:1], accum_out=st[:, 1:2])

        def to_keys2(i):
            hd, m = items[i]
            pb, pt, st = pbuf[i % NBUF], ptb[i % NBUF], stat[i % NBUF]
            t = recip(st[:, 2:3], st[:, 1:2], t_exp[i])
            t = ts(V, pb, pb, st[:, 2:3], None, ALU.mult, None, t)
            b, bank, before = banks.take()
            for kt in range(NT):
                t1 = flip(bank[:, kt * P:(kt + 1) * P], pb[:, kt * P:(kt + 1) * P], t, before)
            p_free[i] = t1
            t_pt[i] = banks.reader[b] = copy(A, pt, bank[:, 0:T], t1, pt_free.get(i - NBUF))

        def values2(i):
            hd, m = items[i]
            g, lo, pt = hd // 4, 64 * (hd % 2), ptb[i % NBUF]
            b, bank, before = banks.take()
            o = bank[lo:lo + 64, 0:P]
            for kt in range(NT):
                t = mm(o, vtok[:, kt * P + 64 * g:kt * P + 64 * g + 64], pt[:, kt * P:(kt + 1) * P], kt == 0, kt == NT - 1,
                       t_pt[i], t_vt, before, signal=True)
            pt_free[i] = t
            at_ = hd // 2 * T + m * P
            banks.reader[b] = copy(V, ycT[lo:lo + 64, at_:at_ + P], o, t)
        t_yb = []

        def pool_product(i):
            if i % 2 == 0:
                g = i // 2
                b, bank, before = banks.take()
                t1 = mm(bank[:, 0:T], col("pool_w", g * P, P), pooled[:, g, :], True, True, t_pooled[g], before, signal=True)
                banks.reader[b] = act(ybT[:, g * T:(g + 1) * T], bank[:, 0:T], ACT.Copy, t1, scale=col("pool_scale", g))
                t_yb.append(banks.reader[b])
        staggered(len(items), (0, scores2), (0, lambda i: pool_product(i) if i < 2 * KR else None), (0, lambda i: fill(AT_SCORES)),
                  (2, to_keys2), (2, lambda i: fill(AT_KEYS)), (3, values2))
        fill(left[0])
        banks.release(FILL, banks.reader[FILL])
        pr.all_join()

        feed.load_ahead(arena.t[:, AHEAD_LO:AHEAD_LO + AHEAD * TPC * P], last_expert, A)
        linear(*branch(ycT, 2, lambda k: None))
        sums = linear_residual(KD, lambda k: mg[:, k, :], lambda k: m_done[k], 0.5)
        pr.all_join()

        h = modulated(hT, "norm_ffn_2", None, None, sums)
        arena.at = 0
        htok_ = arena.take(NT * D)
        htok = tiles(htok_, D)
        sel = arena.take(NT * EXPERTS * CAP)
        gsel = arena.take(NT * EXPERTS * CAP)
        xall = arena.take(KD * EXPERTS * CAP)
        work = arena.at
        aff = arena.take(NT * EXPERTS)
        st = arena.take(4 * NT)
        affT = arena.take(T)[0:EXPERTS, :]
        wk = arena.take(T)[0:EXPERTS, :]
        mk = arena.take(T)[0:EXPERTS, :]
        ps_ = arena.take(T)[0:EXPERTS, :]
        m8 = arena.take(8)[0:EXPERTS, :]
        post = arena.take(NT * EXPERTS)
        for m in range(NT):
            for q in range(2):
                b, bank, before = banks.take()
                for c in range(4):
                    t = flip(bank[:, c * P:(c + 1) * P], hT[:, 4 * q + c, m * P:(m + 1) * P], before, h[-1])
                banks.reader[b] = copy(A, htok[:, m, q * 512:(q + 1) * 512], bank[:, :], t)
        t_ht = A.last()
        for m in range(NT):
            b, bank, before = banks.take()
            for k in range(KD):
                t = mm(bank[:, 0:EXPERTS], hT[:, k, m * P:(m + 1) * P], col("router", k * EXPERTS, EXPERTS), k == 0, k == KD - 1,
                       before, signal=k == KD - 1)
            s_, af = st[:, 4 * m:4 * m + 4], aff[:, m * EXPERTS:(m + 1) * EXPERTS]
            t1 = V.do(lambda e, i, s_=s_, bank=bank: e.tensor_reduce(s_[:, 0:1], bank[:, 0:EXPERTS], AX, ALU.max), t)
            t1 = ts(V, s_[:, 1:2], s_[:, 0:1], -1.0, None, ALU.mult, None, t1)
            t1 = banks.reader[b] = act(af, bank[:, 0:EXPERTS], ACT.Exp, t1, bias=s_[:, 1:2], accum_out=s_[:, 2:3])
            t1 = recip(s_[:, 3:4], s_[:, 2:3], t1)
            t_af = ts(V, af, af, s_[:, 3:4], None, ALU.mult, None, t1)
        b, bank, before = banks.take()
        for m in range(NT):
            t = flip(bank[0:EXPERTS, m * P:(m + 1) * P], aff[:, m * EXPERTS:(m + 1) * EXPERTS], t_af, before)
        t = banks.reader[b] = copy(V, affT, bank[0:EXPERTS, 0:T], t)
        t = copy(V, wk, affT, t)
        for _ in range(CAP // 8):
            t = V.do(lambda e, i: e.max(m8, wk), t)
            t = V.do(lambda e, i: e.match_replace(out=wk, in_to_replace=m8, in_values=wk, imm_value=-1.0), t)
        t_mk = ts(V, mk, wk, 0.0, None, ALU.is_lt, None, t)
        t = V.do(lambda e, i: e.tensor_tensor_scan(ps_, mk, col("zero")[0:EXPERTS, :].to_broadcast([EXPERTS, T]), 0.0, ALU.add, ALU.add), t_mk)
        t = tt(V, ps_, ps_, mk, ALU.mult, t)
        t = ts(V, ps_, ps_, -1.0, None, ALU.add, None, t)
        b, bank, before = banks.take()
        for m in range(NT):
            t1 = flip(bank[:, m * EXPERTS:(m + 1) * EXPERTS], ps_[:, m * P:(m + 1) * P], t, before)
        t = banks.reader[b] = copy(V, post, bank[:, 0:NT * EXPERTS], t1)
        iota = col("iota", 0, CAP).unsqueeze(1).to_broadcast([P, EXPERTS, CAP])
        selv = sel.rearrange("p (m e c) -> p m e c", m=NT, e=EXPERTS)
        gselv = gsel.rearrange("p (m e c) -> p m e c", m=NT, e=EXPERTS)
        for m in range(NT):
            pv = post[:, m * EXPERTS:(m + 1) * EXPERTS].unsqueeze(2).to_broadcast([P, EXPERTS, CAP])
            av = aff[:, m * EXPERTS:(m + 1) * EXPERTS].unsqueeze(2).to_broadcast([P, EXPERTS, CAP])
            t1 = tt(V, selv[:, m], pv, iota, ALU.is_equal, t)
            t2 = tt(V, gselv[:, m], selv[:, m], av, ALU.mult, t1)
        for k in range(KD):
            b, bank, before = banks.take()
            for m in range(NT):
                t = mm(bank[:, :], htok[:, m, k * P:(k + 1) * P], sel[:, m * 512:(m + 1) * 512], m == 0, m == NT - 1,
                       before, t2, t_ht, signal=m == NT - 1)
            banks.reader[b] = copy(A if k % 2 else V, xall[:, k * 512:(k + 1) * 512], bank[:, :], t)
        pr.all_join()

        arena.at = work
        xg, g4 = arena.take(KD * CAP), arena.take(NT * P)
        act_, hid, hidT, ye, comb = [arena.take(T) for _ in range(5)]
        zeros = arena.take(P)
        bG, bU, bT, bY, acc = B[0], B[1], B[2], B[3], B[4:8]
        xv = tiles(xall, EXPERTS * CAP)
        gv = tiles(gsel, EXPERTS * CAP)
        QW = D // 4
        t = G.do(lambda e, i: e.memset(zeros, 0.0))
        for j in range(4):
            mm(acc[j][:, :], zeros, xall[:, 0:512], True, False, t)
        pr.all_join()
        def quarters(bank, lhs, ready, before):
            for k in range(KD):
                for j in range(4):
                    w = feed.tile(2)
                    t = mm(bank[32 * j:32 * j + 32, 0:QW], lhs(k), w, k == 0, k == KD - 1, ready, before if (k, j) == (0, 0) else None,
                           signal=(k, j) == (KD - 1, 3), weight=True)
            return t
        def expert(number, mix_before, up_before, hidT_before, ye_before):
            at = lambda i: bass.ds(number(i) * CAP, CAP)
            t_x = ts(V, tiles(xg, CAP), lambda i: xv[:, :, at(i)], 1.0, None, ALU.mult, None, up_before)
            for m in range(NT):
                t_g4 = ts(V, g4[:, m * P:(m + 1) * P].rearrange("p (j c) -> p j c", j=4),
                          lambda i, m=m: gv[:, m:m + 1, at(i)].to_broadcast([P, 4, CAP]), 1.0, None, ALU.mult, None)
            t_gate = quarters(bG, lambda k: xg[:, k * CAP:(k + 1) * CAP], t_x, hidT_before)
            for m in range(NT):
                t = flip(bT[:, m * P:(m + 1) * P], g4[:, m * P:(m + 1) * P], t_g4, ye_before)
            t_comb = copy(A, comb, bT[:, 0:T], t, mix_before)
            t1 = act(act_, bG[:, 0:QW], ACT.Tanh, t_gate, scale=0.5)
            t_up = quarters(bU, lambda k: xg[:, k * CAP:(k + 1) * CAP], None, None)
            t1 = stt(act_, act_, 1.0, bG[:, 0:QW], ALU.add, ALU.mult, t1)
            t_hid = stt(hid, act_, 0.5, bU[:, 0:QW], ALU.mult, ALU.mult, t1, t_up)
            for a in range(2):
                t = flip(bT[:, a * P:(a + 1) * P], hid[:, a * P:(a + 1) * P], t_hid, t_comb)
            t_hT = copy(V, hidT, bT[:, 0:T], t)
            t_y = quarters(bY, lambda k: hidT[:, (k % 2) * P + (k // 2) * 32:(k % 2) * P + (k // 2) * 32 + 32], t_hT, None)
            t_ye = copy(V, ye, bY[:, 0:QW], t_y)
            for j in range(4):
                for a in range(2):
                    t = mm(acc[j][:, a * T:(a + 1) * T], ye[32 * j:32 * j + 32, a * P:(a + 1) * P], comb[32 * j:32 * j + 32, :],
                           False, False, t_ye, t_comb, signal=(j, a) == (3, 1))
            return t, t_up, t_hT, t_ye

        with pr.repeat(EXPERTS - 1):
            before = [Later() for _ in range(4)]
            for b, t in zip(before, expert(lambda i: i, *before)):
                b.tok = t
        t = expert(lambda i: EXPERTS - 1, *[b.tok for b in before])[0]
        t_x2 = []
        for j in range(4):
            sl = xT_[:, 2 * j * T:(2 * j + 2) * T]
            t_x2 += 2 * [tt(V, sl, acc[j][:, :], sl, ALU.add, t)]
        for b in range(8):
            banks.reader[b] = V.last()
        h = modulated(hT, "norm_final", None, None, squares(*t_x2))
        res = tiles(htok_, D)
        t_res = [[] for _ in range(NT)]
        for m in range(NT):
            for q in range(2):
                b, bank, before = banks.take()
                for c in range(4):
                    t = flip(bank[:, c * P:(c + 1) * P], hT[:, 4 * q + c, m * P:(m + 1) * P], before, h[4 * q + c])
                banks.reader[b] = copy(V if q else A, res[:, m, q * 512:(q + 1) * 512], bank[:, :], t)
                t_res[m].append(banks.reader[b])

        assert feed.tiles == NTILES, (feed.tiles, NTILES)
        block = ctx.enter_context(nc.Block())

        @block.sync
        def _(sp):
            sp.dma_start(pk[:, 0:EARLY_COLS], packed[:, 0:EARLY_COLS]).then_inc(s_in.sem, 16)
            sp.dma_start(xin, x_in.rearrange("(m p) d -> p m d", p=P)).then_inc(s_x.sem, 16)

            def fill(c, s):
                sp.dma_start(ring[:, s * TPC * P:(s + 1) * TPC * P], weights[c]).then_inc(feed.filled[s].sem, 16)
            for s in range(SLOTS):
                fill(s, s)
            full = RING_CHUNKS // SLOTS
            with sp.Fori(1, full) as i:
                for s in range(SLOTS):
                    sp.wait_ge(feed.freed.sem, i * SLOTS + (s + 1 - SLOTS))
                    fill(i * SLOTS + s, s)
            for c in range(full * SLOTS, RING_CHUNKS):
                sp.wait_ge(feed.freed.sem, c - SLOTS + 1)
                fill(c, c % SLOTS)
            for m in range(NT):
                for t in t_res[m]:
                    sp.wait_ge(t.counter.sem, t.value)
                sp.dma_start(out[0, m * P:(m + 1) * P, :], res[:, m, :]).then_inc(s_out.sem, 16)
            sp.wait_ge(s_out.sem, 16 * NT)

        @block.tensor
        def _(e):
            PE.emit(e)

        @block.vector
        def _(e):
            V.emit(e)

        @block.scalar
        def _(e):
            A.emit(e)

        @block.gpsimd
        def _(e):
            G.emit(e)



def bucket_of(dist):
    dist = np.maximum(dist, 0)
    d = np.maximum(dist, 1).astype(np.float32)
    half = BUCKETS // 2
    large = half + (np.log(d / np.float32(half)) / np.float32(math.log(MAX_DIST / half)) * np.float32(BUCKETS - half)).astype(np.int32)
    return np.where(dist < half, dist, np.minimum(large, BUCKETS - 1))


def constants():
    c = {}
    p = np.arange(P)
    eye = np.eye(P, dtype=np.float32)
    c["ident"], c["ones"] = eye, np.ones((P, P), np.float32)
    c["blk"] = (p[:, None] // 64 == p[None, :] // 64).astype(np.float32)
    c["pair"] = eye[p ^ 1]
    c["half"] = eye[p ^ 64]
    c["eps"], c["ln_eps"] = np.full((P, 1), EPS, np.float32), np.full((P, 1), LN_EPS, np.float32)
    c["zero"], c["one"] = np.zeros((P, 1), np.float32), np.ones((P, 1), np.float32)
    c["iota"] = np.tile(np.arange(CAP, dtype=np.float32), (P, 1))
    s, t = p[:, None], p[None, :]
    c["strict"] = np.concatenate([s < t, s > t], 1).astype(np.float32)
    c["incl"] = np.concatenate([s <= t, s >= t], 1).astype(np.float32)
    c["level"] = np.concatenate([((s >> (l + 1)) == (t >> (l + 1))) & ((s >> l) != (t >> l)) for l in range(LEVELS)], 1).astype(np.float32)
    tok = np.arange(T)
    freqs = (10000.0 ** (-np.arange(0, 32, 2, dtype=np.float32) / 32)).astype(np.float32)
    ang = np.concatenate([(tok // 64)[:, None] * freqs, (tok % 64)[:, None] * freqs], 1).astype(np.float32)
    j = (p % 64) // 2
    c["cos"] = np.cos(ang)[:, j].T.astype(np.float32)
    c["sin"] = (np.sin(ang)[:, j].T * np.where(p % 2 == 0, -1.0, 1.0)[:, None]).astype(np.float32)
    rows = []
    for w in WINDOWS:
        lo, hi = w // 2, w - w // 2 - 1
        rows.append(1.0 / (np.clip(tok + hi + 1, 0, T) - np.clip(tok - lo, 0, T)))
    c["inv_cnt"] = np.tile(np.concatenate(rows).astype(np.float32), (P, 1))
    dist = np.arange(2 * T) - (T - 1)
    oh = np.zeros((P, 2 * T), np.float32)
    b = bucket_of(dist)
    oh[b[dist >= 0], np.where(dist >= 0)[0]] = 1.0
    oh[BUCKETS, dist < 0] = 1.0
    c["onehot"] = oh
    return c


def pack_columns(x):
    pk = np.zeros((P, NCOLS), np.float32)

    def put(name, a, at=0):
        s = COLS[name][0] + at
        pk[:a.shape[0], s:s + a.shape[1]] = a

    def vec(name, v, at=0):
        put(name, np.asarray(v).reshape(-1, P).T, at)
    vec("c", x["c"])
    vec("mod_b", x["mod_b"][0]); vec("mod_b", x["mod_b"][1], 48); vec("mod_b", x["kv_mod_b"], 96)
    for l in range(2):
        vec(f"norm_mix{l}", x["norm_mix"][l]); vec(f"norm_ffn{l}", x["norm_ffn"][l])
    vec("kv_norm", x["kv_norm"]); vec("final_norm", x["final_norm"])
    vec("conv_w", x["lru_conv_w"]); vec("conv_b", x["lru_conv_b"]); vec("b_gates", x["lru_b_gates"])
    vec("lambda", x["lru_lambda"]); vec("norm_mix_2", x["norm_mix_2"])
    vec("shift_prev", x["shift_prev_2"]); vec("shift_next", x["shift_next_2"])
    vec("w0", x["rwkv_w0_2"]); vec("a0", x["rwkv_a0_2"])
    for n, m in (("k_k", "k_k"), ("k_a", "k_a"), ("r_k", "r_k"), ("ln_w", "ln_w"), ("ln_b", "ln_b")):
        vec(n, x[f"rwkv_{m}_2"])
    vec("pool_scale", x["pool_scale_2"])
    for n in ("q_norm", "k_norm"):
        put(n, np.tile(x[f"{n}_2"].reshape(-1, 1), (2, 1)))
    vec("norm_ffn_2", x["norm_ffn_2"]); vec("norm_final", x["norm_final_2"])
    put("rel_bias", x["rel_bias"].T)
    pk[BUCKETS, COLS["rel_bias"][0]:COLS["rel_bias"][0] + HEADS] = NEG
    put("w2", x["rwkv_w2_2"].reshape(P, RW)); put("a2", x["rwkv_a2_2"].reshape(P, RW)); put("g2", x["rwkv_g2_2"][0])
    put("pool_w", x["pool_w_2"][0].transpose(1, 0, 2).reshape(P, 4 * P))
    put("router", x["router_2"][0].reshape(KD, P, EXPERTS).transpose(1, 0, 2).reshape(P, -1))
    for n, a in constants().items():
        put(n, a)
    return pk


def pack_weights(x):
    out = np.empty((NTILES, P, P), np.float32)
    at = 0

    def grid(w):
        k, n = w.shape
        return w.reshape(k // P, P, n // P, P).transpose(0, 2, 1, 3)

    def put(a):
        nonlocal at
        a = a.reshape(-1, P, P) if a.ndim > 3 else a
        out[at:at + len(a)] = a
        at += len(a)

    def by_n(w):
        put(grid(w).transpose(1, 0, 2, 3))

    mods = [grid(x["mod_w"][0]), grid(x["mod_w"][1]), grid(x["kv_mod_w"])]
    mods = np.concatenate(mods, 1)

    def mod_blocks(*bs):
        for b in bs:
            for k in range(KD):
                put(mods[k, 16 * b:16 * b + 16])
                yield

    def steps(gen, n):
        for _ in range(n):
            next(gen)
    steps(mod_blocks(0), KD)
    early, later = mod_blocks(1, 2), mod_blocks(3, 4, 6, 5)
    w = grid(x["lru_w_in"][0])
    for n in range(2 * KL):
        put(w[:, (n + KL) % (2 * KL)])
        steps(early, mod_steps(n, 2 * KL, 2))
    for h in range(LRU_HEADS):
        steps(later, MODS_PER_HEAD)
        by_n(x["lru_w_gates"][0, h])
    steps(later, 2 * KD - LRU_HEADS * MODS_PER_HEAD)
    by_n(x["lru_w_out"][0])

    def ffn(l):
        gate, up = grid(x["ffn_w_gate"][l]), grid(x["ffn_w_up"][l])
        for f in range(KF):
            put(gate[:, f])
            put(up[:, f])
            if l == 0:
                steps(later, mod_steps(f, KF, 1))
        by_n(x["ffn_w_down"][l])
    ffn(0)
    kv = x["w_kv"]
    by_n(kv[:, :512])
    put(grid(kv[:, 512:]))
    by_n(x["attn_w_q"][0])
    steps(later, KD)
    by_n(x["attn_w_o"][0])
    ffn(1)
    w = x["w_in_2"][0]
    by_n(w[:, :RWKV_COLS])
    by_n(w[:, RWKV_COLS + POOL_W:RWKV_COLS + POOL_W + ATT_COLS])
    by_n(w[:, RWKV_COLS:RWKV_COLS + POOL_W])
    gates = grid(w[:, RWKV_COLS + POOL_W + ATT_COLS:])
    br = [grid(x[f"w_branch_{n}_2"][0]) for n in ("rwkv", "pool", "attn")]
    for n in range(KD):
        for b in range(3):
            put(gates[:, b * KD + n])
    for b in range(3):
        for n in range(KD):
            put(br[b][:, n])
    by_n(x["w_out_2"][0])
    for e in range(EXPERTS):
        for n in ("gate", "up", "down"):
            put(grid(x[f"exp_{n}_2"][0, e]))
    assert at == NTILES
    return np.ascontiguousarray(out.reshape(NCHUNKS, TPC, P, P).transpose(0, 2, 1, 3)).reshape(NCHUNKS, P, TPC * P)


def kernel(**inputs):
    import concourse.bacc as bacc
    from concourse.bass_utils import run_bass_kernel_spmd

    x = {k: np.asarray(v) for k, v in inputs.items()}
    chunks = pack_weights(x)
    arrays = {"weights": chunks[:RING_CHUNKS],
              "ahead": chunks[RING_CHUNKS:], "packed": pack_columns(x), "x": np.ascontiguousarray(x["x"][0])}
    nc = bacc.Bacc("TRN2", target_bir_lowering=False, num_devices=1)
    aps = {n: nc.dram_tensor(n, a.shape, F32, kind="ExternalInput").ap() for n, a in arrays.items()}
    scratch = nc.dram_tensor("bias_by_distance", (HEADS, 2 * T), F32, kind="Internal").ap()
    out = nc.dram_tensor("out", (1, T, D), F32, kind="ExternalOutput").ap()
    build(nc, aps["weights"], aps["ahead"], aps["packed"], aps["x"], scratch, out)
    return run_bass_kernel_spmd(nc, [arrays], core_ids=[0]).results[0]["out"]
```
